# Optimizing a Trainium2 kernel written in Bass

```python
import math
import jax, jax.numpy as jnp
from jax import lax
import numpy as np

D_MODEL = 1024
BATCH = 1
SEQ = 256
DEPTH = 2

N_A = DEPTH // 2
PLE_DIM = 256
NORM_EPS = 1e-6
L2_EPS = 1e-6
GDN_QK_HEADS = 8
GDN_V_HEADS = 16
GDN_HEAD_DIM = 128
GDN_CONV = 4
GDN_CHUNK = 64
GDN_QK_W = GDN_QK_HEADS * GDN_HEAD_DIM
GDN_V_W = GDN_V_HEADS * GDN_HEAD_DIM
GDN_CONV_W = 2 * GDN_QK_W + GDN_V_W
GDN_IN_W = GDN_CONV_W + GDN_V_W + 2 * GDN_V_HEADS
NSA_HEADS = 16
NSA_GROUPS = 4
NSA_HEAD_DIM = 64
NSA_REP = NSA_HEADS // NSA_GROUPS
CMP_BLOCK = 32
CMP_STRIDE = 16
CMP_HIDDEN = 256
SEL_BLOCK = 64
SEL_TOPK = 16
WINDOW = 512
Q_BLOCK = 128
FORCED_SCORE = 1e4
NSA_Q_W = NSA_HEADS * NSA_HEAD_DIM
NSA_QG_W = NSA_Q_W + 3 * NSA_HEADS
NSA_KV_W = 6 * NSA_GROUPS * NSA_HEAD_DIM
FFN_HIDDEN = ((8 * D_MODEL + 3 * 256 - 1) // (3 * 256)) * 256

kernel_name = "yoco_gdn_nsa_hybrid"

def rms_norm(x, g):
    xf = x.astype(jnp.float32)
    y = xf * lax.rsqrt(jnp.mean(xf * xf, axis=-1, keepdims=True) + NORM_EPS)
    return (y * g.astype(jnp.float32)).astype(x.dtype)

def l2_normalize(x):
    xf = x.astype(jnp.float32)
    return xf * lax.rsqrt(jnp.sum(xf * xf, axis=-1, keepdims=True) + L2_EPS)

def causal_short_conv(x, w):
    k_w, t = w.shape[0], x.shape[1]
    xp = jnp.pad(x, ((0, 0), (k_w - 1, 0), (0, 0)))
    y = xp[:, 0:t] * w[0]
    for j in range(1, k_w):
        y = y + xp[:, j:j + t] * w[j]
    return jax.nn.silu(y)

def chunk_gated_delta_rule(q, k, v, g, beta):
    f32 = jnp.float32
    b, t, h, dk = q.shape
    dv = v.shape[-1]
    c = GDN_CHUNK
    n = t // c

    def chunks(a):
        a = a.astype(f32).reshape((b, n, c, h) + a.shape[3:])
        return jnp.moveaxis(a, 3, 1)

    qc = chunks(q) * (dk ** -0.5)
    kc, vc, gc, bc = chunks(k), chunks(v), chunks(g), chunks(beta)
    gcum = jnp.cumsum(gc, axis=-1)
    causal = jnp.tril(jnp.ones((c, c), dtype=bool))
    strict = jnp.tril(jnp.ones((c, c), dtype=bool), k=-1)
    decay = jnp.exp(jnp.where(causal, gcum[..., :, None] - gcum[..., None, :], -jnp.inf))
    kb = kc * bc[..., None]
    a_mat = jnp.where(strict, jnp.einsum('bhncd,bhnsd->bhncs', kb, kc) * decay, 0.0) + jnp.eye(c, dtype=f32)
    rhs = jnp.concatenate([vc * bc[..., None], kb * jnp.exp(gcum)[..., None]], axis=-1)
    sol = lax.linalg.triangular_solve(a_mat, rhs, left_side=True, lower=True, unit_diagonal=True)
    u, w = sol[..., :dv], sol[..., dv:]
    qk = jnp.einsum('bhncd,bhnsd->bhncs', qc, kc) * decay
    q_dec = qc * jnp.exp(gcum)[..., None]
    g_last = gcum[..., -1]
    k_dec = kc * jnp.exp(g_last[..., None] - gcum)[..., None]

    def step(state, xs):
        u_i, w_i, qk_i, qd_i, kd_i, gl_i = xs
        v_new = u_i - jnp.einsum('bhcd,bhde->bhce', w_i, state)
        o_i = jnp.einsum('bhcd,bhde->bhce', qd_i, state) + jnp.einsum('bhcs,bhse->bhce', qk_i, v_new)
        state = state * jnp.exp(gl_i)[..., None, None] + jnp.einsum('bhcd,bhce->bhde', kd_i, v_new)
        return state, o_i

    xs = tuple(jnp.moveaxis(a, 2, 0) for a in (u, w, qk, q_dec, k_dec, g_last))
    s0 = jnp.zeros((b, h, dk, dv), f32)
    _, o = lax.scan(step, s0, xs)
    return jnp.transpose(o, (1, 0, 3, 2, 4)).reshape(b, t, h, dv)

def gated_deltanet(h, w_in, conv_w, a_log, dt_bias, o_norm, w_out):
    f32 = jnp.float32
    b, t, _ = h.shape
    proj = h @ w_in
    qkv, z, beta_logit, a = jnp.split(
        proj, [GDN_CONV_W, GDN_CONV_W + GDN_V_W, GDN_CONV_W + GDN_V_W + GDN_V_HEADS], axis=-1)
    qkv = causal_short_conv(qkv, conv_w)
    q, k, v = jnp.split(qkv, [GDN_QK_W, 2 * GDN_QK_W], axis=-1)
    rep = GDN_V_HEADS // GDN_QK_HEADS
    q = jnp.repeat(l2_normalize(q.reshape(b, t, GDN_QK_HEADS, GDN_HEAD_DIM)), rep, axis=2)
    k = jnp.repeat(l2_normalize(k.reshape(b, t, GDN_QK_HEADS, GDN_HEAD_DIM)), rep, axis=2)
    v = v.reshape(b, t, GDN_V_HEADS, GDN_HEAD_DIM)
    beta = jax.nn.sigmoid(beta_logit.astype(f32))
    g = -jnp.exp(a_log.astype(f32)) * jax.nn.softplus(a.astype(f32) + dt_bias.astype(f32))
    o = chunk_gated_delta_rule(q, k, v, g, beta)
    o = rms_norm(o, o_norm) * jax.nn.silu(z.reshape(b, t, GDN_V_HEADS, GDN_HEAD_DIM).astype(f32))
    return o.reshape(b, t, GDN_V_W).astype(h.dtype) @ w_out

def compress_blocks(x_raw, pos, w1, w2):
    b, g, t, d = x_raw.shape
    n_c = (t - CMP_BLOCK) // CMP_STRIDE + 1
    idx = CMP_STRIDE * jnp.arange(n_c)[:, None] + jnp.arange(CMP_BLOCK)[None, :]
    blocks = x_raw[:, :, idx] + pos
    flat = blocks.reshape(b, g, n_c, CMP_BLOCK * d)
    return jax.nn.silu(flat @ w1) @ w2

def nsa_shared_kv(h, kv_norm, kv_w, cmp_pos, cmp_w1, cmp_w2):
    b, t, _ = h.shape
    kv = rms_norm(h, kv_norm) @ kv_w
    kv = jnp.transpose(kv.reshape(b, t, 6, NSA_GROUPS, NSA_HEAD_DIM), (2, 0, 3, 1, 4))
    k_c = compress_blocks(kv[0], cmp_pos[0], cmp_w1[0], cmp_w2[0])
    v_c = compress_blocks(kv[1], cmp_pos[1], cmp_w1[1], cmp_w2[1])
    return k_c, v_c, kv[2], kv[3], kv[4], kv[5]

def masked_softmax(s, mask):
    s = jnp.where(mask, s.astype(jnp.float32), -jnp.inf)
    m = jnp.max(s, axis=-1, keepdims=True)
    m = jnp.where(jnp.isfinite(m), m, 0.0)
    e = jnp.where(mask, jnp.exp(s - m), 0.0)
    return e / jnp.maximum(jnp.sum(e, axis=-1, keepdims=True), 1e-30)

def selection_importance(p_cmp, n_sel):
    r = SEL_BLOCK // CMP_STRIDE
    c = CMP_BLOCK // CMP_STRIDE
    n_c = p_cmp.shape[-1]
    pp = jnp.pad(p_cmp, [(0, 0)] * (p_cmp.ndim - 1) + [(c - 1, r * n_sel - n_c)])
    out = jnp.zeros(p_cmp.shape[:-1] + (n_sel,), p_cmp.dtype)
    for m in range(r):
        for n in range(c):
            off = m - n + c - 1
            out = out + pp[..., off:off + r * n_sel:r]
    return out

def nsa_attention(h, w_qg, w_o, k_cmp, v_cmp, k_slc, v_slc, k_win, v_win):
    b, t, _ = h.shape
    G, R, Dh = NSA_GROUPS, NSA_REP, NSA_HEAD_DIM
    qg = h @ w_qg
    q = qg[..., :NSA_Q_W].reshape(b, t, G, R, Dh) * (Dh ** -0.5)
    gates = jax.nn.sigmoid(qg[..., NSA_Q_W:].astype(jnp.float32)).reshape(b, t, G, R, 3)
    n_c = k_cmp.shape[2]
    n_sel = t // SEL_BLOCK
    topk = min(SEL_TOPK, n_sel)
    cmp_end = CMP_STRIDE * jnp.arange(n_c) + CMP_BLOCK - 1
    blk = jnp.arange(n_sel)
    k_sel_blocks = k_slc.reshape(b, G, n_sel, SEL_BLOCK, Dh)
    v_sel_blocks = v_slc.reshape(b, G, n_sel, SEL_BLOCK, Dh)
    k_win_p = jnp.pad(k_win, ((0, 0), (0, 0), (WINDOW, 0), (0, 0)))
    v_win_p = jnp.pad(v_win, ((0, 0), (0, 0), (WINDOW, 0), (0, 0)))
    b_idx = jnp.arange(b)[:, None, None, None]
    g_idx = jnp.arange(G)[None, :, None, None]

    def query_block(i):
        s = i * Q_BLOCK
        qb = lax.dynamic_slice_in_dim(q, s, Q_BLOCK, axis=1)
        gb = lax.dynamic_slice_in_dim(gates, s, Q_BLOCK, axis=1)
        tq = s + jnp.arange(Q_BLOCK)
        sc = jnp.einsum('bqgrd,bgnd->bgrqn', qb, k_cmp)
        p_c = masked_softmax(sc, cmp_end[None, :] <= tq[:, None])
        o_c = jnp.einsum('bgrqn,bgnd->bqgrd', p_c, v_cmp)
        imp = selection_importance(jnp.sum(p_c, axis=2), n_sel)
        cur = tq // SEL_BLOCK
        forced = (blk[None, :] == 0) | (blk[None, :] == cur[:, None]) | (blk[None, :] == cur[:, None] - 1)
        valid = blk[None, :] * SEL_BLOCK <= tq[:, None]
        score = jnp.where(valid, jnp.where(forced, FORCED_SCORE, imp), -jnp.inf)
        _, sel = lax.top_k(score, topk)
        ks = k_sel_blocks[b_idx, g_idx, sel]
        vs = v_sel_blocks[b_idx, g_idx, sel]
        key_pos = sel[..., None] * SEL_BLOCK + jnp.arange(SEL_BLOCK)
        m_s = (key_pos <= tq[None, None, :, None, None]).reshape(b, G, 1, Q_BLOCK, topk * SEL_BLOCK)
        ss = jnp.einsum('bqgrd,bgqkld->bgrqkl', qb, ks).reshape(b, G, R, Q_BLOCK, topk * SEL_BLOCK)
        p_s = masked_softmax(ss, m_s).reshape(b, G, R, Q_BLOCK, topk, SEL_BLOCK)
        o_s = jnp.einsum('bgrqkl,bgqkld->bqgrd', p_s, vs)
        kw = lax.dynamic_slice_in_dim(k_win_p, s, Q_BLOCK + WINDOW, axis=2)
        vw = lax.dynamic_slice_in_dim(v_win_p, s, Q_BLOCK + WINDOW, axis=2)
        wpos = s - WINDOW + jnp.arange(Q_BLOCK + WINDOW)
        m_w = (wpos[None, :] >= 0) & (wpos[None, :] <= tq[:, None]) & (wpos[None, :] > tq[:, None] - WINDOW)
        sw = jnp.einsum('bqgrd,bgkd->bgrqk', qb, kw)
        o_w = jnp.einsum('bgrqk,bgkd->bqgrd', masked_softmax(sw, m_w), vw)
        return gb[..., 0:1] * o_c + gb[..., 1:2] * o_s + gb[..., 2:3] * o_w

    o = lax.map(query_block, jnp.arange(t // Q_BLOCK))
    o = jnp.moveaxis(o, 0, 1).reshape(b, t, NSA_Q_W).astype(h.dtype)
    return o @ w_o

def swiglu(h, w_in, w_out):
    gate, up = jnp.split(h @ w_in, 2, axis=-1)
    return (jax.nn.silu(gate) * up) @ w_out

def setup_inputs(seed: int = 0) -> dict:
    key = jax.random.key(seed)
    ks = jax.random.split(key, 24)
    f32 = jnp.float32
    n_b = DEPTH - N_A

    def nrm(k, shape, fan_in):
        return jax.random.normal(k, shape, f32) * (fan_in ** -0.5)

    def gain(k, shape):
        return 1.0 + 0.05 * jax.random.normal(k, shape, f32)

    dt = jnp.exp(jax.random.uniform(ks[10], (N_A, GDN_V_HEADS), f32, math.log(1e-3), math.log(1e-1)))
    return {
        "x": jax.random.normal(ks[0], (BATCH, SEQ, D_MODEL), f32),
        "p": jax.random.normal(ks[1], (DEPTH, BATCH, SEQ, PLE_DIM), f32),
        "mix_pre_norm": gain(ks[2], (DEPTH, D_MODEL)),
        "mix_post_norm": gain(ks[3], (DEPTH, D_MODEL)),
        "ffn_pre_norm": gain(ks[4], (DEPTH, D_MODEL)),
        "ffn_post_norm": gain(ks[5], (DEPTH, D_MODEL)),
        "gdn_w_in": nrm(ks[6], (N_A, D_MODEL, GDN_IN_W), D_MODEL),
        "gdn_conv_w": nrm(ks[7], (N_A, GDN_CONV, GDN_CONV_W), GDN_CONV),
        "gdn_a_log": jnp.log(jax.random.uniform(ks[8], (N_A, GDN_V_HEADS), f32, 1.0, 16.0)),
        "gdn_dt_bias": dt + jnp.log(-jnp.expm1(-dt)),
        "gdn_o_norm": gain(ks[9], (N_A, GDN_HEAD_DIM)),
        "gdn_w_out": nrm(ks[11], (N_A, GDN_V_W, D_MODEL), GDN_V_W),
        "kv_norm": gain(ks[12], (D_MODEL,)),
        "kv_w": nrm(ks[13], (D_MODEL, NSA_KV_W), D_MODEL),
        "cmp_pos": 0.1 * jax.random.normal(ks[14], (2, CMP_BLOCK, NSA_HEAD_DIM), f32),
        "cmp_w1": nrm(ks[15], (2, CMP_BLOCK * NSA_HEAD_DIM, CMP_HIDDEN), CMP_BLOCK * NSA_HEAD_DIM),
        "cmp_w2": nrm(ks[16], (2, CMP_HIDDEN, NSA_HEAD_DIM), CMP_HIDDEN),
        "nsa_w_qg": nrm(ks[17], (n_b, D_MODEL, NSA_QG_W), D_MODEL),
        "nsa_w_o": nrm(ks[18], (n_b, NSA_Q_W, D_MODEL), NSA_Q_W),
        "ffn_w_in": nrm(ks[19], (DEPTH, D_MODEL, 2 * FFN_HIDDEN), D_MODEL),
        "ffn_w_out": nrm(ks[20], (DEPTH, FFN_HIDDEN, D_MODEL), FFN_HIDDEN),
        "ple_w_in": nrm(ks[21], (DEPTH, PLE_DIM, D_MODEL), PLE_DIM),
        "ple_w_gate": nrm(ks[22], (DEPTH, D_MODEL, D_MODEL), D_MODEL),
    }

def reference(x, p, mix_pre_norm, mix_post_norm, ffn_pre_norm, ffn_post_norm,
              gdn_w_in, gdn_conv_w, gdn_a_log, gdn_dt_bias, gdn_o_norm, gdn_w_out,
              kv_norm, kv_w, cmp_pos, cmp_w1, cmp_w2, nsa_w_qg, nsa_w_o,
              ffn_w_in, ffn_w_out, ple_w_in, ple_w_gate):
    def channel_and_ple(h, i):
        f = swiglu(rms_norm(h, ffn_pre_norm[i]), ffn_w_in[i], ffn_w_out[i])
        h = h + rms_norm(f, ffn_post_norm[i])
        return h + (p[i] @ ple_w_in[i]) * jax.nn.sigmoid(h @ ple_w_gate[i])

    h = x
    for i in range(N_A):
        mix = gated_deltanet(rms_norm(h, mix_pre_norm[i]), gdn_w_in[i], gdn_conv_w[i], gdn_a_log[i],
                             gdn_dt_bias[i], gdn_o_norm[i], gdn_w_out[i])
        h = h + rms_norm(mix, mix_post_norm[i])
        h = channel_and_ple(h, i)
    k_cmp, v_cmp, k_slc, v_slc, k_win, v_win = nsa_shared_kv(h, kv_norm, kv_w, cmp_pos, cmp_w1, cmp_w2)
    for i in range(N_A, DEPTH):
        j = i - N_A
        mix = nsa_attention(rms_norm(h, mix_pre_norm[i]), nsa_w_qg[j], nsa_w_o[j],
                            k_cmp, v_cmp, k_slc, v_slc, k_win, v_win)
        h = h + rms_norm(mix, mix_post_norm[i])
        h = channel_and_ple(h, i)
    return h


_drawn_inputs = setup_inputs


def setup_inputs(seed=0):
    import zlib

    import numpy as np

    out = dict(_drawn_inputs(seed))
    spreads = {}
    factors = {}
    for name, (base, spread) in spreads.items():
        noise = np.random.default_rng([zlib.crc32(name.encode()), seed]).standard_normal(out[name].shape)
        drawn = base * np.exp(spread * noise) if base else spread * noise
        out[name] = __import__('jax').numpy.asarray(drawn.astype(out[name].dtype))
    for name, factor in factors.items():
        out[name] = (out[name] * factor).astype(out[name].dtype)
    return out
```

```python
from contextlib import ExitStack

import concourse.bass as bass
from concourse import mybir

P = 128
T = 256
TT = T // P
DM = 1024
KD = DM // P
HK, HV, HD = 8, 16, 128
CONVW = (2 * HK + HV) * HD
FFN = 2816
KF = FFN // P
NH, NG, ND = 16, 4, 64
NR = NH // NG
NC = (T - 32) // 16 + 1
QK_ORDER = (4, 0, 5, 1, 6, 2, 7, 3)
UW = 256
EPS = 1e-6
NEG = -1e30
N_BA = 18
N_CST = 24
N_DCST = 23
LV = 7

F32 = mybir.dt.float32
F32R = mybir.dt.float32r
BF16 = mybir.dt.bfloat16
ACT = mybir.ActivationFunctionType
ALU = mybir.AluOpType
AX = mybir.AxisListType.X

STAGES = [("qkv", 8, 1), ("z", 4, 1), ("gout", 4, 2), ("fin0", 11, 1), ("fout0", 8, 4), ("ple0", 4, 1),
          ("kv", 3, 1), ("q", 2, 1), ("wo", 2, 1), ("fin1", 11, 1), ("fout1", 8, 4), ("ple1", 4, 1)]
ORDER = [s[0] for s in STAGES]
PAIRS = {s[0]: s[1] for s in STAGES}
U0, B0 = {}, {}
_u = _b = 0
for _n, _p, _s in STAGES:
    U0[_n], B0[_n] = _u, _b
    _u += 2 * _p
    _b += 2 * _p // _s
FOUT_K = (6, 5, 6, 5)


def unit_k(stage, p):
    if stage.startswith("fout"):
        return FOUT_K[p]
    if stage.startswith("ple") and p == 0:
        return 2
    return 8


def build(nc, x, p, mix_pre_norm, mix_post_norm, ffn_pre_norm, ffn_post_norm, gdn_w_in, gdn_conv_w, gdn_a_log,
          gdn_dt_bias, gdn_o_norm, gdn_w_out, kv_norm, kv_w, cmp_pos, cmp_w1, cmp_w2, nsa_w_qg, nsa_w_o,
          ffn_w_in, ffn_w_out, ple_w_in, ple_w_gate, out):
    with ExitStack() as ctx:
        def sb(name, shape, dt=F32):
            return ctx.enter_context(nc.sbuf_tensor(name, shape, dt))

        def sem(name):
            return ctx.enter_context(nc.semaphore(name))

        raw = sb("w_raw", [P, 2, 8 * UW])
        whi = sb("w_hi", [P, 2, 8 * UW], F32R)
        wlo = sb("w_lo", [P, 2, 8 * UW], F32R)
        xhi = sb("x_hi", [P, KD, T], F32R)
        xlo = sb("x_lo", [P, KD, T], F32R)
        h = sb("h", [P, KD, T])
        scr = sb("scr", [P, 16, T])
        y, sq = scr[:, 0:KD, :], scr[:, KD:16, :]
        qkvT = sb("qkvT", [P, 32, T])
        rpre = sb("rstd_pre", [P, T])
        rpost = sb("rstd_post", [P, T])
        rcol = sb("rstd_col", [P, TT])
        epsc = sb("eps_cols", [P, 4])
        ident = sb("ident", [P, P])
        identb = sb("identb", [P, P], BF16)
        causb = sb("causb", [P, P], BF16)
        ones = sb("ones", [P, P])
        tri_le = sb("tri_le", [P, P])
        tri_gt = sb("tri_gt", [P, P])
        masks = sb("level_masks", [P, LV, P])
        m1t = sb("first_level_mask", [P, P])
        rows = sb("vector_rows", [P, P])
        crows = sb("conv_rows", [P, P])
        vecs = sb("vectors", [P, P])
        cw = sb("conv_cols", [P, 4, 32])
        wba = sb("w_beta_a", [P, KD, 2 * HV])
        wgt = sb("w_gates", [P, KD, 3 * NH])
        dtb = sb("dt_bias_b", [P, HV])
        alog = sb("a_log_b", [P, HV])
        w2k = sb("w2k", [P, 2, 2, ND])
        w2v = sb("w2v", [P, 2, ND])
        ptok = sb("p_tok", [P, 2, TT, 256])
        gates = sb("gates", [P, TT, 3 * NH])
        small = sb("small", [P, 12, TT, HV])
        beta, gdec, einc, faft, nbe = (small[:, i] for i in range(5))
        sm = [small[:, i] for i in range(5, 12)]
        balog = sb("beta_a_logits", [P, TT, 2 * HV])
        cmask = sb("cmp_mask", [P, TT, NC])
        rmask = sb("row_masks", [P, NR])
        hcol = sb("head_rstd_cols", [P, TT, 16])
        tcol = sb("table_cols", [P, 12])
        cst = sb("cmp_stats", [P, 3, TT * NH])
        hst = sb("head_stats", [P, 2, 3, 4])
        with nc.sbuf_tensor("big", [P, 2 * KF, T], F32R) as big:
            pass
        gdn = sb("gdn", [P, 12288])

        def views(base):
            used = [0]

            def take(*shape):
                n = 1
                for v in shape:
                    n *= v
                v = base[:, used[0]:used[0] + n]
                used[0] += n
                assert used[0] <= base.shape[1], used[0]
                names = "abcd"[:len(shape)]
                return v.rearrange(f"p ({' '.join(names)}) -> p {' '.join(names)}", **dict(zip(names, shape))) \
                    if len(shape) > 1 else v
            return take

        xtok = views(gdn)(TT, DM)
        ar = views(gdn)
        pre = ar(2, 2, T + 3)
        acc = ar(2, 2, T)
        ar = views(gdn)
        dA = ar(2, 4, P)
        dQ = ar(2, 4, P)
        eq = ar(4, P)
        gtri = ar(2, 4, P)
        TTr = ar(2, 4, P)
        Tr = ar(2, 4, P)
        ktok = ar(2, 2, P)
        bv = ar(2, 4, P)
        Ss = ar(4, P)
        vn = ar(2, 4, P)
        kqf = ar(4, T)
        vf = ar(4, T)
        yb = ar(2, 4, P)
        osq = views(gdn)(16, T)
        zT = scr
        oT = qkvT[:, 16:32, :]
        pw1 = gdn[:, 4096:12288].rearrange("p (v c n) -> p v c n", v=2, c=16)
        qkvf = qkvT[:, :, :].rearrange("p a b -> p (a b)")
        ar = views(qkvf)
        t0 = ar(2, 2, T)
        t1 = ar(2, 2, T)
        t2 = ar(2, 2, T)
        ar = views(qkvf)
        kdup = ar(2, NG, T)
        vtk = ar(2, TT, T)
        ckv = ar(2, 2, T)
        ablk = ar(2, 16, 61)
        hid = ar(2, 2, 60)
        kcd = ar(60)
        vrep = ar(NG, ND)
        cb = ar(2, 2)
        hrep = ar(NG, 2, 60)
        cs = ar(TT, NH, NC)
        qT = scr[:, 0:8, :]
        ar = views(scr[:, 8:16, :].rearrange("p a b -> p (a b)"))
        pr0 = ar(2, 2, P)
        pr1 = ar(2, 2, T)
        qf = ar(2, T)
        ar = views(gdn[:, 4096:12288])
        pct = ar(NG, T)
        kf = ar(2, T)
        vff = ar(2, TT, ND)
        pcf = ar(T)
        vz = ar(NR, ND)
        pts = ar(2, 3, P)
        otok = scr[:, 0:8, :].rearrange("p (a b) t -> p a (b t)", a=TT)

        ps = ctx.enter_context(nc.psum_tensor("ps", [P, 8, 512], F32))

        def bank(b, *shape):
            n = 1
            for v in shape:
                n *= v
            v = ps[:, b, 0:n]
            names = "abcd"[:len(shape)]
            return v.rearrange(f"p ({' '.join(names)}) -> p {' '.join(names)}", **dict(zip(names, shape))) \
                if len(shape) > 1 else v

        def over(ap, axis, n):
            shape = list(ap.shape)
            shape.insert(axis, n)
            return ap.unsqueeze(axis).to_broadcast(shape)

        def gain(col, k):
            return vecs[:, col + k:col + k + 1]
        MIXPRE, MIXPOST, FFNPRE, FFNPOST, KVN, ONORM, POS = (0, 8), (16, 24), (32, 40), (48, 56), 64, 72, 96

        landed = [sem("landed0"), sem("landed1")]
        S = {}
        for name in ("hi_done lo_done unit_done bank_free x_in vec_in small_in cst_pool cst_dve xt_ps h_ready "
                     "sq_ready stat_ps root_done rstd_done xhi_done xlo_done vec_ps vec_sb rc_ps rc_root rcol_done ba_ps ba_dve ba_act "
                     "conv_dve conv_done silu_done l2_sq l2_ps l2_root l2_done gtri_done decay_ps decay_sb kq_ps a_sb qk_raw "
                     "kqf_sb vf_sb hrec l2_rows on_rows "
                     "qk_sb qdec_sb tinit y_ps y_sb z_ps t_upd ktok_ps ktok_sb vtok_ps bv_sb u_ps vn_sb fv_sb s_ps s_sb "
                     "ks_ps r1_sb o_ps oT_sb on_sq on_ps on_root on_done cum_ps cum_act cum_dve sz_done oz_done ohi_done olo_done "
                     "yn_done sg_done hid_done fhi_done flo_done pt_ps phi_done plo_done sgm_done pl_t "
                     "ablk_act ablk_dve hrep_sb pts_act pts_dve out_act w1_in hid_ps hb_sb hid_sb kc_ps kc_sb "
                     "gt_ps gt_dve gt_done cs_ps cs_dve cs_act pct_ps pct_sb fx_act fx_dve "
                     "sc_ps mx_dve p_act rl_dve pw_dve ptr_ps pts_sb av_ps ahi alo out_ps out_sb out_st").split():
            S[name] = sem(name)

        def block_copies(copy, v, done):
            for par in range(2):
                for e in range(2):
                    src = ckv[64 * e:64 * e + 64, v].rearrange("p t (n c r) -> p c t n r", c=8, r=2)[:, :, :, :, par]
                    dst = ablk[64 * par:64 * par + 64, v, :, 0:60].rearrange("p c (t e n) -> p c t e n", t=2, e=2)
                    for half in range(2):
                        for t in range(2):
                            last = copy(dst[:, 8 * half:8 * half + 8, t, e, :], src[:, :, t, half:half + NC], *cargs(v))
                        last.then_inc(done, 1)
            copy(ablk[:, v, :, 60], vecs[:, POS + 16 * v:POS + 16 * v + 16], *cargs(v)).then_inc(done, 1)

        def cargs(v):
            return (ACT.Copy,) if v == 0 else ()

        block = ctx.enter_context(nc.Block())

        win = gdn_w_in[0].rearrange("(k p) n -> p k n", p=P)
        wout = gdn_w_out[0].rearrange("(k p) n -> p k n", p=P)
        fin = [ffn_w_in[i].rearrange("(k p) n -> p k n", p=P) for i in range(2)]
        fout = [ffn_w_out[i].rearrange("(k p) n -> p k n", p=P) for i in range(2)]
        pin = [ple_w_in[i].rearrange("(k p) n -> p k n", p=P) for i in range(2)]
        pgt = [ple_w_gate[i].rearrange("(k p) n -> p k n", p=P) for i in range(2)]
        wkv = kv_w.rearrange("(k p) n -> p k n", p=P)
        wqg = nsa_w_qg[0].rearrange("(k p) n -> p k n", p=P)
        wwo = nsa_w_o[0].rearrange("(k p) n -> p k n", p=P)

        def source(stage, i, q):
            cols = bass.ds(i * (2 * UW) + q * UW, UW)
            one = bass.ds(i * UW, UW)
            if stage == "qkv":
                return win[:, :, cols]
            if stage == "z":
                return win[:, :, bass.ds(i * (2 * UW) + (CONVW + q * UW), UW)]
            if stage == "gout":
                return wout[:, 8 * q:8 * q + 8, one]
            if stage[:3] == "fin":
                w = fin[int(stage[3])]
                return w[:, :, one] if q == 0 else w[:, :, bass.ds(i * UW + FFN, UW)]
            if stage[:4] == "fout":
                k = sum(FOUT_K[:q])
                return fout[int(stage[4])][:, k:k + FOUT_K[q], one]
            if stage[:3] == "ple":
                return (pin if q == 0 else pgt)[int(stage[3])][:, :, one]
            return {"kv": wkv, "q": wqg, "wo": wwo}[stage][:, :, cols]


        @block.sync
        def _(sp):
            def load(stage, i, q):
                n = unit_k(stage, q) * UW
                sp.dma_start(raw[:, q % 2, 0:n].rearrange("p (k n) -> p k n", n=UW),
                             source(stage, i, q)).then_inc(landed[q % 2], 16)

            sp.dma_start(xtok, x[0].rearrange("(a p) d -> p a d", p=P)).then_inc(S["x_in"], 16)
            for stage in ORDER:
                per = 4 if stage.startswith("fout") else 2
                first = 0
                if stage == "qkv":
                    first = 1
                    for q in range(per):
                        load(stage, 0, q)
                with sp.Fori(first, PAIRS[stage] * 2 // per) as i:
                    for q in range(per):
                        sp.wait_ge(S["lo_done"], i * per + (U0[stage] + q - 1))
                        load(stage, i, q)
            for a in range(TT):
                sp.wait_ge(S["out_sb"], a + 1)
                sp.wait_ge(S["out_act"], a + 1)
                sp.dma_start(out[0, a * P:(a + 1) * P, :], otok[:, a, :]).then_inc(S["out_st"], 16)
            sp.wait_ge(S["out_st"], 16 * TT)

        @block.gpsimd
        def _(pool):
            g = nc.gpsimd
            pool.dma_start(wba[:, :, :], win[:, :, 6144:6176]).then_inc(S["small_in"], 16)
            pool.dma_start(dtb[:, :], gdn_dt_bias[0].partition_broadcast(P)).then_inc(S["small_in"], 16)
            pool.dma_start(alog[:, :], gdn_a_log[0].partition_broadcast(P)).then_inc(S["small_in"], 16)
            pool.dma_start(wgt[:, :, :], wqg[:, :, 1024:1072]).then_inc(S["small_in"], 16)
            for d in range(2):
                pool.dma_start(w2k[:, :, d, :], cmp_w2[0].rearrange("(c p) n -> p c n", p=P)).then_inc(S["small_in"], 16)
            pool.dma_start(w2v[:, :, :], cmp_w2[1].rearrange("(c p) n -> p c n", p=P)).then_inc(S["small_in"], 16)
            for i in range(2):
                pool.dma_start(ptok[:, i], p[i, 0].rearrange("(a p) d -> p a d", p=P)).then_inc(S["small_in"], 16)

            n = [0]

            def sel(dst, src, op, fill, base, pattern, cm):
                if n[0]:
                    pool.wait_ge(S["cst_pool"], n[0])
                g.affine_select(out=dst, in_=src, compare_op=op, fill=fill, base=base, pattern=pattern,
                                channel_multiplier=cm).then_inc(S["cst_pool"], 1)
                n[0] += 1
            pool.wait_ge(S["cst_dve"], N_DCST)
            sel(ident[:, :], ident[:, :], ALU.not_equal, 1.0, 0, [[-1, P]], 1)
            sel(tri_le[:, :], ones[:, :], ALU.is_ge, 0.0, 0, [[1, P]], -1)
            sel(tri_gt[:, :], ones[:, :], ALU.is_gt, 0.0, 0, [[-1, P]], 1)
            sel(identb[:, :], ident[:, :], ALU.is_ge, 0.0, 0, [[0, P]], 0)
            sel(causb[:, :], causb[:, :], ALU.is_ge, NEG, 0, [[-1, P]], 1)
            sel(cmask[:, :, :], cmask[:, :, :], ALU.is_ge, NEG, -31, [[P, TT], [-16, NC]], 1)
            for v in range(LV):
                b = 1 << v
                m = masks[:, v, :].rearrange("p (m e b) -> p m e b", e=2, b=b)[:, :, 1, :]
                sel(m, m, ALU.is_ge, 0.0, 0, [[-2 * b, 64 // b], [0, b]], 1)
                sel(m, m, ALU.is_ge, 0.0, b - 1, [[2 * b, 64 // b], [0, b]], -1)
            m1 = m1t[:, :].rearrange("p (m e) -> p m e", e=2)
            sel(m1, m1, ALU.is_equal, 0.0, -1, [[-2, 64], [0, 2]], 1)
            sel(m1, m1, ALU.is_equal, 0.0, 0, [[0, 64], [1, 2]], 0)
            sel(rmask[:, :], rmask[:, :], ALU.is_ge, 0.0, 0, [[-NC, NR]], 1)
            sel(rmask[:, :], rmask[:, :], ALU.is_ge, 0.0, NC - 1, [[NC, NR]], -1)
            assert n[0] == N_CST

            pool.wait_ge(S["ba_dve"], N_BA)
            pool.wait_ge(S["conv_done"], 16)
            with pool.Fori(0, 4) as j:
                pool.wait_ge(S["decay_ps"], j * 5)
                for c in range(2):
                    g.tensor_tensor(gtri[:, c], over(gdec[:, c, bass.ds(j * 4, 4)], 2, P), over(tri_le[:, :], 1, 4),
                                    ALU.mult).then_inc(S["gtri_done"], 1)
                for c in range(2):
                    pool.wait_ge(S["a_sb"], j * 2 + (c + 1))
                    g.tensor_tensor(Tr[:, c], dA[:, c], over(m1t[:, :], 1, 4), ALU.mult).then_inc(S["tinit"], 1)
                    pool.wait_ge(S["tinit"], j * 4 + (2 * c + 1))
                    g.tensor_tensor(Tr[:, c], over(ident[:, :], 1, 4), Tr[:, c], ALU.subtract).then_inc(S["tinit"], 1)
                for c in range(2):
                    pool.wait_ge(S["qk_raw"], j * 2 + (c + 1))
                    g.tensor_tensor(dQ[:, c], dQ[:, c], over(tri_le[:, :], 1, 4), ALU.mult).then_inc(S["qk_sb"], 1)
            pool.wait_ge(S["unit_done"], U0["ple0"])
            pool.wait_ge(S["plo_done"], 1)
            for v in range(2):
                pool.dma_start(pw1[:, v], cmp_w1[v].rearrange("(c p) n -> p c n", p=P)).then_inc(S["w1_in"], 16)

        @block.tensor
        def _(pe):
            mm = nc.tensor.matmul

            def transpose(o, i):
                return nc.tensor.transpose(o, i, ident[:, :])

            def stage_pair(name, xh, xl, i, bank_wait=True):
                for q in range(2):
                    kc = unit_k(name, q)
                    pe.wait_ge(S["lo_done"], i * 2 + (U0[name] + q + 1))
                    if bank_wait:
                        pe.wait_ge(S["bank_free"], i * 2 + (B0[name] + q - 1))
                    xa, xb = (bighi, plelo) if name.startswith("ple") and q == 0 else (xh, xl)
                    for tile in range(2):
                        o = bank(q, 2, T)[:, tile, :]
                        for k in range(kc):
                            col = k * UW + tile * P
                            mm(o, whi[:, q, col:col + P], xa(k), start=k == 0, stop=False)
                            mm(o, whi[:, q, col:col + P], xb(k), start=False, stop=False)
                            last = mm(o, wlo[:, q, col:col + P], xa(k), start=False, stop=k == kc - 1)
                    last.then_inc(S["unit_done"], 1)

            def values_unit(name, i):
                pe.wait_ge(S["lo_done"], i * 2 + (U0[name] + 2))
                pe.wait_ge(S["bank_free"], i * 2 + B0[name])
                for a in range(TT):
                    o = bank(1, TT, T)[:, a, :]
                    tok = slice(a * P, (a + 1) * P)
                    for k in range(KD):
                        w_h, w_l = whi[:, 1, k * UW:(k + 1) * UW], wlo[:, 1, k * UW:(k + 1) * UW]
                        mm(o, xhi[:, k, tok], w_h, start=k == 0, stop=False)
                        mm(o, xhi[:, k, tok], w_l, start=False, stop=False)
                        last = mm(o, xlo[:, k, tok], w_h, start=False, stop=k == KD - 1)
                last.then_inc(S["unit_done"], 1)

            def keys_unit(name, i):
                pe.wait_ge(S["lo_done"], i * 2 + (U0[name] + 1))
                pe.wait_ge(S["bank_free"], i * 2 + (B0[name] - 1))
                for tile in range(2):
                    o = bank(0, 2, T)[:, tile, :]
                    for k in range(KD):
                        col = k * UW + tile * P
                        mm(o, whi[:, 0, col:col + P], xhi[:, k, :], start=k == 0, stop=False)
                        mm(o, whi[:, 0, col:col + P], xlo[:, k, :], start=False, stop=False)
                        last = mm(o, wlo[:, 0, col:col + P], xhi[:, k, :], start=False, stop=k == KD - 1)
                last.then_inc(S["unit_done"], 1)

            def x_hi(k):
                return xhi[:, k, :]

            def x_lo(k):
                return xlo[:, k, :]

            def bighi(k):
                return big[:, k, :]

            def biglo(k):
                return big[:, KF + k, :]

            def plelo(k):
                return big[:, 2 + k, :]

            def biglo8(k):
                return big[:, KD + k, :]

            def accumulating(name, ks, operand=lambda k: None):
                per = len(ks)
                with pe.Fori(0, 2) as i:
                    for grp in range(2):
                        for q in range(per):
                            pe.wait_ge(S["lo_done"], i * (2 * per) + (U0[name] + grp * per + q + 1))
                            if q == 0:
                                pe.wait_ge(S["bank_free"], i * 2 + (B0[name] + grp - 1))
                            k0 = sum(ks[:q])
                            for k in range(ks[q]):
                                if grp == 0:
                                    operand(k0 + k)
                                for tile in range(2):
                                    o = bank(grp, 2, T)[:, tile, :]
                                    col = k * UW + tile * P
                                    f = q == 0 and k == 0 and tile == 0
                                    e = q == per - 1 and k == ks[q] - 1
                                    w_h, w_l = whi[:, q % 2, col:col + P], wlo[:, q % 2, col:col + P]
                                    mm(o, w_h, bighi(k0 + k), start=f, stop=False, skip_group_check=True)
                                    mm(o, w_h, biglo(k0 + k), start=False, stop=False, skip_group_check=True)
                                    last = mm(o, w_l, bighi(k0 + k), start=False, stop=e, skip_group_check=True)
                            last.then_inc(S["unit_done"], 1)

            def stats(n, cols=False):
                pe.wait_ge(S["sq_ready"], 4 * n + 4)
                if n:
                    pe.wait_ge(S["root_done"], n)
                for k in range(KD):
                    last = mm(bank(2, T), ones[:, :], sq[:, k, :], start=(k == 0), stop=(k == KD - 1))
                last.then_inc(S["stat_ps"], 1)
                if cols:
                    for a in range(TT):
                        for k in range(KD):
                            last = mm(bank(3, TT)[:, a:a + 1], sq[:, k, a * P:(a + 1) * P], ones[:, 0:1],
                                      start=(k == 0), stop=(k == KD - 1))
                    last.then_inc(S["rc_ps"], 1)

            def tokens_by(w, b, n, hi_k, lo_k, done):
                for a in range(TT):
                    tok = slice(a * P, (a + 1) * P)
                    for k in range(KD):
                        mm(bank(b, TT, n)[:, a, :], hi_k(k)[:, tok].bitcast(F32), w[:, k, :], start=k == 0, stop=False)
                        last = mm(bank(b, TT, n)[:, a, :], lo_k(k)[:, tok].bitcast(F32), w[:, k, :], start=False,
                                  stop=k == KD - 1)
                last.then_inc(done, 1)

            pe.wait_ge(S["cst_pool"], 1)
            pe.wait_ge(S["x_in"], 16)
            for k in range(KD):
                for a in range(TT):
                    last = transpose(bank(4 + k // 2, 2, T)[:, k % 2, a * P:(a + 1) * P], xtok[:, a, k * P:(k + 1) * P])
                if k % 2:
                    last.then_inc(S["xt_ps"], 1)
            pe.wait_ge(S["vec_in"], 16 * 8)
            transpose(bank(3, 4, P)[:, 0, :], rows[:, :])
            transpose(bank(3, 4, P)[:, 1, :], crows[:, :]).then_inc(S["vec_ps"], 1)
            pe.wait_ge(S["vec_sb"], 2)
            stats(0, cols=True)
            pe.wait_ge(S["xlo_done"], 8)
            pe.wait_ge(S["small_in"], 16 * 9)
            tokens_by(wba, 4, 2 * HV, x_hi, x_lo, S["ba_ps"])
            stage_pair("qkv", x_hi, x_lo, 0, bank_wait=False)
            def head_sums(src, ready, done):
                for s in range(8):
                    pe.wait_ge(ready, s + 1)
                    for hd in (2 * s, 2 * s + 1):
                        for a in range(TT):
                            last = mm(bank(2, TT, 16)[:, a, hd:hd + 1], src[:, hd, a * P:(a + 1) * P], ones[:, 0:1],
                                      start=True, stop=True)
                last.then_inc(done, 1)

            def head_rows(order, ready, freed, done):
                pe.wait_ge(ready, 1)
                for n, s in enumerate(order):
                    if n >= 4:
                        pe.wait_ge(freed, n - 3)
                    for e in range(2):
                        for a in range(TT):
                            last = mm(bank((3, 4, 5, 6)[n % 4], 2, T)[:, e, a * P:(a + 1) * P],
                                      hcol[:, a, 2 * s + e:2 * s + e + 1].to_broadcast([P, P]), ident[:, :],
                                      start=True, stop=True)
                    last.then_inc(done, 1)

            with pe.Fori(1, 6) as i:
                stage_pair("qkv", x_hi, x_lo, i)
            pe.wait_ge(S["root_done"], 1)
            head_sums(scr, S["l2_sq"], S["l2_ps"])
            with pe.Fori(6, PAIRS["qkv"]) as i:
                stage_pair("qkv", x_hi, x_lo, i)
            pe.wait_ge(S["ba_dve"], N_BA)
            pe.wait_ge(S["cst_pool"], N_CST)
            gflat = gdec.rearrange("p a h -> p (a h)")
            mm(bank(7, 2, 32)[:, 0, :], tri_le[:, :], gflat, start=True, stop=True)
            mm(bank(7, 2, 32)[:, 1, :], tri_gt[:, :], gflat, start=True, stop=True).then_inc(S["cum_ps"], 1)

            head_rows(QK_ORDER, S["hrec"], S["l2_done"], S["l2_rows"])

            pe.wait_ge(S["l2_done"], 8)
            pe.wait_ge(S["cum_act"], 2)
            with pe.Fori(0, 4) as j:
                pe.wait_ge(S["bank_free"], j * 2 + B0["z"])
                pe.wait_ge(S["oT_sb"], j * 2 + 1)
                pe.wait_ge(S["kqf_sb"], j * 2 + 2)
                for c in range(2):
                    tok = slice(c * P, (c + 1) * P)
                    for i in range(2):
                        mm(bank(c, 4, P)[:, i, :], kqf[:, i, tok], kqf[:, i, tok], start=True, stop=True)
                        last = mm(bank(c, 4, P)[:, 2 + i, :], kqf[:, i, tok], kqf[:, 2 + i, tok], start=True, stop=True)
                    last.then_inc(S["kq_ps"], 1)
                for c in range(2):
                    pe.wait_ge(S["gtri_done"], j * 2 + (c + 1))
                    mm(bank(2 + 2 * c, 4, P), tri_gt[:, :], gtri[:, c], start=True, stop=True).then_inc(S["decay_ps"], 1)
                    for e in range(4):
                        last = mm(bank(3 + 2 * c, 4, P)[:, e, :], gtri[:, c, e, :], tri_gt[:, :], start=True, stop=True)
                    last.then_inc(S["decay_ps"], 1)
                mm(bank(6, 4, P), ones[:, :], gtri[:, 1], start=True, stop=True).then_inc(S["decay_ps"], 1)
                for c in range(2):
                    for i in range(2):
                        last = transpose(bank(7, 2, 2, P)[:, c, i, :], kqf[:, i, c * P:(c + 1) * P])
                last.then_inc(S["ktok_ps"], 1)
                pe.wait_ge(S["vf_sb"], j + 1)
                for c in range(2):
                    pe.wait_ge(S["decay_sb"], j * 5 + (2 * c + 1))
                    for e in range(4):
                        last = transpose(bank(2 + 2 * c, 4, P)[:, e, :], vf[:, e, c * P:(c + 1) * P])
                    last.then_inc(S["vtok_ps"], 1)

                def y_products(v, c):
                    if v == 0:
                        pe.wait_ge(S["a_sb"], j * 2 + (c + 1))
                        pe.wait_ge(S["decay_sb"], j * 5 + (2 * c + 2))
                    else:
                        pe.wait_ge(S["t_upd"], j * 14 + (2 * (v - 1) + c + 1))
                    for e in range(4):
                        src = ident[:, :] if v == 0 else TTr[:, c, e, :]
                        last = mm(bank(3 + 2 * c, 4, P)[:, e, :], dA[:, c, e, :], src, start=True, stop=True)
                    last.then_inc(S["y_ps"], 1)

                def z_products(v, c):
                    if v == 1:
                        pe.wait_ge(S["tinit"], j * 4 + (2 * c + 2))
                        if c == 0:
                            pe.wait_ge(S["decay_sb"], j * 5 + 5)
                        else:
                            pe.wait_ge(S["ktok_sb"], j + 1)
                        pe.wait_ge(S["qk_raw"], j * 2 + (c + 1))
                    pe.wait_ge(S["y_sb"], j * 14 + (2 * v + c + 1))
                    for e in range(4):
                        last = mm(bank(6 + c, 4, P)[:, e, :], Tr[:, c, e, :], yb[:, c, e, :], start=True, stop=True)
                        if v < LV - 1:
                            last = mm(bank(c, 4, P)[:, e, :], yb[:, c, e, :], Tr[:, c, e, :], start=True, stop=True)
                    last.then_inc(S["z_ps"], 1)

                def z_tile(q, tile):
                    if tile == 0:
                        pe.wait_ge(S["lo_done"], j * 2 + (U0["z"] + q + 1))
                    o = bank(6 + q, 2, T)[:, tile, :]
                    for k in range(KD):
                        col = k * UW + tile * P
                        mm(o, whi[:, q, col:col + P], xhi[:, k, :], start=k == 0, stop=False)
                        mm(o, whi[:, q, col:col + P], xlo[:, k, :], start=False, stop=False)
                        last = mm(o, wlo[:, q, col:col + P], xhi[:, k, :], start=False, stop=k == KD - 1)
                    if tile == 1:
                        last.then_inc(S["unit_done"], 1)

                y_products(0, 0)
                y_products(0, 1)
                for v in range(1, LV):
                    y_products(v, 0)
                    if v > 1:
                        z_products(v - 1, 1)
                    z_products(v, 0)
                    y_products(v, 1)
                z_products(LV - 1, 1)
                pe.wait_ge(S["t_upd"], j * 14 + 13)
                pe.wait_ge(S["bv_sb"], j * 2 + 1)
                pe.wait_ge(S["qk_raw"], j * 2 + 1)
                for e in range(4):
                    last = mm(bank(0, 4, P)[:, e, :], TTr[:, 0, e, :], bv[:, 0, e, :], start=True, stop=True)
                last.then_inc(S["u_ps"], 1)
                z_tile(0, 0)
                pe.wait_ge(S["fv_sb"], j + 1)
                pe.wait_ge(S["ktok_sb"], j + 1)
                for e in range(4):
                    last = mm(bank(2, 4, P)[:, e, :], ktok[:, 0, e // 2, :], bv[:, 0, e, :], start=True, stop=True)
                last.then_inc(S["s_ps"], 1)
                pe.wait_ge(S["vn_sb"], j * 2 + 1)
                pe.wait_ge(S["qk_sb"], j * 2 + 1)
                for e in range(4):
                    last = mm(bank(3, 4, P)[:, e, :], vn[:, 0, e, :], dQ[:, 0, e, :], start=True, stop=True)
                last.then_inc(S["o_ps"], 1)
                pe.wait_ge(S["s_sb"], j + 1)
                pe.wait_ge(S["bv_sb"], j * 2 + 2)
                for e in range(4):
                    last = mm(bank(4, 4, P)[:, e, :], kqf[:, e // 2, P:T], Ss[:, e, :], start=True, stop=True)
                last.then_inc(S["ks_ps"], 1)
                z_tile(0, 1)
                pe.wait_ge(S["r1_sb"], j + 1)
                pe.wait_ge(S["t_upd"], j * 14 + 14)
                for e in range(4):
                    last = mm(bank(1, 4, P)[:, e, :], TTr[:, 1, e, :], bv[:, 1, e, :], start=True, stop=True)
                last.then_inc(S["u_ps"], 1)
                z_tile(1, 0)
                pe.wait_ge(S["vn_sb"], j * 2 + 2)
                pe.wait_ge(S["qk_sb"], j * 2 + 2)
                pe.wait_ge(S["qdec_sb"], j + 1)
                for e in range(4):
                    mm(bank(5, 4, P)[:, e, :], Ss[:, e, :], eq[:, e, :], start=True, stop=False)
                    last = mm(bank(5, 4, P)[:, e, :], vn[:, 1, e, :], dQ[:, 1, e, :], start=False, stop=True)
                last.then_inc(S["o_ps"], 1)
                z_tile(1, 1)
            pe.wait_ge(S["oT_sb"], 9)
            head_sums(osq, S["on_sq"], S["on_ps"])
            pe.wait_ge(S["bank_free"], B0["gout"])
            pe.wait_ge(S["hrec"], 2)
            head_rows(range(8), S["hrec"], S["on_done"], S["on_rows"])
            accumulating("gout", (8, 8), lambda k: pe.wait_ge(S["olo_done"], k // 2 + 1) if k % 2 == 0 else None)
            stats(1)

            def ffn_and_ple(layer):
                n = 2 + 4 * layer
                stats(n)
                pe.wait_ge(S["xlo_done"], 8 * (2 + 4 * layer))
                with pe.Fori(0, PAIRS["fin0"]) as i:
                    stage_pair(f"fin{layer}", x_hi, x_lo, i)
                pe.wait_ge(S["flo_done"], 11 * (layer + 1))
                accumulating(f"fout{layer}", FOUT_K)
                for k in range(2):
                    for a in range(TT):
                        last = transpose(bank(3, 2, T)[:, k, a * P:(a + 1) * P], ptok[:, layer, a, k * P:(k + 1) * P])
                last.then_inc(S["pt_ps"], 1)
                stats(n + 1)
                pe.wait_ge(S["xlo_done"], 8 * (3 + 4 * layer))
                pe.wait_ge(S["plo_done"], layer + 1)
                with pe.Fori(0, PAIRS["ple0"]) as i:
                    stage_pair(f"ple{layer}", x_hi, x_lo, i)

            ffn_and_ple(0)

            stats(4, cols=True)
            pe.wait_ge(S["xlo_done"], 8 * 4)
            stage_pair("kv", x_hi, x_lo, 0)
            for i in (1, 2):
                keys_unit("kv", i)
                values_unit("kv", i)
            pe.wait_ge(S["w1_in"], 32)
            pe.wait_ge(S["ablk_act"], 9)
            pe.wait_ge(S["ablk_dve"], 9)
            for v in range(2):
                for e in range(2):
                    for c in range(16):
                        last = mm(bank(4 + v, 2, 61)[:, e, :], pw1[:, v, c, e * P:(e + 1) * P], ablk[:, v, c, :],
                                  start=c == 0, stop=c == 15)
            last.then_inc(S["hid_ps"], 1)
            pe.wait_ge(S["xlo_done"], 8 * 5)
            tokens_by(wgt, 7, 3 * NH, bighi, biglo8, S["gt_ps"])
            for i in range(2):
                stage_pair("q", bighi, biglo8, i)
            pe.wait_ge(S["hid_sb"], 4)
            for e in range(2):
                last = mm(bank(6, 60), w2k[:, e].rearrange("p d n -> p (d n)"), hid[:, 0, e, :], start=e == 0, stop=e == 1)
            last.then_inc(S["kc_ps"], 1)
            pe.wait_ge(S["gt_dve"], 2)
            for gr in range(NG):
                for e in range(2):
                    last = mm(ps[0:60, 7, gr * ND:(gr + 1) * ND],
                              hrep[:, gr, e, :], w2v[:, e, :], start=e == 0, stop=e == 1)
            last.then_inc(S["kc_ps"], 1)
            pe.wait_ge(S["kc_sb"], 1)
            pe.wait_ge(S["bank_free"], B0["wo"])
            for a in range(TT):
                for hd in range(NH):
                    half = slice(64 * (hd % 2), 64 * (hd % 2) + 64)
                    last = mm(bank(3 - hd % 2, TT, NH // 2, NC)[:, a, hd // 2, :], qT[half, hd // 2, a * P:(a + 1) * P],
                              kcd[half, (hd // NR) * NC:(hd // NR + 1) * NC], start=True, stop=True)
            last.then_inc(S["cs_ps"], 1)
            pe.wait_ge(S["cs_dve"], 10)
            for gr in range(NG):
                for a in range(TT):
                    last = transpose(bank(4 + gr // 2, 2, T)[0:60, gr % 2, a * P:(a + 1) * P],
                                     cs[:, a, NR * gr:NR * gr + NR, :].rearrange("p h n -> p (h n)"))
            last.then_inc(S["pct_ps"], 1)
            pe.wait_ge(S["pct_sb"], 2)
            with pe.Fori(0, NG) as gi:
                pe.wait_ge(S["alo"], gi * 2 + 1)
                pe.wait_ge(S["fx_act"], gi * 2 + 2)
                pe.wait_ge(S["fx_dve"], gi * 3 + 3)

                def scores(r):
                    half = slice(64 * (r % 2), 64 * (r % 2) + 64)
                    if r >= 2:
                        pe.wait_ge(S["p_act"], gi * 4 + (r - 1))
                    s1, s0 = bank(2 + 2 * (r % 2), 2, T), bank(3 + 2 * (r % 2), 2, P)
                    for b in range(2):
                        mm(s0[:, b, :], qf[half, r // 2, 0:P], kf[half, b, 0:P], start=b == 0, stop=False,
                           skip_group_check=True)
                    mm(s0, identb[:, :], over(causb[:, :], 1, 2), start=False, stop=True, skip_group_check=True)
                    for b in range(2):
                        mm(s1[:, b, :], qf[half, r // 2, P:T], kf[half, b, :], start=b == 0, stop=False,
                           skip_group_check=True)
                    mm(s1[:, :, P:T], identb[:, :], over(causb[:, :], 1, 2), start=False, stop=True,
                       skip_group_check=True).then_inc(S["sc_ps"], 1)

                def values(r):
                    pe.wait_ge(S["pw_dve"], gi * 4 + (r + 1))
                    if r:
                        pe.wait_ge(S["pts_act"], gi * 4 + r)
                        pe.wait_ge(S["pts_dve"], gi * 4 + r)
                    for b in range(2):
                        transpose(bank(6 + b, 3, P)[:, 0, :], pr0[:, r % 2, b, :])
                        for s in range(2):
                            last = transpose(bank(6 + b, 3, P)[:, 1 + s, :], pr1[:, r % 2, b, s * P:(s + 1) * P])
                    last.then_inc(S["ptr_ps"], 1)

                def output(r):
                    pe.wait_ge(S["pts_act"], gi * 4 + (r + 1))
                    pe.wait_ge(S["pts_dve"], gi * 4 + (r + 1))
                    o = ps[64 * (r % 2):64 * (r % 2) + 64, r // 2, 0:T]
                    for b in range(2):
                        mm(o, vff[:, b, 0, :], pts[:, b, 0:2, :].rearrange("p s q -> p (s q)"), start=b == 0, stop=False,
                           skip_group_check=True)
                        mm(o[:, P:T], vff[:, b, 1, :], pts[:, b, 2, :], start=False, stop=False, skip_group_check=True)
                    last = mm(o, vz[0:60, r, :], pcf[0:60, :], start=False, stop=True, skip_group_check=True)
                    last.then_inc(S["av_ps"], 1)
                scores(0)
                for r in range(1, NR):
                    scores(r)
                    values(r - 1)
                    output(r - 1)
                values(NR - 1)
                output(NR - 1)
            pe.wait_ge(S["alo"], 9)
            for i in range(2):
                stage_pair("wo", bighi, biglo8, i)
            stats(5)
            ffn_and_ple(1)
            pe.wait_ge(S["h_ready"], 28)
            for a in range(TT):
                for e in range(2):
                    for k in range(4):
                        last = transpose(bank(2 + 2 * a + e, 4, P)[:, k, :], h[:, 4 * e + k, a * P:(a + 1) * P])
                    last.then_inc(S["out_ps"], 1)

        @block.scalar
        def _(act):
            A = nc.scalar.activation

            n_tbl = [0]

            def table(func):
                A(tcol[:, n_tbl[0]:n_tbl[0] + 1], epsc[:, 0:1], func)
                n_tbl[0] += 1

            def split(stage, q, i=0):
                u = i * 2 + (U0[stage] + q)
                n = unit_k(stage, q) * UW
                act.wait_ge(landed[q % 2], i * 16 + (8 * U0[stage] + 16 * (q // 2 + 1)))
                if not isinstance(u, int) or u >= 2:
                    act.wait_ge(S["unit_done"], u - 1)
                A(whi[:, q % 2, 0:n], raw[:, q % 2, 0:n], ACT.Copy).then_inc(S["hi_done"], 1)

            act.wait_ge(S["cst_dve"], 1)
            act.dma_start(rows[0:16, :], mix_pre_norm.rearrange("a (k p) -> (a k) p", p=P)).then_inc(S["vec_in"], 16)
            act.dma_start(rows[16:32, :], mix_post_norm.rearrange("a (k p) -> (a k) p", p=P)).then_inc(S["vec_in"], 16)
            act.dma_start(rows[32:48, :], ffn_pre_norm.rearrange("a (k p) -> (a k) p", p=P)).then_inc(S["vec_in"], 16)
            act.dma_start(rows[48:64, :], ffn_post_norm.rearrange("a (k p) -> (a k) p", p=P)).then_inc(S["vec_in"], 16)
            act.dma_start(rows[64:72, :], kv_norm.rearrange("(k p) -> k p", p=P)).then_inc(S["vec_in"], 16)
            act.dma_start(rows[72:73, :], gdn_o_norm).then_inc(S["vec_in"], 16)
            act.dma_start(rows[96:128, :], cmp_pos.rearrange("v (c e) d -> (v c) (e d)", e=2)).then_inc(S["vec_in"], 16)
            act.dma_start(crows[:, :], gdn_conv_w[0].rearrange("j (t p) -> (j t) p", p=P)).then_inc(S["vec_in"], 16)

            def root(n, cols=False):
                r = rpost if n % 2 else rpre
                act.wait_ge(S["stat_ps"], n + 1)
                A(r[:, :], bank(2, T), ACT.Sqrt, bias=epsc[:, 0:1], scale=1.0 / DM).then_inc(S["root_done"], 1)
                if cols:
                    act.wait_ge(S["rc_ps"], n // 4 + 1)
                    A(rcol[:, :], bank(3, TT), ACT.Sqrt, bias=epsc[:, 0:1], scale=1.0 / DM).then_inc(S["rc_root"], 1)

            def squares_of_h(n, m, e):
                act.wait_ge(S["h_ready"], 4 * m + e + 1)
                A(sq[:, 2 * e:2 * e + 2, :], h[:, 2 * e:2 * e + 2, :], ACT.Square).then_inc(S["sq_ready"], 1)

            def xsplit(dst, cols, e):
                for k in (2 * e, 2 * e + 1):
                    A(dst(k), h[:, k, :], ACT.Copy, scale=gain(cols, k)).then_inc(S["xhi_done"], 1)

            def xh(k):
                return xhi[:, k, :]

            def bh(k):
                return big[:, k, :]

            def squares_of_y(b, e):
                act.wait_ge(S["bank_free"], b + 1)
                A(sq[:, 2 * e:2 * e + 2, :], y[:, 2 * e:2 * e + 2, :], ACT.Square).then_inc(S["sq_ready"], 1)

            split("qkv", 0)
            act.wait_ge(S["cst_dve"], N_DCST)
            for e in range(4):
                squares_of_h(0, 0, e)
            act.wait_ge(S["vec_sb"], 2)
            for e in range(4):
                xsplit(xh, MIXPRE[0], e)
            split("qkv", 1)
            root(0, cols=True)
            act.wait_ge(S["ba_dve"], 2)
            A(beta, balog[:, :, 0:HV], ACT.Sigmoid).then_inc(S["ba_act"], 1)
            act.wait_ge(S["ba_dve"], 5)
            A(sm[2], sm[2], ACT.Exp, scale=-1.0).then_inc(S["ba_act"], 1)
            A(alog[:, :], alog[:, :], ACT.Exp).then_inc(S["ba_act"], 1)

            def silu_qkv(i):
                for q in range(2):
                    act.wait_ge(S["conv_done"], i * 2 + (q + 1))
                    A(qkvT[:, bass.ds(i * 4 + 2 * q, 2), :], acc[:, q], ACT.Silu).then_inc(S["silu_done"], 1)
            table(ACT.Silu)
            act.wait_ge(S["rc_ps"], 1)
            with act.Fori(0, 4) as i:
                split("qkv", 0, i + 1)
                split("qkv", 1, i + 1)
                silu_qkv(i)
                for q in range(2):
                    act.wait_ge(S["silu_done"], i * 2 + (q + 1))
                    tiles = bass.ds(i * 4 + 2 * q, 2)
                    A(scr[:, tiles, :], qkvT[:, tiles, :], ACT.Square).then_inc(S["l2_sq"], 1)
            for i in (4, 5):
                split("qkv", 0, i + 1)
                split("qkv", 1, i + 1)
                silu_qkv(i)
            act.wait_ge(S["l2_ps"], 1)
            l2 = bank(2, TT, 16)
            A(hcol[:, :, 0:8], l2[:, :, 0:8], ACT.Sqrt, bias=epsc[:, 1:2], scale=float(HD)).then_inc(S["l2_root"], 1)
            A(hcol[:, :, 8:16], l2[:, :, 8:16], ACT.Sqrt, bias=epsc[:, 0:1]).then_inc(S["l2_root"], 1)
            split("qkv", 0, 7)
            split("qkv", 1, 7)
            silu_qkv(6)
            silu_qkv(7)

            act.wait_ge(S["cum_ps"], 1)
            A(einc, bank(7, 2, TT, HV)[:, 0], ACT.Exp).then_inc(S["cum_act"], 1)
            A(faft, bank(7, 2, TT, HV)[:, 1], ACT.Exp).then_inc(S["cum_act"], 1)
            A(epsc[:, 3:4], epsc[:, 0:1], ACT.Copy).then_inc(S["oT_sb"], 1)
            act.wait_ge(S["cum_act"], 2)
            act.wait_ge(S["silu_done"], 16)
            with act.Fori(0, 4) as j:
                act.wait_ge(S["l2_done"], j * 2 + 2)
                act.wait_ge(S["oT_sb"], j * 2 + 1)
                A(kqf[:, 0:2, :], qkvT[:, bass.ds(j * 2 + HK, 2), :], ACT.Copy).then_inc(S["kqf_sb"], 1)
                A(kqf[:, 2:4, :], qkvT[:, bass.ds(j * 2, 2), :], ACT.Copy).then_inc(S["kqf_sb"], 1)
                for c in range(2):
                    for part, dst in ((0, dQ), (1, dA)):
                        act.wait_ge(S["decay_ps"], j * 5 + (2 * c + part + 1))
                        A(dst[:, c], bank(2 + 2 * c + part, 4, P), ACT.Exp).then_inc(S["decay_sb"], 1)
                act.wait_ge(S["decay_ps"], j * 5 + 5)
                A(eq, bank(6, 4, P), ACT.Exp).then_inc(S["decay_sb"], 1)
                A(vf, qkvT[:, bass.ds(j * 4 + 2 * HK, 4), :], ACT.Copy).then_inc(S["vf_sb"], 1)
                act.wait_ge(S["ktok_ps"], j + 1)
                A(ktok, bank(7, 2, 2, P), ACT.Copy).then_inc(S["ktok_sb"], 1)
                for c in range(2):
                    act.wait_ge(S["vtok_ps"], j * 2 + (c + 1))
                    for e in range(4):
                        last = A(bv[:, c, e, :], bank(2 + 2 * c, 4, P)[:, e, :], ACT.Copy,
                                 scale=beta[:, c, bass.ds(j * 4 + e, 1)])
                    last.then_inc(S["bv_sb"], 1)
                split("z", 0, j)
                split("z", 1, j)
                act.wait_ge(S["vn_sb"], j * 2 + 1)
                for e in range(4):
                    last = A(bv[:, 0, e, :], vn[:, 0, e, :], ACT.Copy, scale=faft[:, 0, bass.ds(j * 4 + e, 1)])
                last.then_inc(S["fv_sb"], 1)
                act.wait_ge(S["s_ps"], j + 1)
                A(Ss, bank(2, 4, P), ACT.Copy).then_inc(S["s_sb"], 1)
                for c in range(2):
                    act.wait_ge(S["o_ps"], j * 2 + (c + 1))
                    A(oT[:, bass.ds(j * 4, 4), c * P:(c + 1) * P], bank(3 + 2 * c, 4, P), ACT.Copy).then_inc(S["oT_sb"], 1)
            act.wait_ge(S["oT_sb"], 9)
            for s in range(8):
                A(osq[:, 2 * s:2 * s + 2, :], oT[:, 2 * s:2 * s + 2, :], ACT.Square).then_inc(S["on_sq"], 1)
            act.wait_ge(S["on_ps"], 1)
            A(hcol[:, :, :], bank(2, TT, 16), ACT.Sqrt, bias=epsc[:, 0:1], scale=1.0 / HD).then_inc(S["on_root"], 1)
            act.wait_ge(S["bank_free"], B0["gout"])
            for s in range(8):
                A(zT[:, 2 * s:2 * s + 2, :], zT[:, 2 * s:2 * s + 2, :], ACT.Silu).then_inc(S["sz_done"], 1)
            split("gout", 0)
            for s in range(8):
                if s == 4:
                    split("gout", 1)
                act.wait_ge(S["oz_done"], s + 1)
                A(big[:, 2 * s:2 * s + 2, :], oT[:, 2 * s:2 * s + 2, :], ACT.Copy).then_inc(S["ohi_done"], 1)

            def post_then_pre(n, m, cols):
                root(n)
                for e in range(4):
                    squares_of_h(n + 1, m, e)
                    xsplit(xh, cols, e)
                root(n + 1)

            for gr in range(4):
                for q in range(2):
                    split(*(("gout", q, gr + 1) if gr < 3 else ("fin0", q)))
                squares_of_y(B0["gout"] + gr, gr)
            post_then_pre(1, 1, FFNPRE[0])

            def ffn_and_ple(layer, after):
                fin_, fout_, ple_ = f"fin{layer}", f"fout{layer}", f"ple{layer}"

                def hidden(i):
                    act.wait_ge(S["bank_free"], i * 2 + (B0[fin_] + 1))
                    A(t1[:, 0], t0[:, 0], ACT.Silu).then_inc(S["sg_done"], 1)
                    act.wait_ge(S["hid_done"], i + (11 * layer + 1))
                    A(big[:, bass.ds(i * 2, 2), :], t2[:, 1], ACT.Copy).then_inc(S["fhi_done"], 1)
                table(ACT.Silu)
                with act.Fori(0, PAIRS[fin_] - 1) as i:
                    split(fin_, 0, i + 1)
                    split(fin_, 1, i + 1)
                    hidden(i)
                split(fout_, 0)
                split(fout_, 1)
                hidden(PAIRS[fin_] - 1)
                split(fout_, 2)
                split(fout_, 3)
                for gr in range(4):
                    for q in range(2):
                        if gr < 3:
                            split(fout_, q, 2 * gr + 2)
                        else:
                            split(ple_, q)
                    squares_of_y(B0[fout_] + gr, gr)
                    if gr < 3:
                        for q in (2, 3):
                            split(fout_, q, 2 * gr + 2)
                act.wait_ge(S["pt_ps"], layer + 1)
                A(big[:, 0:2, :], bank(3, 2, T), ACT.Copy).then_inc(S["phi_done"], 1)
                root(3 + 4 * layer)
                for e in range(4):
                    act.wait_ge(S["h_ready"], 4 * (2 + 3 * layer) + e + 1)
                    A(xhi[:, 2 * e:2 * e + 2, :], h[:, 2 * e:2 * e + 2, :], ACT.Copy).then_inc(S["xhi_done"], 2)

                def gate(i):
                    act.wait_ge(S["unit_done"], i * 2 + (U0[ple_] + 2))
                    A(t1[:, 0], bank(1, 2, T), ACT.Sigmoid).then_inc(S["sgm_done"], 1)
                table(ACT.Sigmoid)
                with act.Fori(0, PAIRS[ple_] - 1) as i:
                    split(ple_, 0, i + 1)
                    split(ple_, 1, i + 1)
                    gate(i)
                if after:
                    split(after, 0)
                    split(after, 1)
                gate(PAIRS[ple_] - 1)
            ffn_and_ple(0, "kv")

            for e in range(4):
                squares_of_h(4, 3, e)
                xsplit(xh, KVN, e)
            root(4, cols=True)
            for e in range(4):
                xsplit(bh, MIXPRE[1], e)
            split("kv", 0, 1)
            split("kv", 1, 1)
            act.wait_ge(S["vec_sb"], 2)
            act.wait_ge(S["bank_free"], B0["kv"] + 1)
            block_copies(A, 0, S["ablk_act"])
            split("kv", 0, 2)
            split("kv", 1, 2)
            split("q", 0)
            split("q", 1)
            act.wait_ge(S["hb_sb"], 2)
            for v in range(2):
                for e in range(2):
                    A(hid[:, v, e, :], bank(4 + v, 2, 61)[:, e, 0:60], ACT.Silu, bias=cb[:, v, e:e + 1]).then_inc(S["hid_sb"], 1)
            act.wait_ge(S["gt_dve"], 2)
            A(gates[:, :, :], gates[:, :, :], ACT.Sigmoid).then_inc(S["gt_done"], 1)
            split("q", 0, 1)
            split("q", 1, 1)
            split("wo", 0)
            split("wo", 1)
            act.wait_ge(S["cs_dve"], 5)
            A(cs, cs, ACT.Exp, scale=ND ** -0.5).then_inc(S["cs_act"], 1)
            act.wait_ge(S["pct_ps"], 1)
            for e in range(2):
                A(pct[0:60, 2 * e:2 * e + 2, :], ps[0:60, 4 + e, 0:512].rearrange("p (a b) -> p a b", a=2), ACT.Copy).then_inc(S["pct_sb"], 1)
            with act.Fori(0, NG) as gi:
                act.wait_ge(S["alo"], gi * 2 + 1)
                A(qf, qT[:, bass.ds(gi * 2, 2), :], ACT.Copy).then_inc(S["fx_act"], 1)
                A(kf, kdup[:, :, bass.ds(gi, 1), :].rearrange("p b g s -> p (b g) s"), ACT.Copy).then_inc(S["fx_act"], 1)

                def transposed(r):
                    act.wait_ge(S["ptr_ps"], gi * 4 + (r + 1))
                    if r:
                        act.wait_ge(S["av_ps"], gi * 4 + r)
                    A(pts[:, 0], bank(6, 3, P), ACT.Copy).then_inc(S["pts_act"], 1)
                    if r % 2:
                        act.wait_ge(S["av_ps"], gi * 4 + (r + 1))
                        A(big[:, bass.ds(gi * 2 + r // 2, 1), :], bank(r // 2, 1, T), ACT.Copy).then_inc(S["ahi"], 1)
                for r in range(NR):
                    act.wait_ge(S["mx_dve"], gi * 12 + (3 * r + 3))
                    s1, s0 = bank(2 + 2 * (r % 2), 2, T), bank(3 + 2 * (r % 2), 2, P)
                    if r >= 2:
                        act.wait_ge(S["ptr_ps"], gi * 4 + (r - 1))
                    for b in range(2):
                        A(pr0[:, r % 2, b, :], s0[:, b, :], ACT.Exp, scale=ND ** -0.5, bias=hst[:, r % 2, 1, b:b + 1],
                          accum_out=hst[:, r % 2, 2, b:b + 1])
                        last = A(pr1[:, r % 2, b, :], s1[:, b, :], ACT.Exp, scale=ND ** -0.5,
                                 bias=hst[:, r % 2, 1, 2 + b:3 + b], accum_out=hst[:, r % 2, 2, 2 + b:3 + b])
                    last.then_inc(S["p_act"], 1)
                    if r:
                        transposed(r - 1)
                transposed(NR - 1)
            for i in range(2):
                for q in range(2):
                    if i == 0:
                        split("wo", q, 1)
                    else:
                        split("fin1", q)
                for q in range(2):
                    squares_of_y(B0["wo"] + 2 * i + q, 2 * i + q)
            post_then_pre(5, 4, FFNPRE[1])
            ffn_and_ple(1, None)
            for a in range(TT):
                act.wait_ge(S["out_ps"], 2 * a + 2)
                A(otok[:, a, 512:DM], bank(3 + 2 * a, 512), ACT.Copy).then_inc(S["out_act"], 1)

        @block.vector
        def _(dve):
            V = nc.vector
            stt = V.scalar_tensor_tensor

            def split(stage, q, i=0):
                u = i * 2 + (U0[stage] + q)
                n = unit_k(stage, q) * UW
                dve.wait_ge(S["hi_done"], u + 1)
                V.tensor_tensor(wlo[:, q % 2, 0:n], raw[:, q % 2, 0:n], whi[:, q % 2, 0:n],
                                ALU.subtract).then_inc(S["lo_done"], 1)

            for t, v in ((rows, 0.0), (ident, 0.0), (ones, 1.0), (causb, 0.0), (cmask, 0.0), (m1t, 1.0),
                         (rmask, 1.0)):
                V.memset(t[tuple([slice(None)] * len(t.shape))], v).then_inc(S["cst_dve"], 1)
            for v in range(LV):
                m = masks[:, v, :].rearrange("p (m e b) -> p m e b", e=2, b=1 << v)
                for e in range(2):
                    V.memset(m[:, :, e, :], float(e)).then_inc(S["cst_dve"], 1)
            V.memset(epsc[:, 0:1], EPS).then_inc(S["cst_dve"], 1)
            V.memset(epsc[:, 1:2], EPS * HD).then_inc(S["cst_dve"], 1)

            def rstd(n, cols=False):
                r = rpost if n % 2 else rpre
                dve.wait_ge(S["root_done"], n + 1)
                V.reciprocal(r[:, :], r[:, :]).then_inc(S["rstd_done"], 1)
                if cols:
                    dve.wait_ge(S["rc_root"], n // 4 + 1)
                    V.reciprocal(rcol[:, :], rcol[:, :]).then_inc(S["rcol_done"], 1)

            XN = [0]

            def xsplit(hi, lo, cols):
                for k in range(KD):
                    dve.wait_ge(S["xhi_done"], XN[0] + k + 1)
                    if cols is None:
                        V.tensor_tensor(lo(k), h[:, k, :], hi(k), ALU.subtract).then_inc(S["xlo_done"], 1)
                    else:
                        stt(out=lo(k), in0=h[:, k, :], scalar=gain(cols, k), in1=hi(k), op0=ALU.mult,
                            op1=ALU.subtract).then_inc(S["xlo_done"], 1)
                XN[0] += KD

            def xh(k):
                return xhi[:, k, :]

            def xl(k):
                return xlo[:, k, :]

            def times_rstd(dst, q, done_at):
                dve.wait_ge(S["unit_done"], done_at)
                return V.tensor_tensor(dst, bank(q, 2, T), over(rpre[:, :], 1, 2), ALU.mult).then_inc(S["bank_free"], 1)

            for e in range(4):
                dve.wait_ge(S["xt_ps"], e + 1)
                V.tensor_copy(h[:, 2 * e:2 * e + 2, :], bank(4 + e, 2, T)).then_inc(S["h_ready"], 1)
            dve.wait_ge(S["vec_ps"], 1)
            V.tensor_copy(vecs[:, :], bank(3, 4, P)[:, 0, :]).then_inc(S["vec_sb"], 1)
            V.tensor_copy(cw[:, :, :], bank(3, 4, P)[:, 1, :].rearrange("p (j t) -> p j t", j=4)).then_inc(S["vec_sb"], 1)
            dve.wait_ge(S["vec_sb"], 2)
            dve.wait_ge(S["h_ready"], 4)
            split("qkv", 0)
            xsplit(xh, xl, MIXPRE[0])
            split("qkv", 1)
            V.memset(pre[:, :, :, 0:3], 0.0).then_inc(S["conv_dve"], 1)
            rstd(0, cols=True)
            n_ba = [0]

            def ba(ins):
                ins.then_inc(S["ba_dve"], 1)
                n_ba[0] += 1
                dve.wait_ge(S["ba_dve"], n_ba[0])
            dve.wait_ge(S["rcol_done"], 1)
            dve.wait_ge(S["ba_ps"], 1)
            for a in range(TT):
                ba(V.tensor_scalar(balog[:, a, :], bank(4, TT, 2 * HV)[:, a, :], rcol[:, a:a + 1], None, ALU.mult))
            dve.wait_ge(S["small_in"], 16 * 9)
            ba(V.tensor_tensor(sm[0], balog[:, :, HV:2 * HV], over(dtb[:, :], 1, TT), ALU.add))
            ba(V.tensor_scalar(sm[1], sm[0], 0.0, None, ALU.max))
            ba(stt(out=sm[2], in0=sm[0], scalar=-1.0, in1=sm[0], op0=ALU.mult, op1=ALU.max))
            dve.wait_ge(S["ba_act"], 3)
            ba(V.tensor_scalar(sm[3], sm[2], 2.0, None, ALU.add))
            ba(V.reciprocal(sm[3], sm[3]))
            ba(V.tensor_tensor(sm[3], sm[2], sm[3], ALU.mult))
            ba(V.tensor_tensor(sm[4], sm[3], sm[3], ALU.mult))
            ba(V.tensor_scalar(sm[5], sm[4], 1.0 / 13, None, ALU.mult))
            for c in (11, 9, 7, 5, 3):
                ba(stt(out=sm[5], in0=sm[5], scalar=1.0 / c, in1=sm[4], op0=ALU.add, op1=ALU.mult))
            ba(stt(out=sm[5], in0=sm[5], scalar=1.0, in1=sm[3], op0=ALU.add, op1=ALU.mult))
            ba(stt(out=sm[1], in0=sm[5], scalar=2.0, in1=sm[1], op0=ALU.mult, op1=ALU.add))
            ba(stt(out=gdec, in0=sm[1], scalar=-1.0, in1=over(alog[:, :], 1, TT), op0=ALU.mult, op1=ALU.mult))
            assert n_ba[0] == N_BA

            dve.wait_ge(S["rstd_done"], 1)

            def conv_in(i, q):
                dve.wait_ge(S["unit_done"], i * 2 + (q + 1))
                V.tensor_tensor(pre[:, q, :, 3:T + 3], bank(q, 2, T), over(rpre[:, :], 1, 2),
                                ALU.mult).then_inc(S["bank_free"], 1)

            def conv(i, q, n0):
                dve.wait_ge(S["bank_free"], i * 2 + (q + 1))
                for j in range(4):
                    for e in range(2):
                        if j:
                            dve.wait_ge(S["conv_dve"], n0 + 2 * (j - 1) + e + 1)
                        w = cw[:, j, bass.ds(i * 4 + 2 * q + e, 1)]
                        src = pre[:, q, e, j:j + T]
                        if j == 0:
                            ins = V.tensor_scalar(acc[:, q, e, :], src, w, None, ALU.mult)
                        else:
                            ins = stt(out=acc[:, q, e, :], in0=src, scalar=w, in1=acc[:, q, e, :], op0=ALU.mult, op1=ALU.add)
                        ins.then_inc(S["conv_done"] if (j, e) == (3, 1) else S["conv_dve"], 1)

            def conv_pair(i, splits):
                for q in range(2):
                    splits(q)
                    conv_in(i, q)
                    conv(i, q, i * 14 + (7 * q + 1))
            conv_pair(0, lambda q: split("qkv", q, 1))
            with dve.Fori(1, PAIRS["qkv"] - 1) as i:
                dve.wait_ge(S["silu_done"], i * 2)
                conv_pair(i, lambda q: split("qkv", q, i + 1))
            dve.wait_ge(S["l2_root"], 2)
            V.reciprocal(hcol[:, :, :], hcol[:, :, :]).then_inc(S["hrec"], 1)
            dve.wait_ge(S["silu_done"], 14)
            conv_pair(PAIRS["qkv"] - 1, lambda q: None)

            for n, s in enumerate(QK_ORDER):
                dve.wait_ge(S["l2_rows"], n + 1)
                V.tensor_tensor(qkvT[:, 2 * s:2 * s + 2, :], qkvT[:, 2 * s:2 * s + 2, :], bank((3, 4, 5, 6)[n % 4], 2, T),
                                ALU.mult).then_inc(S["l2_done"], 1)
            dve.wait_ge(S["cum_act"], 2)
            stt(out=nbe, in0=beta, scalar=-1.0, in1=einc, op0=ALU.mult, op1=ALU.mult).then_inc(S["cum_dve"], 1)
            dve.wait_ge(S["cum_dve"], 1)
            dve.wait_ge(S["cst_pool"], N_CST)

            def odd(ap, b):
                return ap.rearrange("p h (m e b) -> p h m e b", e=2, b=b)[:, :, :, 1, :]

            def even(ap, b):
                return ap.rearrange("p h (m e b) -> p h m e b", e=2, b=b)[:, :, :, 0, :]

            with dve.Fori(0, 4) as j:
                dve.wait_ge(S["oT_sb"], j * 2 + 1)
                for c in range(2):
                    dve.wait_ge(S["kq_ps"], j * 2 + (c + 1))
                    dve.wait_ge(S["decay_sb"], j * 5 + (2 * c + 2))
                    for e in range(4):
                        last = stt(out=dA[:, c, e, :], in0=bank(c, 4, P)[:, e // 2, :],
                                   scalar=beta[:, c, bass.ds(j * 4 + e, 1)], in1=dA[:, c, e, :], op0=ALU.mult, op1=ALU.mult)
                    last.then_inc(S["a_sb"], 1)
                    d = dQ[:, c].rearrange("p (k r) s -> p k r s", r=2)
                    V.tensor_tensor(d, over(bank(c, 4, P)[:, 2:4, :], 2, 2), d, ALU.mult).then_inc(S["qk_raw"], 1)
                dve.wait_ge(S["decay_sb"], j * 5 + 5)
                e4 = eq.rearrange("p (k r) s -> p k r s", r=2)
                V.tensor_tensor(e4, over(kqf[:, 2:4, P:T], 2, 2), e4, ALU.mult).then_inc(S["qdec_sb"], 1)

                def y_out(v, c):
                    dve.wait_ge(S["y_ps"], j * 14 + (2 * v + c + 1))
                    V.tensor_tensor(yb[:, c], bank(3 + 2 * c, 4, P), over(masks[:, v, :], 1, 4),
                                    ALU.mult).then_inc(S["y_sb"], 1)

                def z_split(q, part):
                    if part == 0:
                        dve.wait_ge(S["hi_done"], j * 2 + (U0["z"] + q + 1))
                    c4 = slice(512 * part, 512 * part + 512)
                    last = V.tensor_tensor(wlo[:, q, c4], raw[:, q, c4], whi[:, q, c4], ALU.subtract)
                    if part == 3:
                        last.then_inc(S["lo_done"], 1)

                def z_out(q):
                    dve.wait_ge(S["unit_done"], j * 2 + (U0["z"] + q + 1))
                    V.tensor_tensor(zT[:, bass.ds(j * 4 + 2 * q, 2), :], bank(6 + q, 2, T), over(rpre[:, :], 1, 2),
                                    ALU.mult).then_inc(S["bank_free"], 1)

                def update(v, c):
                    b = 1 << v
                    if v == 0:
                        dve.wait_ge(S["y_sb"], j * 14 + (c + 1))
                        V.tensor_tensor(TTr[:, c], over(ident[:, :], 1, 4), yb[:, c],
                                        ALU.subtract).then_inc(S["t_upd"], 1)
                        return
                    dve.wait_ge(S["z_ps"], j * 12 + (2 * (v - 1) + c + 1))
                    if v < LV - 1:
                        V.tensor_tensor(even(Tr[:, c], b), even(Tr[:, c], b), even(bank(c, 4, P), b), ALU.subtract)
                    V.tensor_tensor(odd(TTr[:, c], b), odd(TTr[:, c], b), odd(bank(6 + c, 4, P), b), ALU.subtract).then_inc(S["t_upd"], 1)

                y_out(0, 0)
                y_out(0, 1)
                update(0, 0)
                update(0, 1)
                for v in range(1, LV):
                    y_out(v, 0)
                    z_split(*divmod(v - 1, 4))
                    if v > 1:
                        update(v - 1, 1)
                    update(v, 0)
                    y_out(v, 1)
                update(LV - 1, 1)
                dve.wait_ge(S["u_ps"], j * 2 + 1)
                V.tensor_copy(vn[:, 0], bank(0, 4, P)).then_inc(S["vn_sb"], 1)
                z_split(1, 2)
                z_split(1, 3)
                z_out(0)
                dve.wait_ge(S["ks_ps"], j + 1)
                dve.wait_ge(S["bv_sb"], j * 2 + 2)
                for e in range(4):
                    last = stt(out=bv[:, 1, e, :], in0=bank(4, 4, P)[:, e, :], scalar=nbe[:, 1, bass.ds(j * 4 + e, 1)],
                               in1=bv[:, 1, e, :], op0=ALU.mult, op1=ALU.add)
                last.then_inc(S["r1_sb"], 1)
                dve.wait_ge(S["u_ps"], j * 2 + 2)
                V.tensor_copy(vn[:, 1], bank(1, 4, P)).then_inc(S["vn_sb"], 1)
                z_out(1)
            dve.wait_ge(S["on_root"], 1)
            V.reciprocal(hcol[:, :, :], hcol[:, :, :]).then_inc(S["hrec"], 1)
            dve.wait_ge(S["oT_sb"], 9)

            def gated_lo(s):
                dve.wait_ge(S["ohi_done"], s + 1)
                V.tensor_tensor(big[:, KF + 2 * s:KF + 2 * s + 2, :], oT[:, 2 * s:2 * s + 2, :], big[:, 2 * s:2 * s + 2, :],
                                ALU.subtract).then_inc(S["olo_done"], 1)
            for s in range(8):
                o = oT[:, 2 * s:2 * s + 2, :]
                dve.wait_ge(S["on_rows"], s + 1)
                stt(out=o, in0=o, scalar=vecs[:, ONORM:ONORM + 1], in1=bank((3, 4, 5, 6)[s % 4], 2, T), op0=ALU.mult,
                    op1=ALU.mult).then_inc(S["on_done"], 1)
                dve.wait_ge(S["on_done"], s + 1)
                dve.wait_ge(S["sz_done"], s + 1)
                V.tensor_tensor(o, o, zT[:, 2 * s:2 * s + 2, :], ALU.mult).then_inc(S["oz_done"], 1)
                if s in (2, 4):
                    split("gout", s // 2 - 1)
                if s:
                    gated_lo(s - 1)
            gated_lo(7)

            def y_out_group(name, gr, per):
                dve.wait_ge(S["unit_done"], U0[name] + per * (gr + 1))
                V.tensor_copy(y[:, 2 * gr:2 * gr + 2, :], bank(gr % 2, 2, T)).then_inc(S["bank_free"], 1)

            YN = [0]

            def post_norm(n, cols, end):
                rstd(n)
                dve.wait_ge(S["rstd_done"], n + 1)
                dve.wait_ge(S["bank_free"], end)
                for e in range(4):
                    V.tensor_tensor(y[:, 2 * e:2 * e + 2, :], y[:, 2 * e:2 * e + 2, :], over(rpost[:, :], 1, 2),
                                    ALU.mult).then_inc(S["yn_done"], 1)
                for e in range(4):
                    dve.wait_ge(S["yn_done"], YN[0] + e + 1)
                    for k in (2 * e, 2 * e + 1):
                        last = stt(out=h[:, k, :], in0=y[:, k, :], scalar=gain(cols, k), in1=h[:, k, :], op0=ALU.mult,
                                   op1=ALU.add)
                    last.then_inc(S["h_ready"], 1)
                YN[0] += 4

            for gr in range(4):
                for q in range(2):
                    split(*(("gout", q, gr + 1) if gr < 3 else ("fin0", q)))
                y_out_group("gout", gr, 2)
            post_norm(1, MIXPOST[0], B0["fin0"])
            dve.wait_ge(S["h_ready"], 8)
            xsplit(xh, xl, FFNPRE[0])
            rstd(2)

            def ffn_and_ple(layer, after):
                fin_, fout_, ple_ = f"fin{layer}", f"fout{layer}", f"ple{layer}"
                dve.wait_ge(S["rstd_done"], 3 + 4 * layer)

                def hidden(i, splits):
                    splits(0)
                    times_rstd(t0[:, 0], 0, i * 2 + (U0[fin_] + 1))
                    splits(1)
                    times_rstd(t2[:, 0], 1, i * 2 + (U0[fin_] + 2))
                    dve.wait_ge(S["sg_done"], i + (11 * layer + 1))
                    dve.wait_ge(S["bank_free"], i * 2 + (B0[fin_] + 2))
                    V.tensor_tensor(t2[:, 1], t1[:, 0], t2[:, 0], ALU.mult).then_inc(S["hid_done"], 1)
                    dve.wait_ge(S["fhi_done"], i + (11 * layer + 1))
                    V.tensor_tensor(big[:, bass.ds(i * 2 + KF, 2), :], t2[:, 1], big[:, bass.ds(i * 2, 2), :],
                                    ALU.subtract).then_inc(S["flo_done"], 1)
                with dve.Fori(0, PAIRS[fin_] - 1) as i:
                    hidden(i, lambda q: split(fin_, q, i + 1))
                hidden(PAIRS[fin_] - 1, lambda q: split(fout_, q))
                split(fout_, 2)
                split(fout_, 3)
                for gr in range(4):
                    for q in range(2):
                        if gr < 3:
                            split(fout_, q, 2 * gr + 2)
                        else:
                            split(ple_, q)
                    y_out_group(fout_, gr, 4)
                    if gr < 3:
                        for q in (2, 3):
                            split(fout_, q, 2 * gr + 2)
                dve.wait_ge(S["phi_done"], layer + 1)
                V.tensor_tensor(big[:, 2:4, :], bank(3, 2, T), big[:, 0:2, :], ALU.subtract).then_inc(S["plo_done"], 1)
                post_norm(3 + 4 * layer, FFNPOST[layer], B0[ple_])
                dve.wait_ge(S["h_ready"], 4 * (3 + 3 * layer))
                xsplit(xh, xl, None)

                def embed(i, splits):
                    splits(0)
                    splits(1)
                    dve.wait_ge(S["sgm_done"], i + (4 * layer + 1))
                    dve.wait_ge(S["h_ready"], i + 4 * (3 + 3 * layer))
                    V.tensor_tensor(t0[:, 0], bank(0, 2, T), t1[:, 0], ALU.mult).then_inc(S["bank_free"], 2)
                    dve.wait_ge(S["bank_free"], i * 2 + (B0[ple_] + 2))
                    hh = h[:, bass.ds(i * 2, 2), :]
                    V.tensor_tensor(hh, hh, t0[:, 0], ALU.add).then_inc(S["h_ready"], 1)
                with dve.Fori(0, PAIRS[ple_] - 1) as i:
                    embed(i, lambda q: split(ple_, q, i + 1))
                embed(PAIRS[ple_] - 1, (lambda q: split(after, q)) if after else (lambda q: None))
            ffn_and_ple(0, "kv")

            dve.wait_ge(S["h_ready"], 16)
            xsplit(xh, xl, KVN)
            rstd(4, cols=True)
            xsplit(lambda k: big[:, k, :], lambda k: big[:, KD + k, :], MIXPRE[1])
            dve.wait_ge(S["rstd_done"], 5)
            dve.wait_ge(S["rcol_done"], 2)
            for q in range(2):
                split("kv", q, 1)
                times_rstd(ckv[:, q], q, U0["kv"] + q + 1)
            dve.wait_ge(S["bank_free"], B0["kv"] + 2)
            block_copies(V.tensor_copy, 1, S["ablk_dve"])
            for b in range(2):
                split(*(("kv", 0, 2) if b == 0 else ("q", 0)))
                dve.wait_ge(S["unit_done"], U0["kv"] + 2 * b + 3)
                for e in range(2):
                    src = slice(64 * e, 64 * e + 64)
                    for d in range(2):
                        dst = kdup[64 * d:64 * d + 64, b].rearrange("p (t h) s -> p t h s", h=2)[:, :, e, :]
                        last = V.tensor_tensor(dst, bank(0, 2, T)[src], over(rpre[src, :], 1, 2), ALU.mult)
                last.then_inc(S["bank_free"], 1)
                split(*(("kv", 1, 2) if b == 0 else ("q", 1)))
                dve.wait_ge(S["unit_done"], U0["kv"] + 2 * b + 4)
                for a in range(TT):
                    last = V.tensor_scalar(vtk[:, b, a, :], bank(1, TT, T)[:, a, :], rcol[:, a:a + 1], None, ALU.mult)
                last.then_inc(S["bank_free"], 1)
            dve.wait_ge(S["hid_ps"], 1)
            for v in range(2):
                V.tensor_copy(cb[:, v], bank(4 + v, 2, 61)[:, :, 60]).then_inc(S["hb_sb"], 1)
            dve.wait_ge(S["gt_ps"], 1)
            for a in range(TT):
                V.tensor_scalar(gates[:, a, :], bank(7, TT, 3 * NH)[:, a, :], rcol[:, a:a + 1], None,
                                ALU.mult).then_inc(S["gt_dve"], 1)
            dve.wait_ge(S["hid_sb"], 4)
            for e in range(2):
                V.tensor_copy(hrep[:, :, e, :].rearrange("p g (r n) -> p g r n", r=NR),
                              over(hid[:, 1, e, :].rearrange("p (g n) -> p g n", g=NG), 2, NR)).then_inc(S["hrep_sb"], 1)
            for i in range(2):
                for q in range(2):
                    split(*(("q", q, 1) if i == 0 else ("wo", q)))
                    times_rstd(qT[:, 4 * i + 2 * q:4 * i + 2 * q + 2, :], q, U0["q"] + 2 * i + q + 1)
            dve.wait_ge(S["kc_ps"], 2)
            V.tensor_copy(kcd, bank(6, 60)).then_inc(S["kc_sb"], 1)
            V.tensor_copy(vrep[0:60], ps[0:60, 7, 0:256].rearrange("p (g d) -> p g d", g=NG)).then_inc(S["kc_sb"], 1)
            n_cs = [0]

            def csw(ins):
                ins.then_inc(S["cs_dve"], 1)
                n_cs[0] += 1
                dve.wait_ge(S["cs_dve"], n_cs[0])
            dve.wait_ge(S["cs_ps"], 1)
            for e in range(2):
                csw(V.tensor_tensor(cs.rearrange("p a (h e) n -> p a h e n", e=2)[:, :, :, e, :],
                                    bank(3 - e, TT, NH // 2, NC), over(cmask[:, :, :], 2, NH // 2), ALU.add))
            csf = cs.rearrange("p a h n -> p (a h) n")
            csw(V.tensor_reduce(out=cst[:, 0, :], in_=csf, axis=AX, op=ALU.max))
            csw(V.tensor_scalar(cst[:, 0, :], cst[:, 0, :], -1e25, None, ALU.max))
            csw(V.tensor_tensor(csf, csf, over(cst[:, 0, :], 2, NC), ALU.subtract))
            dve.wait_ge(S["cs_act"], 1)
            csw(V.tensor_reduce(out=cst[:, 1, :], in_=csf, axis=AX, op=ALU.add))
            csw(V.tensor_scalar(cst[:, 1, :], cst[:, 1, :], 1e-30, None, ALU.max))
            csw(V.reciprocal(cst[:, 1, :], cst[:, 1, :]))
            dve.wait_ge(S["gt_done"], 1)
            g4 = gates[:, :, :].rearrange("p a (h b) -> p a h b", b=3)
            csw(V.tensor_tensor(cst[:, 2, :].rearrange("p (a h) -> p a h", a=TT),
                                cst[:, 1, :].rearrange("p (a h) -> p a h", a=TT), g4[:, :, :, 0], ALU.mult))
            csw(V.tensor_tensor(csf, csf, over(cst[:, 2, :], 2, NC), ALU.mult))
            V.memset(epsc[:, 2:3], 0.0).then_inc(S["alo"], 1)
            dve.wait_ge(S["pct_sb"], 2)
            dve.wait_ge(S["kc_sb"], 2)
            with dve.Fori(0, NG) as gi:
                dve.wait_ge(S["alo"], gi * 2 + 1)
                V.tensor_copy(vff.rearrange("p b a d -> p (b a) d"),
                              vtk.rearrange("p b a (g d) -> p (b a) g d", g=NG)[:, :, bass.ds(gi, 1), :].rearrange("p b g d -> p b (g d)")).then_inc(S["fx_dve"], 1)
                V.tensor_copy(pcf[0:60, :], pct[0:60, bass.ds(gi, 1), :].rearrange("p g q -> p (g q)")).then_inc(S["fx_dve"], 1)
                V.tensor_tensor(vz[0:60], over(vrep[0:60, bass.ds(gi, 1), :].rearrange("p g d -> p (g d)"), 1, NR),
                                over(rmask[0:60, :], 2, ND), ALU.mult).then_inc(S["fx_dve"], 1)

                def maxima(r):
                    dve.wait_ge(S["sc_ps"], gi * 4 + (r + 1))
                    s1, s0 = bank(2 + 2 * (r % 2), 2, T), bank(3 + 2 * (r % 2), 2, P)
                    V.tensor_reduce(out=hst[:, r % 2, 0, 0:2], in_=s0, axis=AX, op=ALU.max).then_inc(S["mx_dve"], 1)
                    V.tensor_reduce(out=hst[:, r % 2, 0, 2:4], in_=s1, axis=AX, op=ALU.max).then_inc(S["mx_dve"], 1)
                    dve.wait_ge(S["mx_dve"], gi * 12 + (3 * r + 2))
                    V.tensor_scalar(hst[:, r % 2, 1, :], hst[:, r % 2, 0, :], -(ND ** -0.5), None, ALU.mult).then_inc(S["mx_dve"], 1)

                def weights(r):
                    dve.wait_ge(S["p_act"], gi * 4 + (r + 1))
                    l = hst[:, r % 2, 2, :]
                    V.tensor_scalar(l, l, 1e-30, None, ALU.max).then_inc(S["rl_dve"], 1)
                    dve.wait_ge(S["rl_dve"], gi * 12 + (3 * r + 1))
                    V.reciprocal(l, l).then_inc(S["rl_dve"], 1)
                    dve.wait_ge(S["rl_dve"], gi * 12 + (3 * r + 2))
                    l2 = l.rearrange("p (a b) -> p a b", a=TT)
                    V.tensor_tensor(l2, l2, gates[:, :, bass.ds(gi * 12 + (3 * r + 1), 2)], ALU.mult).then_inc(S["rl_dve"], 1)
                    dve.wait_ge(S["rl_dve"], gi * 12 + (3 * r + 3))
                    for b in range(2):
                        V.tensor_scalar(pr0[:, r % 2, b, :], pr0[:, r % 2, b, :], l[:, b:b + 1], None, ALU.mult)
                        last = V.tensor_scalar(pr1[:, r % 2, b, :], pr1[:, r % 2, b, :], l[:, 2 + b:3 + b], None, ALU.mult)
                    last.then_inc(S["pw_dve"], 1)

                def transposed(r):
                    dve.wait_ge(S["ptr_ps"], gi * 4 + (r + 1))
                    if r:
                        dve.wait_ge(S["av_ps"], gi * 4 + r)
                    V.tensor_copy(pts[:, 1], bank(7, 3, P)).then_inc(S["pts_dve"], 1)
                    if r % 2:
                        dve.wait_ge(S["ahi"], gi * 2 + (r // 2 + 1))
                        V.tensor_tensor(big[:, bass.ds(gi * 2 + (KD + r // 2), 1), :], bank(r // 2, 1, T),
                                        big[:, bass.ds(gi * 2 + r // 2, 1), :], ALU.subtract).then_inc(S["alo"], 1)
                maxima(0)
                for r in range(NR):
                    weights(r)
                    if r + 1 < NR:
                        maxima(r + 1)
                    transposed(r)
            for i in range(2):
                for q in range(2):
                    split(*(("wo", q, 1) if i == 0 else ("fin1", q)))
                for q in range(2):
                    gr = 2 * i + q
                    dve.wait_ge(S["unit_done"], U0["wo"] + gr + 1)
                    V.tensor_copy(y[:, 2 * gr:2 * gr + 2, :], bank(q, 2, T)).then_inc(S["bank_free"], 1)
            post_norm(5, MIXPOST[1], B0["fin1"])
            dve.wait_ge(S["h_ready"], 20)
            xsplit(xh, xl, FFNPRE[1])
            rstd(6)
            ffn_and_ple(1, None)
            for a in range(TT):
                dve.wait_ge(S["out_ps"], 2 * a + 1)
                V.tensor_copy(otok[:, a, 0:512], bank(2 + 2 * a, 512)).then_inc(S["out_sb"], 1)
    return nc


_INS = ["x", "p", "mix_pre_norm", "mix_post_norm", "ffn_pre_norm", "ffn_post_norm", "gdn_w_in", "gdn_conv_w",
        "gdn_a_log", "gdn_dt_bias", "gdn_o_norm", "gdn_w_out", "kv_norm", "kv_w", "cmp_pos", "cmp_w1", "cmp_w2",
        "nsa_w_qg", "nsa_w_o", "ffn_w_in", "ffn_w_out", "ple_w_in", "ple_w_gate"]


def kernel(**inputs):
    import numpy as np
    import concourse.bacc as bacc
    from concourse.bass_utils import run_bass_kernel_spmd

    nc = bacc.Bacc("TRN2", target_bir_lowering=False, num_devices=1)
    arrays, args = {}, []
    for name in _INS:
        a = np.ascontiguousarray(inputs[name])
        arrays[f"in_{name}"] = a
        args.append(nc.dram_tensor(f"in_{name}", a.shape, mybir.dt.from_np(a.dtype), kind="ExternalInput").ap())
    out = nc.dram_tensor("out_h", inputs["x"].shape, F32, kind="ExternalOutput").ap()
    build(nc, *args, out)
    r = run_bass_kernel_spmd(nc, [arrays], core_ids=[0])
    return r.results[0]["out_h"]
```

```python
from contextlib import ExitStack

import concourse.bass as bass
from concourse import mybir

P = 128
T = 256
TT = T // P
DM = 1024
KD = DM // P
HK, HV, HD = 8, 16, 128
CONVW = (2 * HK + HV) * HD
FFN = 2816
KF = FFN // P
NH, NG, ND = 16, 4, 64
NR = NH // NG
NC = (T - 32) // 16 + 1
QK_ORDER = (4, 0, 5, 1, 6, 2, 7, 3)
UW = 256
EPS = 1e-6
NEG = -1e30
N_BA = 18
N_CST = 24
N_DCST = 23
LV = 7

F32 = mybir.dt.float32
F32R = mybir.dt.float32r
BF16 = mybir.dt.bfloat16
ACT = mybir.ActivationFunctionType
ALU = mybir.AluOpType
AX = mybir.AxisListType.X

STAGES = [("qkv", 8, 1), ("z", 4, 1), ("gout", 4, 2), ("fin0", 11, 1), ("fout0", 8, 4),
          ("pin0", 1, 0), ("gate0", 2, 1),
          ("kv", 3, 1), ("q", 2, 1), ("wo", 2, 1), ("fin1", 11, 1), ("fout1", 8, 4),
          ("pin1", 1, 0), ("gate1", 2, 1)]
ORDER = [s[0] for s in STAGES]
PAIRS = {s[0]: s[1] for s in STAGES}
U0, B0 = {}, {}
_u = _b = 0
for _n, _p, _s in STAGES:
    U0[_n], B0[_n] = _u, _b
    _u += 2 * _p
    _b += 2 * _p // _s if _s else 0
FOUT_K = (6, 5, 6, 5)


def unit_k(stage, p):
    if stage.startswith("fout"):
        return FOUT_K[p]
    if stage.startswith("pin"):
        return 4
    return 8


def build(nc, x, p, mix_pre_norm, mix_post_norm, ffn_pre_norm, ffn_post_norm, gdn_w_in, gdn_conv_w, gdn_a_log,
          gdn_dt_bias, gdn_o_norm, gdn_w_out, kv_norm, kv_w, cmp_pos, cmp_w1, cmp_w2, nsa_w_qg, nsa_w_o,
          ffn_w_in, ffn_w_out, ple_w_in, ple_w_gate, out):
    with ExitStack() as ctx:
        def sb(name, shape, dt=F32):
            return ctx.enter_context(nc.sbuf_tensor(name, shape, dt))

        def sem(name):
            return ctx.enter_context(nc.semaphore(name))

        raw = sb("w_raw", [P, 2, 8 * UW])
        whi = sb("w_hi", [P, 2, 8 * UW], F32R)
        wlo = sb("w_lo", [P, 2, 8 * UW], F32R)
        xhi = sb("x_hi", [P, KD, T], F32R)
        xlo = sb("x_lo", [P, KD, T], F32R)
        phl = sb("p_hi_lo", [P, 4, T], F32R)
        h = sb("h", [P, KD, T])
        scr = sb("scr", [P, 16, T])
        y, sq = scr[:, 0:KD, :], scr[:, KD:16, :]
        qkvT = sb("qkvT", [P, 32, T])
        rpre = sb("rstd_pre", [P, T])
        rpost = sb("rstd_post", [P, T])
        rcol = sb("rstd_col", [P, TT])
        epsc = sb("eps_cols", [P, 4])
        ident = sb("ident", [P, P])
        identb = sb("identb", [P, P], BF16)
        causb = sb("causb", [P, P], BF16)
        ones = sb("ones", [P, P])
        tri_le = sb("tri_le", [P, P])
        tri_gt = sb("tri_gt", [P, P])
        masks = sb("level_masks", [P, LV, P])
        m1t = sb("first_level_mask", [P, P])
        rows = sb("vector_rows", [P, P])
        crows = sb("conv_rows", [P, P])
        vecs = sb("vectors", [P, P])
        cw = sb("conv_cols", [P, 4, 32])
        wba = sb("w_beta_a", [P, KD, 2 * HV])
        wgt = sb("w_gates", [P, KD, 3 * NH])
        dtb = sb("dt_bias_b", [P, HV])
        alog = sb("a_log_b", [P, HV])
        w2k = sb("w2k", [P, 2, 2, ND])
        w2v = sb("w2v", [P, 2, ND])
        ptok = sb("p_tok", [P, 2, TT, 256])
        gates = sb("gates", [P, TT, 3 * NH])
        small = sb("small", [P, 12, TT, HV])
        beta, gdec, einc, faft, nbe = (small[:, i] for i in range(5))
        sm = [small[:, i] for i in range(5, 12)]
        balog = sb("beta_a_logits", [P, TT, 2 * HV])
        cmask = sb("cmp_mask", [P, TT, NC])
        rmask = sb("row_masks", [P, NR])
        hcol = sb("head_rstd_cols", [P, TT, 16])
        tcol = sb("table_cols", [P, 24])
        cst = sb("cmp_stats", [P, 3, TT * NH])
        hst = sb("head_stats", [P, 2, 3, 4])
        with nc.sbuf_tensor("big", [P, 2 * KF, T], F32R) as big:
            pass
        gdn = sb("gdn", [P, 12288])

        def views(base):
            used = [0]

            def take(*shape):
                n = 1
                for v in shape:
                    n *= v
                v = base[:, used[0]:used[0] + n]
                used[0] += n
                assert used[0] <= base.shape[1], used[0]
                names = "abcd"[:len(shape)]
                return v.rearrange(f"p ({' '.join(names)}) -> p {' '.join(names)}", **dict(zip(names, shape))) \
                    if len(shape) > 1 else v
            return take

        xtok = views(gdn)(TT, DM)
        ar = views(gdn)
        pre = ar(2, 2, T + 3)
        acc = ar(2, 2, T)
        ar = views(gdn)
        dA = ar(2, 4, P)
        dQ = ar(2, 4, P)
        eq = ar(4, P)
        gtri = ar(2, 4, P)
        TTr = ar(2, 4, P)
        Tr = ar(2, 4, P)
        ktok = ar(2, 2, P)
        bv = ar(2, 4, P)
        Ss = ar(4, P)
        vn = ar(2, 4, P)
        kqf = ar(4, T)
        vf = ar(4, T)
        yb = ar(2, 4, P)
        osq = views(gdn)(16, T)
        zT = scr
        oT = qkvT[:, 16:32, :]
        pw1 = gdn[:, 4096:12288].rearrange("p (v c n) -> p v c n", v=2, c=16)
        qkvf = qkvT[:, :, :].rearrange("p a b -> p (a b)")
        ar = views(qkvf)
        t0 = ar(2, 2, T)
        t1 = ar(2, 2, T)
        t2 = ar(2, 2, T)
        ar = views(qkvf)
        kdup = ar(2, NG, T)
        vtk = ar(2, TT, T)
        ckv = ar(2, 2, T)
        ablk = ar(2, 16, 61)
        hid = ar(2, 2, 60)
        kcd = ar(60)
        vrep = ar(NG, ND)
        cb = ar(2, 2)
        hrep = ar(NG, 2, 60)
        cs = ar(TT, NH, NC)
        qT = scr[:, 0:8, :]
        ar = views(scr[:, 8:16, :].rearrange("p a b -> p (a b)"))
        pr0 = ar(2, 2, P)
        pr1 = ar(2, 2, T)
        qf = ar(2, T)
        ar = views(gdn[:, 4096:12288])
        pct = ar(NG, T)
        kf = ar(2, T)
        vff = ar(2, TT, ND)
        pcf = ar(T)
        vz = ar(NR, ND)
        pts = ar(2, 2, 3, P)
        otok = scr[:, 0:8, :].rearrange("p (a b) t -> p a (b t)", a=TT)

        ps = ctx.enter_context(nc.psum_tensor("ps", [P, 8, 512], F32))

        def bank(b, *shape):
            n = 1
            for v in shape:
                n *= v
            v = ps[:, b, 0:n]
            names = "abcd"[:len(shape)]
            return v.rearrange(f"p ({' '.join(names)}) -> p {' '.join(names)}", **dict(zip(names, shape))) \
                if len(shape) > 1 else v

        def over(ap, axis, n):
            shape = list(ap.shape)
            shape.insert(axis, n)
            return ap.unsqueeze(axis).to_broadcast(shape)

        def gain(col, k):
            return vecs[:, col + k:col + k + 1]
        MIXPRE, MIXPOST, FFNPRE, FFNPOST, KVN, ONORM, POS = (0, 8), (16, 24), (32, 40), (48, 56), 64, 72, 96

        landed = [sem("landed0"), sem("landed1")]
        S = {}
        for name in ("hi_done lo_done unit_done bank_free x_in vec_in small_in cst_pool cst_dve xt_ps h_ready "
                     "sq_ready stat_ps root_done rstd_done xhi_done xlo_done vec_ps vec_sb rc_ps rc_root rcol_done ba_ps ba_dve ba_act "
                     "conv_dve conv_done silu_done l2_sq l2_ps l2_root l2_done gtri_done decay_ps decay_sb kq_ps a_sb qk_raw "
                     "kqf_sb vf_sb hrec l2_rows on_rows "
                     "qk_sb qdec_sb tinit y_ps y_sb z_ps t_upd ktok_ps ktok_sb vtok_ps bv_sb u_ps vn_sb fv_sb s_ps s_sb "
                     "ks_ps r1_sb o_ps oT_sb on_sq on_ps on_root on_done cum_ps cum_act cum_dve sz_done oz_done ohi_done olo_done "
                     "yn_done sg_done hid_done fhi_done flo_done pt_ps phi_done plo_done sgm_done pl_t "
                     "ablk_act ablk_dve hrep_sb pts_act pts_dve out_act w1_in hid_ps hb_sb hid_sb kc_ps kc_sb "
                     "gt_ps gt_dve gt_done cs_ps cs_dve cs_act pct_ps pct_sb fx_act fx_dve "
                     "sc_ps mx_dve p_act rl_dve pw_dve ptr_ps pts_sb av_ps ahi alo out_ps out_sb out_st").split():
            S[name] = sem(name)

        def block_copies(copy, v, done):
            for par in range(2):
                for e in range(2):
                    src = ckv[64 * e:64 * e + 64, v].rearrange("p t (n c r) -> p c t n r", c=8, r=2)[:, :, :, :, par]
                    dst = ablk[64 * par:64 * par + 64, v, :, 0:60].rearrange("p c (t e n) -> p c t e n", t=2, e=2)
                    for half in range(2):
                        for t in range(2):
                            last = copy(dst[:, 8 * half:8 * half + 8, t, e, :], src[:, :, t, half:half + NC], *cargs(v))
                        last.then_inc(done, 1)
            copy(ablk[:, v, :, 60], vecs[:, POS + 16 * v:POS + 16 * v + 16], *cargs(v)).then_inc(done, 1)

        def cargs(v):
            return (ACT.Copy,) if v == 0 else ()

        block = ctx.enter_context(nc.Block())

        win = gdn_w_in[0].rearrange("(k p) n -> p k n", p=P)
        wout = gdn_w_out[0].rearrange("(k p) n -> p k n", p=P)
        fin = [ffn_w_in[i].rearrange("(k p) n -> p k n", p=P) for i in range(2)]
        fout = [ffn_w_out[i].rearrange("(k p) n -> p k n", p=P) for i in range(2)]
        pin = [ple_w_in[i].rearrange("(k p) n -> p k n", p=P) for i in range(2)]
        pgt = [ple_w_gate[i].rearrange("(k p) n -> p k n", p=P) for i in range(2)]
        wkv = kv_w.rearrange("(k p) n -> p k n", p=P)
        wqg = nsa_w_qg[0].rearrange("(k p) n -> p k n", p=P)
        wwo = nsa_w_o[0].rearrange("(k p) n -> p k n", p=P)

        def source(stage, i, q):
            cols = bass.ds(i * (2 * UW) + q * UW, UW)
            one = bass.ds(i * UW, UW)
            if stage == "qkv":
                return win[:, :, cols]
            if stage == "z":
                return win[:, :, bass.ds(i * (2 * UW) + (CONVW + q * UW), UW)]
            if stage == "gout":
                return wout[:, 8 * q:8 * q + 8, one]
            if stage[:3] == "fin":
                w = fin[int(stage[3])]
                return w[:, :, one] if q == 0 else w[:, :, bass.ds(i * UW + FFN, UW)]
            if stage[:4] == "fout":
                k = sum(FOUT_K[:q])
                return fout[int(stage[4])][:, k:k + FOUT_K[q], one]
            if stage[:4] == "gate":
                return pgt[int(stage[4])][:, :, cols]
            return {"kv": wkv, "q": wqg, "wo": wwo}[stage][:, :, cols]


        @block.sync
        def _(sp):
            def load(stage, i, q):
                n = unit_k(stage, q) * UW
                if stage.startswith("pin"):
                    sp.dma_start(raw[:, q, 0:n], pin[int(stage[3])][:, q, :]).then_inc(landed[q], 16)
                    return
                sp.dma_start(raw[:, q % 2, 0:n].rearrange("p (k n) -> p k n", n=UW),
                             source(stage, i, q)).then_inc(landed[q % 2], 16)

            sp.dma_start(xtok, x[0].rearrange("(a p) d -> p a d", p=P)).then_inc(S["x_in"], 16)
            for stage in ORDER:
                per = 4 if stage.startswith("fout") else 2
                first = 0
                if stage == "qkv":
                    first = 1
                    for q in range(per):
                        load(stage, 0, q)
                with sp.Fori(first, PAIRS[stage] * 2 // per) as i:
                    for q in range(per):
                        sp.wait_ge(S["lo_done"], i * per + (U0[stage] + q - 1))
                        load(stage, i, q)
            for a in range(TT):
                sp.wait_ge(S["out_sb"], a + 1)
                sp.wait_ge(S["out_act"], a + 1)
                sp.dma_start(out[0, a * P:(a + 1) * P, :], otok[:, a, :]).then_inc(S["out_st"], 16)
            sp.wait_ge(S["out_st"], 16 * TT)

        @block.gpsimd
        def _(pool):
            g = nc.gpsimd
            pool.dma_start(wba[:, :, :], win[:, :, 6144:6176]).then_inc(S["small_in"], 16)
            pool.dma_start(dtb[:, :], gdn_dt_bias[0].partition_broadcast(P)).then_inc(S["small_in"], 16)
            pool.dma_start(alog[:, :], gdn_a_log[0].partition_broadcast(P)).then_inc(S["small_in"], 16)
            pool.dma_start(wgt[:, :, :], wqg[:, :, 1024:1072]).then_inc(S["small_in"], 16)
            for d in range(2):
                pool.dma_start(w2k[:, :, d, :], cmp_w2[0].rearrange("(c p) n -> p c n", p=P)).then_inc(S["small_in"], 16)
            pool.dma_start(w2v[:, :, :], cmp_w2[1].rearrange("(c p) n -> p c n", p=P)).then_inc(S["small_in"], 16)
            for i in range(2):
                pool.dma_start(ptok[:, i], p[i, 0].rearrange("(a p) d -> p a d", p=P)).then_inc(S["small_in"], 16)

            n = [0]

            def sel(dst, src, op, fill, base, pattern, cm):
                if n[0]:
                    pool.wait_ge(S["cst_pool"], n[0])
                g.affine_select(out=dst, in_=src, compare_op=op, fill=fill, base=base, pattern=pattern,
                                channel_multiplier=cm).then_inc(S["cst_pool"], 1)
                n[0] += 1
            pool.wait_ge(S["cst_dve"], N_DCST)
            sel(ident[:, :], ident[:, :], ALU.not_equal, 1.0, 0, [[-1, P]], 1)
            sel(tri_le[:, :], ones[:, :], ALU.is_ge, 0.0, 0, [[1, P]], -1)
            sel(tri_gt[:, :], ones[:, :], ALU.is_gt, 0.0, 0, [[-1, P]], 1)
            sel(identb[:, :], ident[:, :], ALU.is_ge, 0.0, 0, [[0, P]], 0)
            sel(causb[:, :], causb[:, :], ALU.is_ge, NEG, 0, [[-1, P]], 1)
            sel(cmask[:, :, :], cmask[:, :, :], ALU.is_ge, NEG, -31, [[P, TT], [-16, NC]], 1)
            for v in range(LV):
                b = 1 << v
                m = masks[:, v, :].rearrange("p (m e b) -> p m e b", e=2, b=b)[:, :, 1, :]
                sel(m, m, ALU.is_ge, 0.0, 0, [[-2 * b, 64 // b], [0, b]], 1)
                sel(m, m, ALU.is_ge, 0.0, b - 1, [[2 * b, 64 // b], [0, b]], -1)
            m1 = m1t[:, :].rearrange("p (m e) -> p m e", e=2)
            sel(m1, m1, ALU.is_equal, 0.0, -1, [[-2, 64], [0, 2]], 1)
            sel(m1, m1, ALU.is_equal, 0.0, 0, [[0, 64], [1, 2]], 0)
            sel(rmask[:, :], rmask[:, :], ALU.is_ge, 0.0, 0, [[-NC, NR]], 1)
            sel(rmask[:, :], rmask[:, :], ALU.is_ge, 0.0, NC - 1, [[NC, NR]], -1)
            assert n[0] == N_CST

            pool.wait_ge(S["ba_dve"], N_BA)
            pool.wait_ge(S["conv_done"], 16)
            with pool.Fori(0, 4) as j:
                pool.wait_ge(S["ktok_ps"], j + 1)
                for c in range(2):
                    g.tensor_tensor(gtri[:, c], over(gdec[:, c, bass.ds(j * 4, 4)], 2, P), over(tri_le[:, :], 1, 4),
                                    ALU.mult).then_inc(S["gtri_done"], 1)
                for c in range(2):
                    pool.wait_ge(S["a_sb"], j * 2 + (c + 1))
                    g.tensor_tensor(Tr[:, c], dA[:, c], over(m1t[:, :], 1, 4), ALU.mult).then_inc(S["tinit"], 1)
                    pool.wait_ge(S["tinit"], j * 4 + (2 * c + 1))
                    g.tensor_tensor(Tr[:, c], over(ident[:, :], 1, 4), Tr[:, c], ALU.subtract).then_inc(S["tinit"], 1)
                for c in range(2):
                    pool.wait_ge(S["qk_raw"], j * 2 + (c + 1))
                    g.tensor_tensor(dQ[:, c], dQ[:, c], over(tri_le[:, :], 1, 4), ALU.mult).then_inc(S["qk_sb"], 1)
            pool.wait_ge(S["unit_done"], U0["pin0"])
            pool.wait_ge(S["plo_done"], 1)
            for v in range(2):
                pool.dma_start(pw1[:, v], cmp_w1[v].rearrange("(c p) n -> p c n", p=P)).then_inc(S["w1_in"], 16)

        @block.tensor
        def _(pe):
            mm = nc.tensor.matmul

            def transpose(o, i):
                return nc.tensor.transpose(o, i, ident[:, :])

            def stage_unit(name, q, xh, xl, i, bank_wait=True, operand=None):
                pe.wait_ge(S["lo_done"], i * 2 + (U0[name] + q + 1))
                if bank_wait:
                    pe.wait_ge(S["bank_free"], i * 2 + (B0[name] + q - 1))

                def products(tile, k, first, end):
                    o, col = bank(q, 2, T)[:, tile, :], k * UW + tile * P
                    mm(o, whi[:, q, col:col + P], xh(k), start=first, stop=False, skip_group_check=True)
                    mm(o, whi[:, q, col:col + P], xl(k), start=False, stop=False, skip_group_check=True)
                    return mm(o, wlo[:, q, col:col + P], xh(k), start=False, stop=end, skip_group_check=True)
                if operand is None:
                    for tile in range(2):
                        for k in range(KD):
                            last = products(tile, k, k == 0, k == KD - 1)
                else:
                    for k in range(KD):
                        operand(k)
                        for tile in range(2):
                            last = products(tile, k, k == 0 and tile == 0, k == KD - 1)
                last.then_inc(S["unit_done"], 1)

            def stage_pair(name, xh, xl, i, bank_wait=True):
                for q in range(2):
                    stage_unit(name, q, xh, xl, i, bank_wait)

            def values_unit(name, i):
                pe.wait_ge(S["lo_done"], i * 2 + (U0[name] + 2))
                pe.wait_ge(S["bank_free"], i * 2 + B0[name])
                for a in range(TT):
                    o = bank(1, TT, T)[:, a, :]
                    tok = slice(a * P, (a + 1) * P)
                    for k in range(KD):
                        w_h, w_l = whi[:, 1, k * UW:(k + 1) * UW], wlo[:, 1, k * UW:(k + 1) * UW]
                        mm(o, big[:, k, tok], w_h, start=k == 0, stop=False)
                        mm(o, big[:, k, tok], w_l, start=False, stop=False)
                        last = mm(o, big[:, KD + k, tok], w_h, start=False, stop=k == KD - 1)
                last.then_inc(S["unit_done"], 1)

            def keys_unit(name, i):
                pe.wait_ge(S["lo_done"], i * 2 + (U0[name] + 1))
                pe.wait_ge(S["bank_free"], i * 2 + (B0[name] - 1))
                for tile in range(2):
                    o = bank(0, 2, T)[:, tile, :]
                    for k in range(KD):
                        col = k * UW + tile * P
                        mm(o, whi[:, 0, col:col + P], big[:, k, :], start=k == 0, stop=False)
                        mm(o, whi[:, 0, col:col + P], big[:, KD + k, :], start=False, stop=False)
                        last = mm(o, wlo[:, 0, col:col + P], big[:, k, :], start=False, stop=k == KD - 1)
                last.then_inc(S["unit_done"], 1)

            def x_hi(k):
                return xhi[:, k, :]

            def x_lo(k):
                return xlo[:, k, :]

            def bighi(k):
                return big[:, k, :]

            def biglo(k):
                return big[:, KF + k, :]

            def biglo8(k):
                return big[:, KD + k, :]

            def stats_part(n, e, cols=False):
                pe.wait_ge(S["sq_ready"], 4 * n + e + 1)
                if n and e == 0:
                    pe.wait_ge(S["root_done"], n)
                for k in (2 * e, 2 * e + 1):
                    last = mm(bank(2, T), ones[:, :], sq[:, k, :], start=(k == 0), stop=(k == KD - 1),
                              skip_group_check=True)
                if e == 3:
                    last.then_inc(S["stat_ps"], 1)

            def stats(n, cols=False):
                for e in range(4):
                    stats_part(n, e)
                if cols:
                    for a in range(TT):
                        for k in range(KD):
                            last = mm(bank(3, TT)[:, a:a + 1], sq[:, k, a * P:(a + 1) * P], ones[:, 0:1],
                                      start=(k == 0), stop=(k == KD - 1))
                    last.then_inc(S["rc_ps"], 1)

            def accumulating(name, ks, operand, n):
                per = len(ks)
                for grp in range(4):
                    for q in range(per):
                        pe.wait_ge(S["lo_done"], U0[name] + grp * per + q + 1)
                        if q == 0:
                            pe.wait_ge(S["bank_free"], B0[name] + grp - 1)
                        if q == 1 and grp:
                            stats_part(n, grp - 1)
                        k0 = sum(ks[:q])
                        for k in range(ks[q]):
                            if grp == 0:
                                operand(k0 + k)
                            for tile in range(2):
                                o = bank(grp % 2, 2, T)[:, tile, :]
                                col = k * UW + tile * P
                                f = q == 0 and k == 0 and tile == 0
                                e = q == per - 1 and k == ks[q] - 1
                                w_h, w_l = whi[:, q % 2, col:col + P], wlo[:, q % 2, col:col + P]
                                mm(o, w_h, bighi(k0 + k), start=f, stop=False, skip_group_check=True)
                                mm(o, w_h, biglo(k0 + k), start=False, stop=False, skip_group_check=True)
                                last = mm(o, w_l, bighi(k0 + k), start=False, stop=e, skip_group_check=True)
                        last.then_inc(S["unit_done"], 1)

            def tokens_by(w, b, n, hi_k, lo_k, done):
                for a in range(TT):
                    tok = slice(a * P, (a + 1) * P)
                    for k in range(KD):
                        mm(bank(b, TT, n)[:, a, :], hi_k(k)[:, tok].bitcast(F32), w[:, k, :], start=k == 0, stop=False)
                        last = mm(bank(b, TT, n)[:, a, :], lo_k(k)[:, tok].bitcast(F32), w[:, k, :], start=False,
                                  stop=k == KD - 1)
                last.then_inc(done, 1)

            pe.wait_ge(S["cst_pool"], 1)
            pe.wait_ge(S["x_in"], 16)
            for k in range(KD):
                for a in range(TT):
                    last = transpose(bank(4 + k // 2, 2, T)[:, k % 2, a * P:(a + 1) * P], xtok[:, a, k * P:(k + 1) * P])
                if k % 2:
                    last.then_inc(S["xt_ps"], 1)
            pe.wait_ge(S["vec_in"], 16 * 8)
            transpose(bank(3, 4, P)[:, 0, :], rows[:, :])
            transpose(bank(3, 4, P)[:, 1, :], crows[:, :]).then_inc(S["vec_ps"], 1)
            pe.wait_ge(S["vec_sb"], 2)
            stats(0, cols=True)
            pe.wait_ge(S["xlo_done"], 8)
            pe.wait_ge(S["small_in"], 16 * 9)
            tokens_by(wba, 4, 2 * HV, x_hi, x_lo, S["ba_ps"])
            stage_pair("qkv", x_hi, x_lo, 0, bank_wait=False)
            def head_sums(src, ready, done):
                for s in range(8):
                    pe.wait_ge(ready, s + 1)
                    for hd in (2 * s, 2 * s + 1):
                        for a in range(TT):
                            last = mm(bank(2, TT, 16)[:, a, hd:hd + 1], src[:, hd, a * P:(a + 1) * P], ones[:, 0:1],
                                      start=True, stop=True)
                last.then_inc(done, 1)

            def head_rows(order, ready, freed, done):
                pe.wait_ge(ready, 1)
                for n, s in enumerate(order):
                    if n >= 4:
                        pe.wait_ge(freed, n - 3)
                    for e in range(2):
                        for a in range(TT):
                            last = mm(bank((3, 4, 5, 6)[n % 4], 2, T)[:, e, a * P:(a + 1) * P],
                                      hcol[:, a, 2 * s + e:2 * s + e + 1].to_broadcast([P, P]), ident[:, :],
                                      start=True, stop=True)
                    last.then_inc(done, 1)

            with pe.Fori(1, 6) as i:
                stage_pair("qkv", x_hi, x_lo, i)
            pe.wait_ge(S["root_done"], 1)
            head_sums(scr, S["l2_sq"], S["l2_ps"])
            with pe.Fori(6, PAIRS["qkv"]) as i:
                stage_pair("qkv", x_hi, x_lo, i)
            pe.wait_ge(S["ba_dve"], N_BA)
            pe.wait_ge(S["cst_pool"], N_CST)
            gflat = gdec.rearrange("p a h -> p (a h)")
            mm(bank(7, 2, 32)[:, 0, :], tri_le[:, :], gflat, start=True, stop=True).then_inc(S["ktok_ps"], 1)
            mm(bank(7, 2, 32)[:, 1, :], tri_gt[:, :], gflat, start=True, stop=True).then_inc(S["cum_ps"], 1)

            head_rows(QK_ORDER, S["hrec"], S["l2_done"], S["l2_rows"])

            pe.wait_ge(S["l2_done"], 8)
            pe.wait_ge(S["cum_act"], 2)
            with pe.Fori(0, 4) as j:
                pe.wait_ge(S["bank_free"], j * 2 + B0["z"])
                pe.wait_ge(S["oT_sb"], j * 2 + 1)
                pe.wait_ge(S["kqf_sb"], j * 2 + 2)
                for c in range(2):
                    tok = slice(c * P, (c + 1) * P)
                    for i in range(2):
                        mm(bank(c, 4, P)[:, i, :], kqf[:, i, tok], kqf[:, i, tok], start=True, stop=True)
                        last = mm(bank(c, 4, P)[:, 2 + i, :], kqf[:, i, tok], kqf[:, 2 + i, tok], start=True, stop=True)
                    last.then_inc(S["kq_ps"], 1)
                for c in range(2):
                    pe.wait_ge(S["gtri_done"], j * 2 + (c + 1))
                    mm(bank(2 + 2 * c, 4, P), tri_gt[:, :], gtri[:, c], start=True, stop=True).then_inc(S["decay_ps"], 1)
                    for e in range(4):
                        last = mm(bank(3 + 2 * c, 4, P)[:, e, :], gtri[:, c, e, :], tri_gt[:, :], start=True, stop=True)
                    last.then_inc(S["decay_ps"], 1)
                mm(bank(6, 4, P), ones[:, :], gtri[:, 1], start=True, stop=True).then_inc(S["decay_ps"], 1)
                for c in range(2):
                    for i in range(2):
                        last = transpose(bank(7, 2, 2, P)[:, c, i, :], kqf[:, i, c * P:(c + 1) * P])
                last.then_inc(S["ktok_ps"], 1)
                pe.wait_ge(S["vf_sb"], j + 1)
                for c in range(2):
                    pe.wait_ge(S["decay_sb"], j * 5 + (2 * c + 1))
                    for e in range(4):
                        last = transpose(bank(2 + 2 * c, 4, P)[:, e, :], vf[:, e, c * P:(c + 1) * P])
                    last.then_inc(S["vtok_ps"], 1)

                def y_products(v, c):
                    if v == 0:
                        pe.wait_ge(S["a_sb"], j * 2 + (c + 1))
                        pe.wait_ge(S["decay_sb"], j * 5 + (2 * c + 2))
                    else:
                        pe.wait_ge(S["t_upd"], j * 14 + (2 * (v - 1) + c + 1))
                    for e in range(4):
                        src = ident[:, :] if v == 0 else TTr[:, c, e, :]
                        last = mm(bank(3 + 2 * c, 4, P)[:, e, :], dA[:, c, e, :], src, start=True, stop=True)
                    last.then_inc(S["y_ps"], 1)

                def z_products(v, c):
                    if v == 1:
                        pe.wait_ge(S["tinit"], j * 4 + (2 * c + 2))
                        if c == 0:
                            pe.wait_ge(S["decay_sb"], j * 5 + 5)
                        else:
                            pe.wait_ge(S["ktok_sb"], j + 1)
                        pe.wait_ge(S["qk_raw"], j * 2 + (c + 1))
                    pe.wait_ge(S["y_sb"], j * 14 + (2 * v + c + 1))
                    for e in range(4):
                        last = mm(bank(6 + c, 4, P)[:, e, :], Tr[:, c, e, :], yb[:, c, e, :], start=True, stop=True)
                        if v < LV - 1:
                            last = mm(bank(c, 4, P)[:, e, :], yb[:, c, e, :], Tr[:, c, e, :], start=True, stop=True)
                    last.then_inc(S["z_ps"], 1)

                def z_tile(q, tile):
                    if tile == 0:
                        pe.wait_ge(S["lo_done"], j * 2 + (U0["z"] + q + 1))
                    o = bank(6 + q, 2, T)[:, tile, :]
                    for k in range(KD):
                        col = k * UW + tile * P
                        mm(o, whi[:, q, col:col + P], xhi[:, k, :], start=k == 0, stop=False)
                        mm(o, whi[:, q, col:col + P], xlo[:, k, :], start=False, stop=False)
                        last = mm(o, wlo[:, q, col:col + P], xhi[:, k, :], start=False, stop=k == KD - 1)
                    if tile == 1:
                        last.then_inc(S["unit_done"], 1)

                y_products(0, 0)
                y_products(0, 1)
                for v in range(1, LV):
                    y_products(v, 0)
                    if v > 1:
                        z_products(v - 1, 1)
                    z_products(v, 0)
                    y_products(v, 1)
                z_products(LV - 1, 1)
                pe.wait_ge(S["t_upd"], j * 14 + 13)
                pe.wait_ge(S["bv_sb"], j * 2 + 1)
                pe.wait_ge(S["qk_raw"], j * 2 + 1)
                for e in range(4):
                    last = mm(bank(0, 4, P)[:, e, :], TTr[:, 0, e, :], bv[:, 0, e, :], start=True, stop=True)
                last.then_inc(S["u_ps"], 1)
                z_tile(0, 0)
                pe.wait_ge(S["fv_sb"], j + 1)
                pe.wait_ge(S["ktok_sb"], j + 1)
                for e in range(4):
                    last = mm(bank(2, 4, P)[:, e, :], ktok[:, 0, e // 2, :], bv[:, 0, e, :], start=True, stop=True)
                last.then_inc(S["s_ps"], 1)
                pe.wait_ge(S["vn_sb"], j * 2 + 1)
                pe.wait_ge(S["qk_sb"], j * 2 + 1)
                for e in range(4):
                    last = mm(bank(3, 4, P)[:, e, :], vn[:, 0, e, :], dQ[:, 0, e, :], start=True, stop=True)
                last.then_inc(S["o_ps"], 1)
                pe.wait_ge(S["s_sb"], j + 1)
                pe.wait_ge(S["bv_sb"], j * 2 + 2)
                for e in range(4):
                    last = mm(bank(4, 4, P)[:, e, :], kqf[:, e // 2, P:T], Ss[:, e, :], start=True, stop=True)
                last.then_inc(S["ks_ps"], 1)
                z_tile(0, 1)
                pe.wait_ge(S["r1_sb"], j + 1)
                pe.wait_ge(S["t_upd"], j * 14 + 14)
                for e in range(4):
                    last = mm(bank(1, 4, P)[:, e, :], TTr[:, 1, e, :], bv[:, 1, e, :], start=True, stop=True)
                last.then_inc(S["u_ps"], 1)
                z_tile(1, 0)
                pe.wait_ge(S["vn_sb"], j * 2 + 2)
                pe.wait_ge(S["qk_sb"], j * 2 + 2)
                pe.wait_ge(S["qdec_sb"], j + 1)
                for e in range(4):
                    mm(bank(5, 4, P)[:, e, :], Ss[:, e, :], eq[:, e, :], start=True, stop=False)
                    last = mm(bank(5, 4, P)[:, e, :], vn[:, 1, e, :], dQ[:, 1, e, :], start=False, stop=True)
                last.then_inc(S["o_ps"], 1)
                z_tile(1, 1)
            pe.wait_ge(S["oT_sb"], 9)
            head_sums(osq, S["on_sq"], S["on_ps"])
            pe.wait_ge(S["bank_free"], B0["gout"])
            pe.wait_ge(S["hrec"], 2)
            head_rows(range(8), S["hrec"], S["on_done"], S["on_rows"])
            accumulating("gout", (8, 8), lambda k: pe.wait_ge(S["olo_done"], k // 2 + 1) if k % 2 == 0 else None, 1)
            stats_part(1, 3)

            def ffn_and_ple(layer):
                n = 2 + 4 * layer
                fin_, fout_, pin_, gate_ = (f"{v}{layer}" for v in ("fin", "fout", "pin", "gate"))
                stage_unit(fin_, 0, x_hi, x_lo, 0, operand=lambda k: pe.wait_ge(S["xlo_done"], 8 * (1 + 4 * layer) + k + 1))
                stats(n)
                stage_unit(fin_, 1, x_hi, x_lo, 0)
                with pe.Fori(1, PAIRS[fin_]) as i:
                    stage_pair(fin_, x_hi, x_lo, i)
                for k in range(2):
                    for a in range(TT):
                        last = transpose(bank(3, 2, T)[:, k, a * P:(a + 1) * P], ptok[:, layer, a, k * P:(k + 1) * P])
                last.then_inc(S["pt_ps"], 1)
                accumulating(fout_, FOUT_K, lambda k: pe.wait_ge(S["flo_done"], 11 * layer + k // 2 + 1)
                             if k % 2 == 0 else None, n + 1)

                def embeddings(q, groups):
                    for g in groups:
                        for tile in range(2):
                            o, col = bank(4 + g, 2, T)[:, tile, :], g * UW + tile * P
                            f = q == 0 and tile == 0
                            mm(o, whi[:, q, col:col + P], phl[:, q, :], start=f, stop=False, skip_group_check=True)
                            mm(o, whi[:, q, col:col + P], phl[:, 2 + q, :], start=False, stop=False, skip_group_check=True)
                            last = mm(o, wlo[:, q, col:col + P], phl[:, q, :], start=False, stop=q == 1,
                                      skip_group_check=True)
                    return last
                pe.wait_ge(S["plo_done"], layer + 1)
                pe.wait_ge(S["lo_done"], U0[pin_] + 1)
                embeddings(0, (0, 1))
                stats_part(n + 1, 3)
                embeddings(0, (2, 3)).then_inc(S["unit_done"], 1)
                pe.wait_ge(S["lo_done"], U0[pin_] + 2)
                embeddings(1, range(4)).then_inc(S["unit_done"], 1)
                stage_unit(gate_, 0, x_hi, x_lo, 0, operand=lambda k: pe.wait_ge(S["xlo_done"], 8 * (2 + 4 * layer) + k + 1))
                stage_unit(gate_, 1, x_hi, x_lo, 0)
                stage_pair(gate_, x_hi, x_lo, 1)

            ffn_and_ple(0)

            stage_unit("kv", 0, bighi, biglo8, 0, operand=lambda k: pe.wait_ge(S["xlo_done"], 8 * 3 + k + 1))
            stats(4, cols=True)
            stage_unit("kv", 1, bighi, biglo8, 0)
            for i in (1, 2):
                keys_unit("kv", i)
                values_unit("kv", i)
            pe.wait_ge(S["w1_in"], 32)
            pe.wait_ge(S["ablk_act"], 9)
            pe.wait_ge(S["ablk_dve"], 9)
            for v in range(2):
                for e in range(2):
                    for c in range(16):
                        last = mm(bank(4 + v, 2, 61)[:, e, :], pw1[:, v, c, e * P:(e + 1) * P], ablk[:, v, c, :],
                                  start=c == 0, stop=c == 15)
            last.then_inc(S["hid_ps"], 1)
            pe.wait_ge(S["xlo_done"], 8 * 5)
            tokens_by(wgt, 7, 3 * NH, x_hi, x_lo, S["gt_ps"])
            for i in range(2):
                stage_pair("q", x_hi, x_lo, i)
            pe.wait_ge(S["hid_sb"], 4)
            for e in range(2):
                last = mm(bank(6, 60), w2k[:, e].rearrange("p d n -> p (d n)"), hid[:, 0, e, :], start=e == 0, stop=e == 1)
            last.then_inc(S["kc_ps"], 1)
            pe.wait_ge(S["gt_dve"], 2)
            for gr in range(NG):
                for e in range(2):
                    last = mm(ps[0:60, 7, gr * ND:(gr + 1) * ND],
                              hrep[:, gr, e, :], w2v[:, e, :], start=e == 0, stop=e == 1)
            last.then_inc(S["kc_ps"], 1)
            pe.wait_ge(S["kc_sb"], 1)
            pe.wait_ge(S["bank_free"], B0["wo"])
            for a in range(TT):
                for hd in range(NH):
                    half = slice(64 * (hd % 2), 64 * (hd % 2) + 64)
                    last = mm(bank(3 - hd % 2, TT, NH // 2, NC)[:, a, hd // 2, :], qT[half, hd // 2, a * P:(a + 1) * P],
                              kcd[half, (hd // NR) * NC:(hd // NR + 1) * NC], start=True, stop=True)
            last.then_inc(S["cs_ps"], 1)
            pe.wait_ge(S["cs_dve"], 10)
            for gr in range(NG):
                for a in range(TT):
                    last = transpose(bank(4 + gr // 2, 2, T)[0:60, gr % 2, a * P:(a + 1) * P],
                                     cs[:, a, NR * gr:NR * gr + NR, :].rearrange("p h n -> p (h n)"))
            last.then_inc(S["pct_ps"], 1)
            pe.wait_ge(S["pct_sb"], 2)
            def scores(gi, r, skip):
                half = slice(64 * (r % 2), 64 * (r % 2) + 64)
                if r == 0:
                    pe.wait_ge(S["fx_act"], gi * 2 + 2)
                if not skip:
                    pe.wait_ge(S["p_act"], gi * 8 + (2 * r - 2))
                s1, s0 = bank(2 + 2 * (r % 2), 2, T), bank(3 + 2 * (r % 2), 2, P)
                for b in range(2):
                    mm(s0[:, b, :], qf[half, r // 2, 0:P], kf[half, b, 0:P], start=b == 0, stop=False,
                       skip_group_check=True)
                mm(s0, identb[:, :], over(causb[:, :], 1, 2), start=False, stop=True, skip_group_check=True)
                for b in range(2):
                    mm(s1[:, b, :], qf[half, r // 2, P:T], kf[half, b, :], start=b == 0, stop=False,
                       skip_group_check=True)
                mm(s1[:, :, P:T], identb[:, :], over(causb[:, :], 1, 2), start=False, stop=True,
                   skip_group_check=True).then_inc(S["sc_ps"], 1)

            def turned(gi, r, skip):
                for b in range(2):
                    pe.wait_ge(S["pw_dve"], gi * 8 + (2 * r + b + 1))
                    if not skip:
                        pe.wait_ge(S["pts_act"], gi * 8 + (2 * r + b - 1))
                    transpose(bank(6 + b, 3, P)[:, 0, :], pr0[:, r % 2, b, :])
                    for s in range(2):
                        last = transpose(bank(6 + b, 3, P)[:, 1 + s, :], pr1[:, r % 2, b, s * P:(s + 1) * P])
                    last.then_inc(S["ptr_ps"], 1)

            def output(gi, r, first):
                pe.wait_ge(S["pts_act"], gi * 8 + (2 * r + 2))
                if r == 0:
                    pe.wait_ge(S["fx_dve"], gi * 3 + 3)
                if r % 2 == 0 and not first:
                    pe.wait_ge(S["alo"], gi * 2 + (r // 2 - 1))
                o = ps[64 * (r % 2):64 * (r % 2) + 64, r // 2, 0:T]
                for b in range(2):
                    mm(o, vff[:, b, 0, :], pts[:, r % 2, b, 0:2, :].rearrange("p s q -> p (s q)"), start=b == 0,
                       stop=False, skip_group_check=True)
                    mm(o[:, P:T], vff[:, b, 1, :], pts[:, r % 2, b, 2, :], start=False, stop=False,
                       skip_group_check=True)
                last = mm(o, vz[0:60, r, :], pcf[0:60, :], start=False, stop=True, skip_group_check=True)
                last.then_inc(S["av_ps"], 1)

            def group(gi, first, last):
                scores(gi, 1, first)
                turned(gi, 0, first)
                if not first:
                    output(gi - 1, 3, False)
                for r in (2, 3):
                    scores(gi, r, False)
                    turned(gi, r - 1, False)
                    output(gi, r - 2, first)
                if not last:
                    scores(gi + 1, 0, False)
                turned(gi, 3, False)
                output(gi, 2, first)
            scores(0, 0, True)
            group(0, True, False)
            with pe.Fori(1, NG - 1) as gi:
                group(gi, False, False)
            group(NG - 1, False, True)
            output(NG - 1, 3, False)
            pe.wait_ge(S["alo"], 8)
            for i in range(2):
                for q in range(2):
                    stage_unit("wo", q, bighi, biglo8, i)
                    if i or q:
                        stats_part(5, 2 * i + q - 1)
            stats_part(5, 3)
            ffn_and_ple(1)
            pe.wait_ge(S["h_ready"], 28)
            for a in range(TT):
                for e in range(2):
                    for k in range(4):
                        last = transpose(bank(2 + 2 * a + e, 4, P)[:, k, :], h[:, 4 * e + k, a * P:(a + 1) * P])
                    last.then_inc(S["out_ps"], 1)

        @block.scalar
        def _(act):
            A = nc.scalar.activation

            n_tbl = [0]

            def table(func):
                A(tcol[:, n_tbl[0]:n_tbl[0] + 1], epsc[:, 0:1], func)
                n_tbl[0] += 1

            def split(stage, q, i=0):
                u = i * 2 + (U0[stage] + q)
                n = unit_k(stage, q) * UW
                act.wait_ge(landed[q % 2], i * 16 + (8 * U0[stage] + 16 * (q // 2 + 1)))
                if not isinstance(u, int) or u >= 2:
                    act.wait_ge(S["unit_done"], u - 1)
                A(whi[:, q % 2, 0:n], raw[:, q % 2, 0:n], ACT.Copy).then_inc(S["hi_done"], 1)

            act.wait_ge(S["cst_dve"], 1)
            act.dma_start(rows[0:16, :], mix_pre_norm.rearrange("a (k p) -> (a k) p", p=P)).then_inc(S["vec_in"], 16)
            act.dma_start(rows[16:32, :], mix_post_norm.rearrange("a (k p) -> (a k) p", p=P)).then_inc(S["vec_in"], 16)
            act.dma_start(rows[32:48, :], ffn_pre_norm.rearrange("a (k p) -> (a k) p", p=P)).then_inc(S["vec_in"], 16)
            act.dma_start(rows[48:64, :], ffn_post_norm.rearrange("a (k p) -> (a k) p", p=P)).then_inc(S["vec_in"], 16)
            act.dma_start(rows[64:72, :], kv_norm.rearrange("(k p) -> k p", p=P)).then_inc(S["vec_in"], 16)
            act.dma_start(rows[72:73, :], gdn_o_norm).then_inc(S["vec_in"], 16)
            act.dma_start(rows[96:128, :], cmp_pos.rearrange("v (c e) d -> (v c) (e d)", e=2)).then_inc(S["vec_in"], 16)
            act.dma_start(crows[:, :], gdn_conv_w[0].rearrange("j (t p) -> (j t) p", p=P)).then_inc(S["vec_in"], 16)

            def root(n, cols=False):
                r = rpost if n % 2 else rpre
                act.wait_ge(S["stat_ps"], n + 1)
                A(r[:, :], bank(2, T), ACT.Sqrt, bias=epsc[:, 0:1], scale=1.0 / DM).then_inc(S["root_done"], 1)
                if cols:
                    act.wait_ge(S["rc_ps"], n // 4 + 1)
                    A(rcol[:, :], bank(3, TT), ACT.Sqrt, bias=epsc[:, 0:1], scale=1.0 / DM).then_inc(S["rc_root"], 1)

            def squares_of_h(n, m, e):
                act.wait_ge(S["h_ready"], 4 * m + e + 1)
                A(sq[:, 2 * e:2 * e + 2, :], h[:, 2 * e:2 * e + 2, :], ACT.Square).then_inc(S["sq_ready"], 1)

            def xsplit(dst, cols, e):
                for k in (2 * e, 2 * e + 1):
                    A(dst(k), h[:, k, :], ACT.Copy, scale=gain(cols, k)).then_inc(S["xhi_done"], 1)

            def xh(k):
                return xhi[:, k, :]

            def bh(k):
                return big[:, k, :]

            def squares_of_y(b, e):
                act.wait_ge(S["bank_free"], b + 1)
                A(sq[:, 2 * e:2 * e + 2, :], y[:, 2 * e:2 * e + 2, :], ACT.Square).then_inc(S["sq_ready"], 1)

            split("qkv", 0)
            act.wait_ge(S["cst_dve"], N_DCST)
            for e in range(4):
                squares_of_h(0, 0, e)
            act.wait_ge(S["vec_sb"], 2)
            for e in range(4):
                xsplit(xh, MIXPRE[0], e)
            split("qkv", 1)
            root(0, cols=True)
            act.wait_ge(S["ba_dve"], 2)
            A(beta, balog[:, :, 0:HV], ACT.Sigmoid).then_inc(S["ba_act"], 1)
            act.wait_ge(S["ba_dve"], 5)
            A(sm[2], sm[2], ACT.Exp, scale=-1.0).then_inc(S["ba_act"], 1)
            A(alog[:, :], alog[:, :], ACT.Exp).then_inc(S["ba_act"], 1)

            def silu_qkv(i):
                for q in range(2):
                    act.wait_ge(S["conv_done"], i * 2 + (q + 1))
                    A(qkvT[:, bass.ds(i * 4 + 2 * q, 2), :], acc[:, q], ACT.Silu).then_inc(S["silu_done"], 1)
            table(ACT.Silu)
            act.wait_ge(S["rc_ps"], 1)
            with act.Fori(0, 4) as i:
                split("qkv", 0, i + 1)
                split("qkv", 1, i + 1)
                silu_qkv(i)
                for q in range(2):
                    act.wait_ge(S["silu_done"], i * 2 + (q + 1))
                    tiles = bass.ds(i * 4 + 2 * q, 2)
                    A(scr[:, tiles, :], qkvT[:, tiles, :], ACT.Square).then_inc(S["l2_sq"], 1)
            for i in (4, 5):
                split("qkv", 0, i + 1)
                split("qkv", 1, i + 1)
                silu_qkv(i)
            act.wait_ge(S["l2_ps"], 1)
            l2 = bank(2, TT, 16)
            A(hcol[:, :, 0:8], l2[:, :, 0:8], ACT.Sqrt, bias=epsc[:, 1:2], scale=float(HD)).then_inc(S["l2_root"], 1)
            A(hcol[:, :, 8:16], l2[:, :, 8:16], ACT.Sqrt, bias=epsc[:, 0:1]).then_inc(S["l2_root"], 1)
            split("qkv", 0, 7)
            split("qkv", 1, 7)
            silu_qkv(6)
            silu_qkv(7)

            act.wait_ge(S["cum_ps"], 1)
            A(einc, bank(7, 2, TT, HV)[:, 0], ACT.Exp).then_inc(S["cum_act"], 1)
            A(faft, bank(7, 2, TT, HV)[:, 1], ACT.Exp).then_inc(S["cum_act"], 1)
            A(epsc[:, 3:4], epsc[:, 0:1], ACT.Copy).then_inc(S["oT_sb"], 1)
            act.wait_ge(S["cum_act"], 2)
            act.wait_ge(S["silu_done"], 16)
            with act.Fori(0, 4) as j:
                act.wait_ge(S["l2_done"], j * 2 + 2)
                act.wait_ge(S["oT_sb"], j * 2 + 1)
                A(kqf[:, 0:2, :], qkvT[:, bass.ds(j * 2 + HK, 2), :], ACT.Copy).then_inc(S["kqf_sb"], 1)
                A(kqf[:, 2:4, :], qkvT[:, bass.ds(j * 2, 2), :], ACT.Copy).then_inc(S["kqf_sb"], 1)
                for c in range(2):
                    for part, dst in ((0, dQ), (1, dA)):
                        act.wait_ge(S["decay_ps"], j * 5 + (2 * c + part + 1))
                        A(dst[:, c], bank(2 + 2 * c + part, 4, P), ACT.Exp).then_inc(S["decay_sb"], 1)
                act.wait_ge(S["decay_ps"], j * 5 + 5)
                A(eq, bank(6, 4, P), ACT.Exp).then_inc(S["decay_sb"], 1)
                A(vf, qkvT[:, bass.ds(j * 4 + 2 * HK, 4), :], ACT.Copy).then_inc(S["vf_sb"], 1)
                act.wait_ge(S["ktok_ps"], j + 2)
                A(ktok, bank(7, 2, 2, P), ACT.Copy).then_inc(S["ktok_sb"], 1)
                for c in range(2):
                    act.wait_ge(S["vtok_ps"], j * 2 + (c + 1))
                    for e in range(4):
                        last = A(bv[:, c, e, :], bank(2 + 2 * c, 4, P)[:, e, :], ACT.Copy,
                                 scale=beta[:, c, bass.ds(j * 4 + e, 1)])
                    last.then_inc(S["bv_sb"], 1)
                split("z", 0, j)
                split("z", 1, j)
                act.wait_ge(S["vn_sb"], j * 2 + 1)
                for e in range(4):
                    last = A(bv[:, 0, e, :], vn[:, 0, e, :], ACT.Copy, scale=faft[:, 0, bass.ds(j * 4 + e, 1)])
                last.then_inc(S["fv_sb"], 1)
                act.wait_ge(S["s_ps"], j + 1)
                A(Ss, bank(2, 4, P), ACT.Copy).then_inc(S["s_sb"], 1)
                for c in range(2):
                    act.wait_ge(S["o_ps"], j * 2 + (c + 1))
                    A(oT[:, bass.ds(j * 4, 4), c * P:(c + 1) * P], bank(3 + 2 * c, 4, P), ACT.Copy).then_inc(S["oT_sb"], 1)
            act.wait_ge(S["oT_sb"], 9)
            for s in range(8):
                A(osq[:, 2 * s:2 * s + 2, :], oT[:, 2 * s:2 * s + 2, :], ACT.Square).then_inc(S["on_sq"], 1)
            act.wait_ge(S["on_ps"], 1)
            A(hcol[:, :, :], bank(2, TT, 16), ACT.Sqrt, bias=epsc[:, 0:1], scale=1.0 / HD).then_inc(S["on_root"], 1)
            act.wait_ge(S["bank_free"], B0["gout"])
            for s in range(8):
                A(zT[:, 2 * s:2 * s + 2, :], zT[:, 2 * s:2 * s + 2, :], ACT.Silu).then_inc(S["sz_done"], 1)
            split("gout", 0)
            for s in range(8):
                if s == 4:
                    split("gout", 1)
                act.wait_ge(S["oz_done"], s + 1)
                A(big[:, 2 * s:2 * s + 2, :], oT[:, 2 * s:2 * s + 2, :], ACT.Copy).then_inc(S["ohi_done"], 1)

            def post_then_pre(n, m, cols):
                root(n)
                for e in range(4):
                    act.wait_ge(S["h_ready"], 4 * m + e + 1)
                    xsplit(xh, cols, e)
                    squares_of_h(n + 1, m, e)
                root(n + 1)

            for gr in range(4):
                for q in range(2):
                    split(*(("gout", q, gr + 1) if gr < 3 else ("fin0", q)))
                if gr == 3:
                    table(ACT.Sqrt)
                squares_of_y(B0["gout"] + gr, gr)
            post_then_pre(1, 1, FFNPRE[0])

            def ffn_and_ple(layer, after):
                fin_, fout_, pin_, gate_ = (f"{v}{layer}" for v in ("fin", "fout", "pin", "gate"))

                def hidden(i):
                    act.wait_ge(S["bank_free"], i * 2 + (B0[fin_] + 1))
                    A(t1[:, 0], t0[:, 0], ACT.Silu).then_inc(S["sg_done"], 1)
                    act.wait_ge(S["hid_done"], i + (11 * layer + 1))
                    A(big[:, bass.ds(i * 2, 2), :], t2[:, 1], ACT.Copy).then_inc(S["fhi_done"], 1)
                table(ACT.Silu)
                with act.Fori(0, PAIRS[fin_] - 1) as i:
                    split(fin_, 0, i + 1)
                    split(fin_, 1, i + 1)
                    hidden(i)
                split(fout_, 0)
                split(fout_, 1)
                hidden(PAIRS[fin_] - 1)
                act.wait_ge(S["pt_ps"], layer + 1)
                A(phl[:, 0:2, :], bank(3, 2, T), ACT.Copy).then_inc(S["phi_done"], 1)
                split(fout_, 2)
                split(fout_, 3)
                for gr in range(4):
                    for q in range(2):
                        if gr < 3:
                            split(fout_, q, 2 * gr + 2)
                        else:
                            split(pin_, q)
                    if gr == 3:
                        table(ACT.Sqrt)
                    squares_of_y(B0[fout_] + gr, gr)
                    if gr < 3:
                        for q in (2, 3):
                            split(fout_, q, 2 * gr + 2)
                root(3 + 4 * layer)
                split(gate_, 0)
                for e in range(4):
                    act.wait_ge(S["h_ready"], 4 * (2 + 3 * layer) + e + 1)
                    A(xhi[:, 2 * e:2 * e + 2, :], h[:, 2 * e:2 * e + 2, :], ACT.Copy).then_inc(S["xhi_done"], 2)
                table(ACT.Sigmoid)
                split(gate_, 1)

                def next_hi(e):
                    act.wait_ge(S["h_ready"], 4 * (3 + 3 * layer) + e + 1)
                    xsplit(bh, KVN, e)
                    squares_of_h(4, 3, e)
                for g in range(4):
                    act.wait_ge(S["unit_done"], U0[gate_] + g + 1)
                    if g >= 2:
                        act.wait_ge(S["bank_free"], B0[gate_] + g - 1)
                    A(t1[:, g % 2], bank(g % 2, 2, T), ACT.Sigmoid).then_inc(S["sgm_done"], 1)
                    if g < 2:
                        split(gate_, g, 1)
                    elif after:
                        split(after, g - 2)
                    if after and g:
                        next_hi(g - 1)
                if after:
                    next_hi(3)
            ffn_and_ple(0, "kv")

            root(4, cols=True)
            act.wait_ge(S["unit_done"], U0["kv"])
            for e in range(4):
                xsplit(xh, MIXPRE[1], e)
            split("kv", 0, 1)
            split("kv", 1, 1)
            act.wait_ge(S["vec_sb"], 2)
            act.wait_ge(S["bank_free"], B0["kv"] + 1)
            block_copies(A, 0, S["ablk_act"])
            split("kv", 0, 2)
            split("kv", 1, 2)
            split("q", 0)
            split("q", 1)
            act.wait_ge(S["hb_sb"], 2)
            for v in range(2):
                for e in range(2):
                    A(hid[:, v, e, :], bank(4 + v, 2, 61)[:, e, 0:60], ACT.Silu, bias=cb[:, v, e:e + 1]).then_inc(S["hid_sb"], 1)
            act.wait_ge(S["gt_dve"], 2)
            A(gates[:, :, :], gates[:, :, :], ACT.Sigmoid).then_inc(S["gt_done"], 1)
            split("q", 0, 1)
            split("q", 1, 1)
            split("wo", 0)
            split("wo", 1)
            act.wait_ge(S["cs_dve"], 5)
            A(cs, cs, ACT.Exp, scale=ND ** -0.5).then_inc(S["cs_act"], 1)
            act.wait_ge(S["pct_ps"], 1)
            for e in range(2):
                A(pct[0:60, 2 * e:2 * e + 2, :], ps[0:60, 4 + e, 0:512].rearrange("p (a b) -> p a b", a=2), ACT.Copy).then_inc(S["pct_sb"], 1)
            def operands(gi):
                A(qf, qT[:, bass.ds(gi * 2, 2), :], ACT.Copy).then_inc(S["fx_act"], 1)
                A(kf, kdup[:, :, bass.ds(gi, 1), :].rearrange("p b g s -> p (b g) s"), ACT.Copy).then_inc(S["fx_act"], 1)

            def exps(gi, r, skip):
                act.wait_ge(S["mx_dve"], gi * 12 + (3 * r + 3))
                s1, s0 = bank(2 + 2 * (r % 2), 2, T), bank(3 + 2 * (r % 2), 2, P)
                if not skip:
                    act.wait_ge(S["ptr_ps"], gi * 8 + (2 * r - 2))
                for b in range(2):
                    A(pr0[:, r % 2, b, :], s0[:, b, :], ACT.Exp, scale=ND ** -0.5, bias=hst[:, r % 2, 1, b:b + 1],
                      accum_out=hst[:, r % 2, 2, b:b + 1])
                    A(pr1[:, r % 2, b, :], s1[:, b, :], ACT.Exp, scale=ND ** -0.5, bias=hst[:, r % 2, 1, 2 + b:3 + b],
                      accum_out=hst[:, r % 2, 2, 2 + b:3 + b]).then_inc(S["p_act"], 1)

            def turned(gi, r, skip):
                if not skip:
                    act.wait_ge(S["av_ps"], gi * 4 + (r - 1))
                for b in range(2):
                    act.wait_ge(S["ptr_ps"], gi * 8 + (2 * r + b + 1))
                    A(pts[:, r % 2, b], bank(6 + b, 3, P), ACT.Copy).then_inc(S["pts_act"], 1)

            def out_hi(gi, c):
                act.wait_ge(S["av_ps"], gi * 4 + (2 * c + 2))
                A(big[:, bass.ds(gi * 2 + c, 1), :], bank(c, 1, T), ACT.Copy).then_inc(S["ahi"], 1)

            def group(gi, first, last):
                exps(gi, 1, first)
                turned(gi, 0, first)
                if not first:
                    out_hi(gi - 1, 1)
                exps(gi, 2, False)
                turned(gi, 1, first)
                if not last:
                    act.wait_ge(S["sc_ps"], gi * 4 + 4)
                    operands(gi + 1)
                exps(gi, 3, False)
                turned(gi, 2, False)
                out_hi(gi, 0)
                if not last:
                    exps(gi + 1, 0, False)
                turned(gi, 3, False)
            operands(0)
            exps(0, 0, True)
            group(0, True, False)
            with act.Fori(1, NG - 1) as gi:
                group(gi, False, False)
            group(NG - 1, False, True)
            out_hi(NG - 1, 1)
            for i in range(2):
                for q in range(2):
                    if i == 0:
                        split("wo", q, 1)
                    else:
                        split("fin1", q)
                for q in range(2):
                    if i and q:
                        table(ACT.Sqrt)
                    squares_of_y(B0["wo"] + 2 * i + q, 2 * i + q)
            post_then_pre(5, 4, FFNPRE[1])
            ffn_and_ple(1, None)
            for a in range(TT):
                act.wait_ge(S["out_ps"], 2 * a + 2)
                A(otok[:, a, 512:DM], bank(3 + 2 * a, 512), ACT.Copy).then_inc(S["out_act"], 1)

        @block.vector
        def _(dve):
            V = nc.vector
            stt = V.scalar_tensor_tensor

            def split(stage, q, i=0):
                u = i * 2 + (U0[stage] + q)
                n = unit_k(stage, q) * UW
                dve.wait_ge(S["hi_done"], u + 1)
                V.tensor_tensor(wlo[:, q % 2, 0:n], raw[:, q % 2, 0:n], whi[:, q % 2, 0:n],
                                ALU.subtract).then_inc(S["lo_done"], 1)

            for t, v in ((rows, 0.0), (ident, 0.0), (ones, 1.0), (causb, 0.0), (cmask, 0.0), (m1t, 1.0),
                         (rmask, 1.0)):
                V.memset(t[tuple([slice(None)] * len(t.shape))], v).then_inc(S["cst_dve"], 1)
            for v in range(LV):
                m = masks[:, v, :].rearrange("p (m e b) -> p m e b", e=2, b=1 << v)
                for e in range(2):
                    V.memset(m[:, :, e, :], float(e)).then_inc(S["cst_dve"], 1)
            V.memset(epsc[:, 0:1], EPS).then_inc(S["cst_dve"], 1)
            V.memset(epsc[:, 1:2], EPS * HD).then_inc(S["cst_dve"], 1)

            def rstd(n, cols=False):
                r = rpost if n % 2 else rpre
                dve.wait_ge(S["root_done"], n + 1)
                V.reciprocal(r[:, :], r[:, :]).then_inc(S["rstd_done"], 1)
                if cols:
                    dve.wait_ge(S["rc_root"], n // 4 + 1)
                    V.reciprocal(rcol[:, :], rcol[:, :]).then_inc(S["rcol_done"], 1)

            XN = [0]

            def xlo_part(hi, lo, cols, e):
                for k in (2 * e, 2 * e + 1):
                    dve.wait_ge(S["xhi_done"], XN[0] + k + 1)
                    if cols is None:
                        V.tensor_tensor(lo(k), h[:, k, :], hi(k), ALU.subtract).then_inc(S["xlo_done"], 1)
                    else:
                        stt(out=lo(k), in0=h[:, k, :], scalar=gain(cols, k), in1=hi(k), op0=ALU.mult,
                            op1=ALU.subtract).then_inc(S["xlo_done"], 1)
                if e == 3:
                    XN[0] += KD

            def xsplit(hi, lo, cols):
                for e in range(4):
                    xlo_part(hi, lo, cols, e)

            def xh(k):
                return xhi[:, k, :]

            def xl(k):
                return xlo[:, k, :]

            def times_rstd(dst, q, done_at):
                dve.wait_ge(S["unit_done"], done_at)
                return V.tensor_tensor(dst, bank(q, 2, T), over(rpre[:, :], 1, 2), ALU.mult).then_inc(S["bank_free"], 1)

            for e in range(4):
                dve.wait_ge(S["xt_ps"], e + 1)
                V.tensor_copy(h[:, 2 * e:2 * e + 2, :], bank(4 + e, 2, T)).then_inc(S["h_ready"], 1)
            dve.wait_ge(S["vec_ps"], 1)
            V.tensor_copy(vecs[:, :], bank(3, 4, P)[:, 0, :]).then_inc(S["vec_sb"], 1)
            V.tensor_copy(cw[:, :, :], bank(3, 4, P)[:, 1, :].rearrange("p (j t) -> p j t", j=4)).then_inc(S["vec_sb"], 1)
            dve.wait_ge(S["vec_sb"], 2)
            dve.wait_ge(S["h_ready"], 4)
            split("qkv", 0)
            xsplit(xh, xl, MIXPRE[0])
            split("qkv", 1)
            V.memset(pre[:, :, :, 0:3], 0.0).then_inc(S["conv_dve"], 1)
            rstd(0, cols=True)
            n_ba = [0]

            def ba(ins):
                ins.then_inc(S["ba_dve"], 1)
                n_ba[0] += 1
                dve.wait_ge(S["ba_dve"], n_ba[0])
            dve.wait_ge(S["rcol_done"], 1)
            dve.wait_ge(S["ba_ps"], 1)
            for a in range(TT):
                ba(V.tensor_scalar(balog[:, a, :], bank(4, TT, 2 * HV)[:, a, :], rcol[:, a:a + 1], None, ALU.mult))
            dve.wait_ge(S["small_in"], 16 * 9)
            ba(V.tensor_tensor(sm[0], balog[:, :, HV:2 * HV], over(dtb[:, :], 1, TT), ALU.add))
            ba(V.tensor_scalar(sm[1], sm[0], 0.0, None, ALU.max))
            ba(stt(out=sm[2], in0=sm[0], scalar=-1.0, in1=sm[0], op0=ALU.mult, op1=ALU.max))
            dve.wait_ge(S["ba_act"], 3)
            ba(V.tensor_scalar(sm[3], sm[2], 2.0, None, ALU.add))
            ba(V.reciprocal(sm[3], sm[3]))
            ba(V.tensor_tensor(sm[3], sm[2], sm[3], ALU.mult))
            ba(V.tensor_tensor(sm[4], sm[3], sm[3], ALU.mult))
            ba(V.tensor_scalar(sm[5], sm[4], 1.0 / 13, None, ALU.mult))
            for c in (11, 9, 7, 5, 3):
                ba(stt(out=sm[5], in0=sm[5], scalar=1.0 / c, in1=sm[4], op0=ALU.add, op1=ALU.mult))
            ba(stt(out=sm[5], in0=sm[5], scalar=1.0, in1=sm[3], op0=ALU.add, op1=ALU.mult))
            ba(stt(out=sm[1], in0=sm[5], scalar=2.0, in1=sm[1], op0=ALU.mult, op1=ALU.add))
            ba(stt(out=gdec, in0=sm[1], scalar=-1.0, in1=over(alog[:, :], 1, TT), op0=ALU.mult, op1=ALU.mult))
            assert n_ba[0] == N_BA

            dve.wait_ge(S["rstd_done"], 1)

            def conv_in(i, q):
                dve.wait_ge(S["unit_done"], i * 2 + (q + 1))
                V.tensor_tensor(pre[:, q, :, 3:T + 3], bank(q, 2, T), over(rpre[:, :], 1, 2),
                                ALU.mult).then_inc(S["bank_free"], 1)

            def conv(i, q, n0):
                dve.wait_ge(S["bank_free"], i * 2 + (q + 1))
                for j in range(4):
                    for e in range(2):
                        if j:
                            dve.wait_ge(S["conv_dve"], n0 + 2 * (j - 1) + e + 1)
                        w = cw[:, j, bass.ds(i * 4 + 2 * q + e, 1)]
                        src = pre[:, q, e, j:j + T]
                        if j == 0:
                            ins = V.tensor_scalar(acc[:, q, e, :], src, w, None, ALU.mult)
                        else:
                            ins = stt(out=acc[:, q, e, :], in0=src, scalar=w, in1=acc[:, q, e, :], op0=ALU.mult, op1=ALU.add)
                        ins.then_inc(S["conv_done"] if (j, e) == (3, 1) else S["conv_dve"], 1)

            def conv_pair(i, splits):
                for q in range(2):
                    splits(q)
                    conv_in(i, q)
                    conv(i, q, i * 14 + (7 * q + 1))
            conv_pair(0, lambda q: split("qkv", q, 1))
            with dve.Fori(1, PAIRS["qkv"] - 1) as i:
                dve.wait_ge(S["silu_done"], i * 2)
                conv_pair(i, lambda q: split("qkv", q, i + 1))
            dve.wait_ge(S["l2_root"], 2)
            V.reciprocal(hcol[:, :, :], hcol[:, :, :]).then_inc(S["hrec"], 1)
            dve.wait_ge(S["silu_done"], 14)
            conv_pair(PAIRS["qkv"] - 1, lambda q: None)

            for n, s in enumerate(QK_ORDER):
                dve.wait_ge(S["l2_rows"], n + 1)
                V.tensor_tensor(qkvT[:, 2 * s:2 * s + 2, :], qkvT[:, 2 * s:2 * s + 2, :], bank((3, 4, 5, 6)[n % 4], 2, T),
                                ALU.mult).then_inc(S["l2_done"], 1)
            dve.wait_ge(S["cum_act"], 2)
            stt(out=nbe, in0=beta, scalar=-1.0, in1=einc, op0=ALU.mult, op1=ALU.mult).then_inc(S["cum_dve"], 1)
            dve.wait_ge(S["cum_dve"], 1)
            dve.wait_ge(S["cst_pool"], N_CST)

            def odd(ap, b):
                return ap.rearrange("p h (m e b) -> p h m e b", e=2, b=b)[:, :, :, 1, :]

            def even(ap, b):
                return ap.rearrange("p h (m e b) -> p h m e b", e=2, b=b)[:, :, :, 0, :]

            with dve.Fori(0, 4) as j:
                dve.wait_ge(S["oT_sb"], j * 2 + 1)
                for c in range(2):
                    dve.wait_ge(S["kq_ps"], j * 2 + (c + 1))
                    dve.wait_ge(S["decay_sb"], j * 5 + (2 * c + 2))
                    for e in range(4):
                        last = stt(out=dA[:, c, e, :], in0=bank(c, 4, P)[:, e // 2, :],
                                   scalar=beta[:, c, bass.ds(j * 4 + e, 1)], in1=dA[:, c, e, :], op0=ALU.mult, op1=ALU.mult)
                    last.then_inc(S["a_sb"], 1)
                    d = dQ[:, c].rearrange("p (k r) s -> p k r s", r=2)
                    V.tensor_tensor(d, over(bank(c, 4, P)[:, 2:4, :], 2, 2), d, ALU.mult).then_inc(S["qk_raw"], 1)
                dve.wait_ge(S["decay_sb"], j * 5 + 5)
                e4 = eq.rearrange("p (k r) s -> p k r s", r=2)
                V.tensor_tensor(e4, over(kqf[:, 2:4, P:T], 2, 2), e4, ALU.mult).then_inc(S["qdec_sb"], 1)

                def y_out(v, c):
                    dve.wait_ge(S["y_ps"], j * 14 + (2 * v + c + 1))
                    V.tensor_tensor(yb[:, c], bank(3 + 2 * c, 4, P), over(masks[:, v, :], 1, 4),
                                    ALU.mult).then_inc(S["y_sb"], 1)

                def z_split(q, part):
                    if part == 0:
                        dve.wait_ge(S["hi_done"], j * 2 + (U0["z"] + q + 1))
                    c4 = slice(512 * part, 512 * part + 512)
                    last = V.tensor_tensor(wlo[:, q, c4], raw[:, q, c4], whi[:, q, c4], ALU.subtract)
                    if part == 3:
                        last.then_inc(S["lo_done"], 1)

                def z_out(q):
                    dve.wait_ge(S["unit_done"], j * 2 + (U0["z"] + q + 1))
                    V.tensor_tensor(zT[:, bass.ds(j * 4 + 2 * q, 2), :], bank(6 + q, 2, T), over(rpre[:, :], 1, 2),
                                    ALU.mult).then_inc(S["bank_free"], 1)

                def update(v, c):
                    b = 1 << v
                    if v == 0:
                        dve.wait_ge(S["y_sb"], j * 14 + (c + 1))
                        V.tensor_tensor(TTr[:, c], over(ident[:, :], 1, 4), yb[:, c],
                                        ALU.subtract).then_inc(S["t_upd"], 1)
                        return
                    dve.wait_ge(S["z_ps"], j * 12 + (2 * (v - 1) + c + 1))
                    if v < LV - 1:
                        V.tensor_tensor(even(Tr[:, c], b), even(Tr[:, c], b), even(bank(c, 4, P), b), ALU.subtract)
                    V.tensor_tensor(odd(TTr[:, c], b), odd(TTr[:, c], b), odd(bank(6 + c, 4, P), b), ALU.subtract).then_inc(S["t_upd"], 1)

                y_out(0, 0)
                y_out(0, 1)
                update(0, 0)
                update(0, 1)
                for v in range(1, LV):
                    y_out(v, 0)
                    z_split(*divmod(v - 1, 4))
                    if v > 1:
                        update(v - 1, 1)
                    update(v, 0)
                    y_out(v, 1)
                update(LV - 1, 1)
                dve.wait_ge(S["u_ps"], j * 2 + 1)
                V.tensor_copy(vn[:, 0], bank(0, 4, P)).then_inc(S["vn_sb"], 1)
                z_split(1, 2)
                z_split(1, 3)
                z_out(0)
                dve.wait_ge(S["ks_ps"], j + 1)
                dve.wait_ge(S["bv_sb"], j * 2 + 2)
                for e in range(4):
                    last = stt(out=bv[:, 1, e, :], in0=bank(4, 4, P)[:, e, :], scalar=nbe[:, 1, bass.ds(j * 4 + e, 1)],
                               in1=bv[:, 1, e, :], op0=ALU.mult, op1=ALU.add)
                last.then_inc(S["r1_sb"], 1)
                dve.wait_ge(S["u_ps"], j * 2 + 2)
                V.tensor_copy(vn[:, 1], bank(1, 4, P)).then_inc(S["vn_sb"], 1)
                z_out(1)
            dve.wait_ge(S["on_root"], 1)
            V.reciprocal(hcol[:, :, :], hcol[:, :, :]).then_inc(S["hrec"], 1)
            dve.wait_ge(S["oT_sb"], 9)

            def gated_lo(s):
                dve.wait_ge(S["ohi_done"], s + 1)
                V.tensor_tensor(big[:, KF + 2 * s:KF + 2 * s + 2, :], oT[:, 2 * s:2 * s + 2, :], big[:, 2 * s:2 * s + 2, :],
                                ALU.subtract).then_inc(S["olo_done"], 1)
            for s in range(8):
                o = oT[:, 2 * s:2 * s + 2, :]
                dve.wait_ge(S["on_rows"], s + 1)
                stt(out=o, in0=o, scalar=vecs[:, ONORM:ONORM + 1], in1=bank((3, 4, 5, 6)[s % 4], 2, T), op0=ALU.mult,
                    op1=ALU.mult).then_inc(S["on_done"], 1)
                dve.wait_ge(S["on_done"], s + 1)
                dve.wait_ge(S["sz_done"], s + 1)
                V.tensor_tensor(o, o, zT[:, 2 * s:2 * s + 2, :], ALU.mult).then_inc(S["oz_done"], 1)
                if s in (2, 4):
                    split("gout", s // 2 - 1)
                if s:
                    gated_lo(s - 1)
            gated_lo(7)

            def y_out_group(name, gr, per):
                dve.wait_ge(S["unit_done"], U0[name] + per * (gr + 1))
                V.tensor_copy(y[:, 2 * gr:2 * gr + 2, :], bank(gr % 2, 2, T)).then_inc(S["bank_free"], 1)

            YN = [0]

            def post_norm(n, cols, end, lo_part, between=None):
                rstd(n)
                dve.wait_ge(S["rstd_done"], n + 1)
                dve.wait_ge(S["bank_free"], end)
                y0 = YN[0]

                def scaled(e):
                    V.tensor_tensor(y[:, 2 * e:2 * e + 2, :], y[:, 2 * e:2 * e + 2, :], over(rpost[:, :], 1, 2),
                                    ALU.mult).then_inc(S["yn_done"], 1)

                def added(e):
                    dve.wait_ge(S["yn_done"], y0 + e + 1)
                    for k in (2 * e, 2 * e + 1):
                        last = stt(out=h[:, k, :], in0=y[:, k, :], scalar=gain(cols, k), in1=h[:, k, :], op0=ALU.mult,
                                   op1=ALU.add)
                    last.then_inc(S["h_ready"], 1)
                scaled(0)
                scaled(1)
                added(0)
                scaled(2)
                added(1)
                if between:
                    between()
                lo_part(0)
                scaled(3)
                added(2)
                lo_part(1)
                added(3)
                lo_part(2)
                lo_part(3)
                YN[0] += 4

            for gr in range(4):
                for q in range(2):
                    split(*(("gout", q, gr + 1) if gr < 3 else ("fin0", q)))
                y_out_group("gout", gr, 2)
            post_norm(1, MIXPOST[0], B0["fin0"], lambda e: xlo_part(xh, xl, FFNPRE[0], e))
            rstd(2)

            def ffn_and_ple(layer, after):
                fin_, fout_, pin_, gate_ = (f"{v}{layer}" for v in ("fin", "fout", "pin", "gate"))
                dve.wait_ge(S["rstd_done"], 3 + 4 * layer)

                def hidden(i, splits):
                    splits(0)
                    times_rstd(t0[:, 0], 0, i * 2 + (U0[fin_] + 1))
                    splits(1)
                    times_rstd(t2[:, 0], 1, i * 2 + (U0[fin_] + 2))
                    dve.wait_ge(S["sg_done"], i + (11 * layer + 1))
                    dve.wait_ge(S["bank_free"], i * 2 + (B0[fin_] + 2))
                    V.tensor_tensor(t2[:, 1], t1[:, 0], t2[:, 0], ALU.mult).then_inc(S["hid_done"], 1)
                    dve.wait_ge(S["fhi_done"], i + (11 * layer + 1))
                    V.tensor_tensor(big[:, bass.ds(i * 2 + KF, 2), :], t2[:, 1], big[:, bass.ds(i * 2, 2), :],
                                    ALU.subtract).then_inc(S["flo_done"], 1)
                with dve.Fori(0, PAIRS[fin_] - 1) as i:
                    hidden(i, lambda q: split(fin_, q, i + 1))
                hidden(PAIRS[fin_] - 1, lambda q: split(fout_, q))
                dve.wait_ge(S["phi_done"], layer + 1)
                V.tensor_tensor(phl[:, 2:4, :], bank(3, 2, T), phl[:, 0:2, :], ALU.subtract).then_inc(S["plo_done"], 1)
                split(fout_, 2)
                split(fout_, 3)
                for gr in range(4):
                    for q in range(2):
                        if gr < 3:
                            split(fout_, q, 2 * gr + 2)
                        else:
                            split(pin_, q)
                    y_out_group(fout_, gr, 4)
                    if gr < 3:
                        for q in (2, 3):
                            split(fout_, q, 2 * gr + 2)
                post_norm(3 + 4 * layer, FFNPOST[layer], B0[gate_], lambda e: xlo_part(xh, xl, None, e),
                          lambda: split(gate_, 0))
                split(gate_, 1)

                def next_lo(e):
                    xlo_part(lambda k: big[:, k, :], lambda k: big[:, KD + k, :], KVN, e)
                for g in range(4):
                    if g < 2:
                        split(gate_, g, 1)
                    elif after:
                        split(after, g - 2)
                    dve.wait_ge(S["sgm_done"], g + (4 * layer + 1))
                    if g >= 2:
                        dve.wait_ge(S["h_ready"], 4 * (3 + 3 * layer) + g - 1)
                    V.tensor_tensor(t0[:, g % 2], bank(4 + g, 2, T), t1[:, g % 2], ALU.mult).then_inc(S["bank_free"], 1)
                    dve.wait_ge(S["bank_free"], B0[gate_] + g + 1)
                    hh = h[:, 2 * g:2 * g + 2, :]
                    V.tensor_tensor(hh, hh, t0[:, g % 2], ALU.add).then_inc(S["h_ready"], 1)
                    if after and g:
                        next_lo(g - 1)
                if after:
                    next_lo(3)
            ffn_and_ple(0, "kv")

            rstd(4, cols=True)
            xsplit(xh, xl, MIXPRE[1])
            dve.wait_ge(S["rstd_done"], 5)
            dve.wait_ge(S["rcol_done"], 2)
            for q in range(2):
                split("kv", q, 1)
                times_rstd(ckv[:, q], q, U0["kv"] + q + 1)
            dve.wait_ge(S["bank_free"], B0["kv"] + 2)
            block_copies(V.tensor_copy, 1, S["ablk_dve"])
            for b in range(2):
                split(*(("kv", 0, 2) if b == 0 else ("q", 0)))
                dve.wait_ge(S["unit_done"], U0["kv"] + 2 * b + 3)
                for e in range(2):
                    src = slice(64 * e, 64 * e + 64)
                    for d in range(2):
                        dst = kdup[64 * d:64 * d + 64, b].rearrange("p (t h) s -> p t h s", h=2)[:, :, e, :]
                        last = V.tensor_tensor(dst, bank(0, 2, T)[src], over(rpre[src, :], 1, 2), ALU.mult)
                last.then_inc(S["bank_free"], 1)
                split(*(("kv", 1, 2) if b == 0 else ("q", 1)))
                dve.wait_ge(S["unit_done"], U0["kv"] + 2 * b + 4)
                for a in range(TT):
                    last = V.tensor_scalar(vtk[:, b, a, :], bank(1, TT, T)[:, a, :], rcol[:, a:a + 1], None, ALU.mult)
                last.then_inc(S["bank_free"], 1)
            dve.wait_ge(S["hid_ps"], 1)
            for v in range(2):
                V.tensor_copy(cb[:, v], bank(4 + v, 2, 61)[:, :, 60]).then_inc(S["hb_sb"], 1)
            dve.wait_ge(S["gt_ps"], 1)
            for a in range(TT):
                V.tensor_scalar(gates[:, a, :], bank(7, TT, 3 * NH)[:, a, :], rcol[:, a:a + 1], None,
                                ALU.mult).then_inc(S["gt_dve"], 1)
            dve.wait_ge(S["hid_sb"], 4)
            for e in range(2):
                V.tensor_copy(hrep[:, :, e, :].rearrange("p g (r n) -> p g r n", r=NR),
                              over(hid[:, 1, e, :].rearrange("p (g n) -> p g n", g=NG), 2, NR)).then_inc(S["hrep_sb"], 1)
            for i in range(2):
                for q in range(2):
                    split(*(("q", q, 1) if i == 0 else ("wo", q)))
                    times_rstd(qT[:, 4 * i + 2 * q:4 * i + 2 * q + 2, :], q, U0["q"] + 2 * i + q + 1)
            dve.wait_ge(S["kc_ps"], 2)
            V.tensor_copy(kcd, bank(6, 60)).then_inc(S["kc_sb"], 1)
            V.tensor_copy(vrep[0:60], ps[0:60, 7, 0:256].rearrange("p (g d) -> p g d", g=NG)).then_inc(S["kc_sb"], 1)
            n_cs = [0]

            def csw(ins):
                ins.then_inc(S["cs_dve"], 1)
                n_cs[0] += 1
                dve.wait_ge(S["cs_dve"], n_cs[0])
            dve.wait_ge(S["cs_ps"], 1)
            for e in range(2):
                csw(V.tensor_tensor(cs.rearrange("p a (h e) n -> p a h e n", e=2)[:, :, :, e, :],
                                    bank(3 - e, TT, NH // 2, NC), over(cmask[:, :, :], 2, NH // 2), ALU.add))
            csf = cs.rearrange("p a h n -> p (a h) n")
            csw(V.tensor_reduce(out=cst[:, 0, :], in_=csf, axis=AX, op=ALU.max))
            csw(V.tensor_scalar(cst[:, 0, :], cst[:, 0, :], -1e25, None, ALU.max))
            csw(V.tensor_tensor(csf, csf, over(cst[:, 0, :], 2, NC), ALU.subtract))
            dve.wait_ge(S["cs_act"], 1)
            csw(V.tensor_reduce(out=cst[:, 1, :], in_=csf, axis=AX, op=ALU.add))
            csw(V.tensor_scalar(cst[:, 1, :], cst[:, 1, :], 1e-30, None, ALU.max))
            csw(V.reciprocal(cst[:, 1, :], cst[:, 1, :]))
            dve.wait_ge(S["gt_done"], 1)
            g4 = gates[:, :, :].rearrange("p a (h b) -> p a h b", b=3)
            csw(V.tensor_tensor(cst[:, 2, :].rearrange("p (a h) -> p a h", a=TT),
                                cst[:, 1, :].rearrange("p (a h) -> p a h", a=TT), g4[:, :, :, 0], ALU.mult))
            csw(V.tensor_tensor(csf, csf, over(cst[:, 2, :], 2, NC), ALU.mult))
            dve.wait_ge(S["pct_sb"], 2)
            dve.wait_ge(S["kc_sb"], 2)
            def values(gi, first):
                if not first:
                    dve.wait_ge(S["av_ps"], gi * 4)
                V.tensor_copy(vff.rearrange("p b a d -> p (b a) d"),
                              vtk.rearrange("p b a (g d) -> p (b a) g d", g=NG)[:, :, bass.ds(gi, 1), :]
                              .rearrange("p b g d -> p b (g d)")).then_inc(S["fx_dve"], 1)
                V.tensor_copy(pcf[0:60, :], pct[0:60, bass.ds(gi, 1), :].rearrange("p g q -> p (g q)")).then_inc(S["fx_dve"], 1)
                V.tensor_tensor(vz[0:60], over(vrep[0:60, bass.ds(gi, 1), :].rearrange("p g d -> p (g d)"), 1, NR),
                                over(rmask[0:60, :], 2, ND), ALU.mult).then_inc(S["fx_dve"], 1)

            def maxima(gi, r):
                dve.wait_ge(S["sc_ps"], gi * 4 + (r + 1))
                s1, s0 = bank(2 + 2 * (r % 2), 2, T), bank(3 + 2 * (r % 2), 2, P)
                V.tensor_reduce(out=hst[:, r % 2, 0, 0:2], in_=s0, axis=AX, op=ALU.max).then_inc(S["mx_dve"], 1)
                V.tensor_reduce(out=hst[:, r % 2, 0, 2:4], in_=s1, axis=AX, op=ALU.max).then_inc(S["mx_dve"], 1)
                dve.wait_ge(S["mx_dve"], gi * 12 + (3 * r + 2))
                V.tensor_scalar(hst[:, r % 2, 1, :], hst[:, r % 2, 0, :], -(ND ** -0.5), None, ALU.mult).then_inc(S["mx_dve"], 1)

            def weights(gi, r):
                for b in range(2):
                    dve.wait_ge(S["p_act"], gi * 8 + (2 * r + b + 1))
                    l = hst[:, r % 2, 2, :].rearrange("p (a b) -> p a b", a=TT)[:, :, b:b + 1]
                    V.reciprocal(l, l).then_inc(S["rl_dve"], 1)
                    dve.wait_ge(S["rl_dve"], gi * 16 + (4 * r + 2 * b + 1))
                    stt(out=l, in0=l, scalar=1e30, in1=gates[:, :, bass.ds(gi * 12 + (3 * r + 1 + b), 1)], op0=ALU.min,
                        op1=ALU.mult).then_inc(S["rl_dve"], 1)
                    dve.wait_ge(S["rl_dve"], gi * 16 + (4 * r + 2 * b + 2))
                    V.tensor_scalar(pr0[:, r % 2, b, :], pr0[:, r % 2, b, :], l[:, 0, :], None, ALU.mult)
                    V.tensor_scalar(pr1[:, r % 2, b, :], pr1[:, r % 2, b, :], l[:, 1, :], None,
                                    ALU.mult).then_inc(S["pw_dve"], 1)

            def out_lo(gi, c):
                dve.wait_ge(S["ahi"], gi * 2 + (c + 1))
                V.tensor_tensor(big[:, bass.ds(gi * 2 + (KD + c), 1), :], bank(c, 1, T),
                                big[:, bass.ds(gi * 2 + c, 1), :], ALU.subtract).then_inc(S["alo"], 1)

            def group(gi, first, last):
                weights(gi, 0)
                maxima(gi, 1)
                weights(gi, 1)
                values(gi, first)
                maxima(gi, 2)
                if not first:
                    out_lo(gi - 1, 1)
                weights(gi, 2)
                maxima(gi, 3)
                weights(gi, 3)
                out_lo(gi, 0)
                if not last:
                    maxima(gi + 1, 0)
            maxima(0, 0)
            group(0, True, False)
            with dve.Fori(1, NG - 1) as gi:
                group(gi, False, False)
            group(NG - 1, False, True)
            out_lo(NG - 1, 1)
            for i in range(2):
                for q in range(2):
                    split(*(("wo", q, 1) if i == 0 else ("fin1", q)))
                for q in range(2):
                    gr = 2 * i + q
                    dve.wait_ge(S["unit_done"], U0["wo"] + gr + 1)
                    V.tensor_copy(y[:, 2 * gr:2 * gr + 2, :], bank(q, 2, T)).then_inc(S["bank_free"], 1)
            post_norm(5, MIXPOST[1], B0["fin1"], lambda e: xlo_part(xh, xl, FFNPRE[1], e))
            rstd(6)
            ffn_and_ple(1, None)
            for a in range(TT):
                dve.wait_ge(S["out_ps"], 2 * a + 1)
                V.tensor_copy(otok[:, a, 0:512], bank(2 + 2 * a, 512)).then_inc(S["out_sb"], 1)
    return nc


_INS = ["x", "p", "mix_pre_norm", "mix_post_norm", "ffn_pre_norm", "ffn_post_norm", "gdn_w_in", "gdn_conv_w",
        "gdn_a_log", "gdn_dt_bias", "gdn_o_norm", "gdn_w_out", "kv_norm", "kv_w", "cmp_pos", "cmp_w1", "cmp_w2",
        "nsa_w_qg", "nsa_w_o", "ffn_w_in", "ffn_w_out", "ple_w_in", "ple_w_gate"]


def kernel(**inputs):
    import numpy as np
    import concourse.bacc as bacc
    from concourse.bass_utils import run_bass_kernel_spmd

    nc = bacc.Bacc("TRN2", target_bir_lowering=False, num_devices=1)
    arrays, args = {}, []
    for name in _INS:
        a = np.ascontiguousarray(inputs[name])
        arrays[f"in_{name}"] = a
        args.append(nc.dram_tensor(f"in_{name}", a.shape, mybir.dt.from_np(a.dtype), kind="ExternalInput").ap())
    out = nc.dram_tensor("out_h", inputs["x"].shape, F32, kind="ExternalOutput").ap()
    build(nc, *args, out)
    r = run_bass_kernel_spmd(nc, [arrays], core_ids=[0])
    return r.results[0]["out_h"]
```

```python
from contextlib import ExitStack

import concourse.bass as bass
from concourse import mybir

P = 128
T = 256
TT = T // P
DM = 1024
KD = DM // P
HK, HV, HD = 8, 16, 128
CONVW = (2 * HK + HV) * HD
FFN = 2816
KF = FFN // P
NH, NG, ND = 16, 4, 64
NR = NH // NG
NC = (T - 32) // 16 + 1
QK_ORDER = (4, 0, 5, 1, 6, 2, 7, 3)
UW = 256
EPS = 1e-6
NEG = -1e30
N_BA = 18
N_CST = 24
N_DCST = 24
LV = 7

F32 = mybir.dt.float32
F32R = mybir.dt.float32r
BF16 = mybir.dt.bfloat16
ACT = mybir.ActivationFunctionType
ALU = mybir.AluOpType
AX = mybir.AxisListType.X

STAGES = [("qkv", 8, 1), ("z", 4, 1), ("gout", 4, 2), ("fin0", 11, 1), ("fout0", 8, 4),
          ("pin0", 1, 0), ("gate0", 2, 1),
          ("kv", 3, 1), ("q", 2, 1), ("wo", 2, 1), ("fin1", 11, 1), ("fout1", 8, 4),
          ("pin1", 1, 0), ("gate1", 2, 1)]
ORDER = [s[0] for s in STAGES]
PAIRS = {s[0]: s[1] for s in STAGES}
U0, B0 = {}, {}
_u = _b = 0
for _n, _p, _s in STAGES:
    U0[_n], B0[_n] = _u, _b
    _u += 2 * _p
    _b += 2 * _p // _s if _s else 0
FOUT_K = (6, 5, 6, 5)


def unit_k(stage, p):
    if stage.startswith("fout"):
        return FOUT_K[p]
    if stage.startswith("pin"):
        return 4
    return 8


def build(nc, x, p, mix_pre_norm, mix_post_norm, ffn_pre_norm, ffn_post_norm, gdn_w_in, gdn_conv_w, gdn_a_log,
          gdn_dt_bias, gdn_o_norm, gdn_w_out, kv_norm, kv_w, cmp_pos, cmp_w1, cmp_w2, nsa_w_qg, nsa_w_o,
          ffn_w_in, ffn_w_out, ple_w_in, ple_w_gate, out):
    with ExitStack() as ctx:
        def sb(name, shape, dt=F32):
            return ctx.enter_context(nc.sbuf_tensor(name, shape, dt))

        def sem(name):
            return ctx.enter_context(nc.semaphore(name))

        raw = sb("w_raw", [P, 2, 8 * UW])
        whi = sb("w_hi", [P, 2, 8 * UW], F32R)
        wlo = sb("w_lo", [P, 2, 8 * UW], F32R)
        xhi = sb("x_hi", [P, KD, T], F32R)
        xlo = sb("x_lo", [P, KD, T], F32R)
        phl = sb("p_hi_lo", [P, 4, T], F32R)
        h = sb("h", [P, KD, T])
        scr = sb("scr", [P, 16, T])
        y, sq = scr[:, 0:KD, :], scr[:, KD:16, :]
        qkvT = sb("qkvT", [P, 32, T])
        rpre = sb("rstd_pre", [P, T])
        rpost = sb("rstd_post", [P, T])
        rcol = sb("rstd_col", [P, TT])
        epsc = sb("eps_cols", [P, 4])
        ident = sb("ident", [P, P])
        identb = sb("identb", [P, P], BF16)
        causb = sb("causb", [P, P], BF16)
        ones = sb("ones", [P, P])
        tri_le = sb("tri_le", [P, P])
        tri_gt = sb("tri_gt", [P, P])
        masks = sb("level_masks", [P, LV, P])
        m1t = sb("first_level_mask", [P, P])
        rows = sb("vector_rows", [P, P])
        crows = sb("conv_rows", [P, P])
        vecs = sb("vectors", [P, P])
        cw = sb("conv_cols", [P, 4, 32])
        wba = sb("w_beta_a", [P, KD, 2 * HV])
        wgt = sb("w_gates", [P, KD, 3 * NH])
        kcz = sb("cmp_keys", [P, NG, 2, NC])
        wtok = sb("w_small_split", [P, 2, KD, 5 * 16], F32R)
        tkr = sb("logit_rows", [P, T])
        dtb = sb("dt_bias_b", [P, HV])
        alog = sb("a_log_b", [P, HV])
        w2k = sb("w2k", [P, 2, 2, ND])
        w2v = sb("w2v", [P, 2, ND])
        ptok = sb("p_tok", [P, 2, TT, 256])
        gates = sb("gates", [P, TT, 3 * NH])
        small = sb("small", [P, 12, TT, HV])
        beta, gdec, einc, faft, nbe = (small[:, i] for i in range(5))
        sm = [small[:, i] for i in range(5, 12)]
        balog = sb("beta_a_logits", [P, TT, 2 * HV])
        cmask = sb("cmp_mask", [P, TT, NC])
        rmask = sb("row_masks", [P, NR])
        hcol = sb("head_rstd_cols", [P, TT, 16])
        tcol = sb("table_cols", [P, 24])
        cst = sb("cmp_stats", [P, 3, TT * NH])
        hst = sb("head_stats", [P, 2, 3, 4])
        with nc.sbuf_tensor("big", [P, 2 * KF, T], F32R) as big:
            pass
        gdn = sb("gdn", [P, 12800])

        def views(base):
            used = [0]

            def take(*shape):
                n = 1
                for v in shape:
                    n *= v
                v = base[:, used[0]:used[0] + n]
                used[0] += n
                assert used[0] <= base.shape[1], used[0]
                names = "abcd"[:len(shape)]
                return v.rearrange(f"p ({' '.join(names)}) -> p {' '.join(names)}", **dict(zip(names, shape))) \
                    if len(shape) > 1 else v
            return take

        xtok = views(gdn)(TT, DM)
        ar = views(gdn)
        pre = ar(2, 2, T + 3)
        acc = ar(2, 2, T)
        ar = views(gdn)
        dA = ar(2, 4, P)
        dQ = ar(2, 4, P)
        eq = ar(4, P)
        gtri = ar(2, 4, P)
        TTr = ar(2, 4, P)
        Tr = ar(2, 4, P)
        ktok = ar(2, 2, P)
        bv = ar(2, 4, P)
        Ss = ar(4, P)
        vn = ar(2, 4, P)
        kqf = ar(4, T)
        vf = ar(4, T)
        ATr = ar(2, 4, P)
        yb = ar(2, 4, P)
        osq = views(gdn)(16, T)
        zT = scr
        oT = qkvT[:, 16:32, :]
        pw1 = gdn[:, 4096:12288].rearrange("p (v c n) -> p v c n", v=2, c=16)
        qkvf = qkvT[:, :, :].rearrange("p a b -> p (a b)")
        ar = views(qkvf)
        t0 = ar(2, 2, T)
        t1 = ar(2, 2, T)
        t2 = ar(2, 2, T)
        ar = views(qkvf)
        kdup = ar(2, NG, T)
        vtk = ar(2, TT, T)
        ckv = ar(2, 2, T)
        ablk = ar(2, 16, 61)
        hid = ar(2, 2, 60)
        vrep = ar(NG, ND)
        cb = ar(2, 2)
        hrep = ar(NG, 2, 60)
        cs = ar(TT, NH, NC)
        qT = scr[:, 0:8, :]
        ar = views(scr[:, 8:16, :].rearrange("p a b -> p (a b)"))
        pr0 = ar(2, 2, P)
        pr1 = ar(2, 2, T)
        qf = ar(2, T)
        ar = views(gdn[:, 4096:12288])
        pct = ar(NG, T)
        kf = ar(2, T)
        vff = ar(2, TT, ND)
        pcf = ar(T)
        vz = ar(NR, ND)
        pts = ar(2, 2, 3, P)
        otok = scr[:, 0:8, :].rearrange("p (a b) t -> p a (b t)", a=TT)

        ps = ctx.enter_context(nc.psum_tensor("ps", [P, 8, 512], F32))

        def bank(b, *shape):
            n = 1
            for v in shape:
                n *= v
            v = ps[:, b, 0:n]
            names = "abcd"[:len(shape)]
            return v.rearrange(f"p ({' '.join(names)}) -> p {' '.join(names)}", **dict(zip(names, shape))) \
                if len(shape) > 1 else v

        def over(ap, axis, n):
            shape = list(ap.shape)
            shape.insert(axis, n)
            return ap.unsqueeze(axis).to_broadcast(shape)

        def gain(col, k):
            return vecs[:, col + k:col + k + 1]
        MIXPRE, MIXPOST, FFNPRE, FFNPOST, KVN, ONORM, POS = (0, 8), (16, 24), (32, 40), (48, 56), 64, 72, 96

        landed = [sem("landed0"), sem("landed1")]
        S = {}
        for name in ("wt_act wt_dve hi_done lo_done lo_pool unit_done bank_free x_in vec_in small_in cst_pool cst_dve xt_ps h_ready "
                     "at_ps at_sb x_ps tt_sb t0init tk_ps tk_sb "
                     "sq_ready stat_ps root_done rstd_done xhi_done xlo_done vec_ps vec_sb rc_ps rc_root rcol_done ba_ps ba_dve ba_act "
                     "conv_dve conv_done silu_done l2_sq l2_ps l2_root l2_done gtri_done decay_ps decay_sb kq_ps a_sb qk_raw "
                     "kqf_sb vf_sb hrec l2_rows on_rows "
                     "qk_sb qdec_sb tinit y_ps y_sb z_ps t_upd ktok_ps ktok_sb vtok_ps bv_sb u_ps vn_sb fv_sb s_ps s_sb "
                     "ks_ps r1_sb o_ps oT_sb on_sq on_ps on_root on_done cum_ps cum_act cum_dve sz_done oz_done ohi_done olo_done "
                     "yn_done yn_pool sg_done hid_done fhi_done flo_done pt_ps phi_done plo_done sgm_done "
                     "ablk_act ablk_dve pts_act out_act w1_in hid_ps hb_sb hid_sb kc_ps kc_sb "
                     "gt_ps gt_dve gt_done cs_ps cs_dve cs_act pct_ps pct_sb fx_act fx_dve "
                     "sc_ps mx_dve p_act rl_dve pw_dve ptr_ps av_ps ahi alo out_ps out_sb out_st").split():
            S[name] = sem(name)

        def block_copies(copy, v, done):
            for par in range(2):
                for e in range(2):
                    src = ckv[64 * e:64 * e + 64, v].rearrange("p t (n c r) -> p c t n r", c=8, r=2)[:, :, :, :, par]
                    dst = ablk[64 * par:64 * par + 64, v, :, 0:60].rearrange("p c (t e n) -> p c t e n", t=2, e=2)
                    for half in range(2):
                        for t in range(2):
                            last = copy(dst[:, 8 * half:8 * half + 8, t, e, :], src[:, :, t, half:half + NC], *cargs(v))
                        last.then_inc(done, 1)
            copy(ablk[:, v, :, 60], vecs[:, POS + 16 * v:POS + 16 * v + 16], *cargs(v)).then_inc(done, 1)

        def cargs(v):
            return (ACT.Copy,) if v == 0 else ()

        block = ctx.enter_context(nc.Block())

        win = gdn_w_in[0].rearrange("(k p) n -> p k n", p=P)
        wout = gdn_w_out[0].rearrange("(k p) n -> p k n", p=P)
        fin = [ffn_w_in[i].rearrange("(k p) n -> p k n", p=P) for i in range(2)]
        fout = [ffn_w_out[i].rearrange("(k p) n -> p k n", p=P) for i in range(2)]
        pin = [ple_w_in[i].rearrange("(k p) n -> p k n", p=P) for i in range(2)]
        pgt = [ple_w_gate[i].rearrange("(k p) n -> p k n", p=P) for i in range(2)]
        wkv = kv_w.rearrange("(k p) n -> p k n", p=P)
        wqg = nsa_w_qg[0].rearrange("(k p) n -> p k n", p=P)
        wwo = nsa_w_o[0].rearrange("(k p) n -> p k n", p=P)

        def source(stage, i, q):
            cols = bass.ds(i * (2 * UW) + q * UW, UW)
            one = bass.ds(i * UW, UW)
            if stage == "qkv":
                return win[:, :, cols]
            if stage == "z":
                return win[:, :, bass.ds(i * (2 * UW) + (CONVW + q * UW), UW)]
            if stage == "gout":
                return wout[:, 8 * q:8 * q + 8, one]
            if stage[:3] == "fin":
                w = fin[int(stage[3])]
                return w[:, :, one] if q == 0 else w[:, :, bass.ds(i * UW + FFN, UW)]
            if stage[:4] == "fout":
                k = sum(FOUT_K[:q])
                return fout[int(stage[4])][:, k:k + FOUT_K[q], one]
            if stage[:4] == "gate":
                return pgt[int(stage[4])][:, :, cols]
            return {"kv": wkv, "q": wqg, "wo": wwo}[stage][:, :, cols]


        @block.sync
        def _(sp):
            def load(stage, i, q):
                n = unit_k(stage, q) * UW
                if stage.startswith("pin"):
                    sp.dma_start(raw[:, q, 0:n], pin[int(stage[3])][:, q, :]).then_inc(landed[q], 16)
                    return
                sp.dma_start(raw[:, q % 2, 0:n].rearrange("p (k n) -> p k n", n=UW),
                             source(stage, i, q)).then_inc(landed[q % 2], 16)

            sp.dma_start(xtok, x[0].rearrange("(a p) d -> p a d", p=P)).then_inc(S["x_in"], 16)
            for stage in ORDER:
                per = 4 if stage.startswith("fout") else 2
                first = 0
                if stage == "qkv":
                    first = 1
                    for q in range(per):
                        load(stage, 0, q)
                    for i in range(1, PAIRS[stage]):
                        for q in range(per):
                            u = i * per + q
                            sp.wait_ge(S["lo_done"], u - 1)
                            if u >= 4:
                                sp.wait_ge(S["lo_pool"], u - 3)
                            load(stage, i, q)
                    continue
                with sp.Fori(first, PAIRS[stage] * 2 // per) as i:
                    for q in range(per):
                        sp.wait_ge(S["lo_done"], i * per + (U0[stage] + q - 1))
                        if stage == "z":
                            sp.wait_ge(S["lo_pool"], 2 * PAIRS["qkv"] - 2)
                        load(stage, i, q)
            for a in range(TT):
                sp.wait_ge(S["out_sb"], a + 1)
                sp.wait_ge(S["out_act"], a + 1)
                sp.dma_start(out[0, a * P:(a + 1) * P, :], otok[:, a, :]).then_inc(S["out_st"], 16)
            sp.wait_ge(S["out_st"], 16 * TT)

        @block.gpsimd
        def _(pool):
            g = nc.gpsimd
            pool.dma_start(wba[:, :, :], win[:, :, 6144:6176]).then_inc(S["small_in"], 16)
            pool.dma_start(dtb[:, :], gdn_dt_bias[0].partition_broadcast(P)).then_inc(S["small_in"], 16)
            pool.dma_start(alog[:, :], gdn_a_log[0].partition_broadcast(P)).then_inc(S["small_in"], 16)
            pool.dma_start(wgt[:, :, :], wqg[:, :, 1024:1072]).then_inc(S["small_in"], 16)
            for d in range(2):
                pool.dma_start(w2k[:, :, d, :], cmp_w2[0].rearrange("(c p) n -> p c n", p=P)).then_inc(S["small_in"], 16)
            pool.dma_start(w2v[:, :, :], cmp_w2[1].rearrange("(c p) n -> p c n", p=P)).then_inc(S["small_in"], 16)
            for i in range(2):
                pool.dma_start(ptok[:, i], p[i, 0].rearrange("(a p) d -> p a d", p=P)).then_inc(S["small_in"], 16)

            n = [0]

            def sel(dst, src, op, fill, base, pattern, cm):
                if n[0]:
                    pool.wait_ge(S["cst_pool"], n[0])
                g.affine_select(out=dst, in_=src, compare_op=op, fill=fill, base=base, pattern=pattern,
                                channel_multiplier=cm).then_inc(S["cst_pool"], 1)
                n[0] += 1
            pool.wait_ge(S["cst_dve"], N_DCST)
            sel(ident[:, :], ident[:, :], ALU.not_equal, 1.0, 0, [[-1, P]], 1)
            sel(tri_le[:, :], ones[:, :], ALU.is_ge, 0.0, 0, [[1, P]], -1)
            sel(tri_gt[:, :], ones[:, :], ALU.is_gt, 0.0, 0, [[-1, P]], 1)
            sel(identb[:, :], ident[:, :], ALU.is_ge, 0.0, 0, [[0, P]], 0)
            sel(causb[:, :], causb[:, :], ALU.is_ge, NEG, 0, [[-1, P]], 1)
            sel(cmask[:, :, :], cmask[:, :, :], ALU.is_ge, NEG, -31, [[P, TT], [-16, NC]], 1)
            for v in range(LV):
                b = 1 << v
                m = masks[:, v, :].rearrange("p (m e b) -> p m e b", e=2, b=b)[:, :, 0, :]
                sel(m, m, ALU.is_ge, 0.0, -b, [[-2 * b, 64 // b], [0, b]], 1)
                sel(m, m, ALU.is_ge, 0.0, 2 * b - 1, [[2 * b, 64 // b], [0, b]], -1)
            m1 = m1t[:, :].rearrange("p (m e) -> p m e", e=2)
            sel(m1, m1, ALU.is_equal, 0.0, -1, [[-2, 64], [0, 2]], 1)
            sel(m1, m1, ALU.is_equal, 0.0, 0, [[0, 64], [1, 2]], 0)
            sel(rmask[:, :], rmask[:, :], ALU.is_ge, 0.0, 0, [[-NC, NR]], 1)
            sel(rmask[:, :], rmask[:, :], ALU.is_ge, 0.0, NC - 1, [[NC, NR]], -1)
            assert n[0] == N_CST

            with pool.Fori(1, PAIRS["qkv"]) as i:
                for q in range(2):
                    pool.wait_ge(S["hi_done"], i * 2 + (q + 1))
                    g.tensor_tensor(wlo[:, q, 4 * UW:], raw[:, q, 4 * UW:], whi[:, q, 4 * UW:],
                                    ALU.subtract).then_inc(S["lo_pool"], 1)
            pool.wait_ge(S["ba_dve"], N_BA)
            pool.wait_ge(S["conv_done"], 16)
            with pool.Fori(0, 4) as j:
                pool.wait_ge(S["ktok_ps"], j + 1)
                for c in range(2):
                    g.tensor_tensor(gtri[:, c], over(gdec[:, c, bass.ds(j * 4, 4)], 2, P), over(tri_le[:, :], 1, 4),
                                    ALU.mult).then_inc(S["gtri_done"], 1)
                pool.wait_ge(S["a_sb"], j * 2 + 2)
                g.tensor_tensor(Tr[:, 1], dA[:, 1], over(m1t[:, :], 1, 4), ALU.mult).then_inc(S["tinit"], 1)
                pool.wait_ge(S["tinit"], j * 2 + 1)
                g.tensor_tensor(Tr[:, 1], over(ident[:, :], 1, 4), Tr[:, 1], ALU.subtract).then_inc(S["tinit"], 1)
                for c in range(2):
                    pool.wait_ge(S["qk_raw"], j * 2 + (c + 1))
                    g.tensor_tensor(dQ[:, c], dQ[:, c], over(tri_le[:, :], 1, 4), ALU.mult).then_inc(S["qk_sb"], 1)
            for s in range(8):
                pool.wait_ge(S["ohi_done"], s + 1)
                g.tensor_tensor(big[:, KF + 2 * s:KF + 2 * s + 2, :], oT[:, 2 * s:2 * s + 2, :], big[:, 2 * s:2 * s + 2, :],
                                ALU.subtract).then_inc(S["olo_done"], 1)

            def scale_y(n, end):
                pool.wait_ge(S["rstd_done"], n + 1)
                pool.wait_ge(S["bank_free"], end)
                for e in (1, 2, 3):
                    g.tensor_tensor(y[:, 2 * e:2 * e + 2, :], y[:, 2 * e:2 * e + 2, :], over(rpost[:, :], 1, 2),
                                    ALU.mult).then_inc(S["yn_pool"], 1)

            scale_y(1, B0["fin0"])
            pool.wait_ge(S["unit_done"], U0["pin0"])
            pool.wait_ge(S["plo_done"], 1)
            for v in range(2):
                pool.dma_start(pw1[:, v], cmp_w1[v].rearrange("(c p) n -> p c n", p=P)).then_inc(S["w1_in"], 16)
            scale_y(3, B0["gate0"])
            scale_y(5, B0["fin1"])
            scale_y(7, B0["gate1"])

        @block.tensor
        def _(pe):
            mm = nc.tensor.matmul

            def transpose(o, i):
                return nc.tensor.transpose(o, i, ident[:, :])

            def stage_unit(name, q, xh, xl, i, bank_wait=True, operand=None):
                pe.wait_ge(S["lo_done"], i * 2 + (U0[name] + q + 1))
                if name == "qkv" and not (isinstance(i, int) and i == 0):
                    pe.wait_ge(S["lo_pool"], i * 2 + (q - 1))
                if bank_wait:
                    pe.wait_ge(S["bank_free"], i * 2 + (B0[name] + q - 1))

                def products(tile, k, first, end):
                    o, col = bank(q, 2, T)[:, tile, :], k * UW + tile * P
                    mm(o, whi[:, q, col:col + P], xh(k), start=first, stop=False, skip_group_check=True)
                    mm(o, whi[:, q, col:col + P], xl(k), start=False, stop=False, skip_group_check=True)
                    return mm(o, wlo[:, q, col:col + P], xh(k), start=False, stop=end, skip_group_check=True)
                if operand is None:
                    for tile in range(2):
                        for k in range(KD):
                            last = products(tile, k, k == 0, k == KD - 1)
                else:
                    for k in range(KD):
                        operand(k)
                        for tile in range(2):
                            last = products(tile, k, k == 0 and tile == 0, k == KD - 1)
                last.then_inc(S["unit_done"], 1)

            def stage_pair(name, xh, xl, i, bank_wait=True):
                for q in range(2):
                    stage_unit(name, q, xh, xl, i, bank_wait)

            def values_unit(name, i):
                pe.wait_ge(S["lo_done"], i * 2 + (U0[name] + 2))
                pe.wait_ge(S["bank_free"], i * 2 + B0[name])
                for a in range(TT):
                    o = bank(1, TT, T)[:, a, :]
                    tok = slice(a * P, (a + 1) * P)
                    for k in range(KD):
                        w_h, w_l = whi[:, 1, k * UW:(k + 1) * UW], wlo[:, 1, k * UW:(k + 1) * UW]
                        mm(o, big[:, k, tok], w_h, start=k == 0, stop=False)
                        mm(o, big[:, k, tok], w_l, start=False, stop=False)
                        last = mm(o, big[:, KD + k, tok], w_h, start=False, stop=k == KD - 1)
                last.then_inc(S["unit_done"], 1)

            def keys_unit(name, i):
                pe.wait_ge(S["lo_done"], i * 2 + (U0[name] + 1))
                pe.wait_ge(S["bank_free"], i * 2 + (B0[name] - 1))
                for tile in range(2):
                    o = bank(0, 2, T)[:, tile, :]
                    for k in range(KD):
                        col = k * UW + tile * P
                        mm(o, whi[:, 0, col:col + P], big[:, k, :], start=k == 0, stop=False)
                        mm(o, whi[:, 0, col:col + P], big[:, KD + k, :], start=False, stop=False)
                        last = mm(o, wlo[:, 0, col:col + P], big[:, k, :], start=False, stop=k == KD - 1)
                last.then_inc(S["unit_done"], 1)

            def x_hi(k):
                return xhi[:, k, :]

            def x_lo(k):
                return xlo[:, k, :]

            def bighi(k):
                return big[:, k, :]

            def biglo(k):
                return big[:, KF + k, :]

            def biglo8(k):
                return big[:, KD + k, :]

            def stats_part(n, e):
                pe.wait_ge(S["sq_ready"], 4 * n + e + 1)
                if n and e == 0:
                    pe.wait_ge(S["root_done"], n)
                for k in (2 * e, 2 * e + 1):
                    last = mm(bank(2, T), ones[:, :], sq[:, k, :], start=(k == 0), stop=(k == KD - 1),
                              skip_group_check=True)
                if e == 3:
                    last.then_inc(S["stat_ps"], 1)

            def stats(n, cols=False):
                for e in range(4):
                    stats_part(n, e)
                if cols:
                    for a in range(TT):
                        for k in range(KD):
                            last = mm(bank(3, TT)[:, a:a + 1], sq[:, k, a * P:(a + 1) * P], ones[:, 0:1],
                                      start=(k == 0), stop=(k == KD - 1))
                    last.then_inc(S["rc_ps"], 1)

            def accumulating(name, ks, operand, n):
                per = len(ks)
                for grp in range(4):
                    for q in range(per):
                        pe.wait_ge(S["lo_done"], U0[name] + grp * per + q + 1)
                        if q == 0:
                            pe.wait_ge(S["bank_free"], B0[name] + grp - 1)
                        if q == 1 and grp:
                            stats_part(n, grp - 1)
                        k0 = sum(ks[:q])
                        for k in range(ks[q]):
                            if grp == 0:
                                operand(k0 + k)
                            for tile in range(2):
                                o = bank(grp % 2, 2, T)[:, tile, :]
                                col = k * UW + tile * P
                                f = q == 0 and k == 0 and tile == 0
                                e = q == per - 1 and k == ks[q] - 1
                                w_h, w_l = whi[:, q % 2, col:col + P], wlo[:, q % 2, col:col + P]
                                mm(o, w_h, bighi(k0 + k), start=f, stop=False, skip_group_check=True)
                                mm(o, w_h, biglo(k0 + k), start=False, stop=False, skip_group_check=True)
                                last = mm(o, w_l, bighi(k0 + k), start=False, stop=e, skip_group_check=True)
                        last.then_inc(S["unit_done"], 1)

            def logit_rows(c0, n, b, hi_k, lo_k):
                o, cols = ps[0:n, b, 0:T], slice(c0, c0 + n)
                for k in range(KD):
                    mm(o, wtok[:, 0, k, cols], hi_k(k), start=k == 0, stop=False)
                    mm(o, wtok[:, 0, k, cols], lo_k(k), start=False, stop=False)
                    last = mm(o, wtok[:, 1, k, cols], hi_k(k), start=False, stop=k == KD - 1)
                last.then_inc(S["tk_ps"], 1)

            def logit_cols(n, b, count, done):
                pe.wait_ge(S["tk_sb"], count)
                for a in range(TT):
                    last = nc.tensor.transpose(bank(b, TT, n)[:, a, :], tkr[0:n, a * P:(a + 1) * P], ident[0:n, 0:n])
                last.then_inc(done, 1)

            pe.wait_ge(S["cst_pool"], 1)
            pe.wait_ge(S["x_in"], 16)
            for k in range(KD):
                for a in range(TT):
                    last = transpose(bank(4 + k // 2, 2, T)[:, k % 2, a * P:(a + 1) * P], xtok[:, a, k * P:(k + 1) * P])
                if k % 2:
                    last.then_inc(S["xt_ps"], 1)
            pe.wait_ge(S["vec_in"], 16 * 8)
            transpose(bank(3, 4, P)[:, 0, :], rows[:, :])
            transpose(bank(3, 4, P)[:, 1, :], crows[:, :]).then_inc(S["vec_ps"], 1)
            pe.wait_ge(S["vec_sb"], 2)
            stage_unit("qkv", 0, x_hi, x_lo, 0, False, operand=lambda k: pe.wait_ge(S["xlo_done"], k + 1))
            stats(0, cols=True)
            stage_unit("qkv", 1, x_hi, x_lo, 0, False)
            pe.wait_ge(S["wt_dve"], 2)
            pe.wait_ge(S["h_ready"], 4)
            logit_rows(0, 2 * HV, 4, x_hi, x_lo)
            stage_pair("qkv", x_hi, x_lo, 1)
            logit_cols(2 * HV, 4, 1, S["ba_ps"])
            def head_sums(src, ready, done):
                for s in range(8):
                    pe.wait_ge(ready, s + 1)
                    for hd in (2 * s, 2 * s + 1):
                        for a in range(TT):
                            last = mm(bank(2, TT, 16)[:, a, hd:hd + 1], src[:, hd, a * P:(a + 1) * P], ones[:, 0:1],
                                      start=True, stop=True)
                last.then_inc(done, 1)

            def head_rows(order, ready, freed, done):
                pe.wait_ge(ready, 1)
                for n, s in enumerate(order):
                    if n >= 4:
                        pe.wait_ge(freed, n - 3)
                    for e in range(2):
                        for a in range(TT):
                            last = mm(bank((3, 4, 5, 6)[n % 4], 2, T)[:, e, a * P:(a + 1) * P],
                                      hcol[:, a, 2 * s + e:2 * s + e + 1].to_broadcast([P, P]), ident[:, :],
                                      start=True, stop=True)
                    last.then_inc(done, 1)

            with pe.Fori(2, 5) as i:
                stage_pair("qkv", x_hi, x_lo, i)
            pe.wait_ge(S["root_done"], 1)
            head_sums(scr, S["l2_sq"], S["l2_ps"])
            with pe.Fori(5, PAIRS["qkv"]) as i:
                stage_pair("qkv", x_hi, x_lo, i)
            pe.wait_ge(S["ba_dve"], N_BA)
            pe.wait_ge(S["cst_pool"], N_CST)
            gflat = gdec.rearrange("p a h -> p (a h)")
            mm(bank(7, 2, 32)[:, 0, :], tri_le[:, :], gflat, start=True, stop=True).then_inc(S["ktok_ps"], 1)
            mm(bank(7, 2, 32)[:, 1, :], tri_gt[:, :], gflat, start=True, stop=True).then_inc(S["cum_ps"], 1)

            head_rows(QK_ORDER, S["hrec"], S["l2_done"], S["l2_rows"])

            pe.wait_ge(S["l2_done"], 8)
            pe.wait_ge(S["cum_act"], 2)
            with pe.Fori(0, 4) as j:
                pe.wait_ge(S["bank_free"], j * 2 + B0["z"])
                pe.wait_ge(S["oT_sb"], j * 2 + 1)
                pe.wait_ge(S["kqf_sb"], j * 2 + 2)
                for c in range(2):
                    tok = slice(c * P, (c + 1) * P)
                    for i in range(2):
                        mm(bank(c, 4, P)[:, i, :], kqf[:, i, tok], kqf[:, i, tok], start=True, stop=True)
                        last = mm(bank(c, 4, P)[:, 2 + i, :], kqf[:, i, tok], kqf[:, 2 + i, tok], start=True, stop=True)
                    last.then_inc(S["kq_ps"], 1)
                for c in range(2):
                    pe.wait_ge(S["gtri_done"], j * 2 + (c + 1))
                    mm(bank(2 + 2 * c, 4, P), tri_gt[:, :], gtri[:, c], start=True, stop=True).then_inc(S["decay_ps"], 1)
                    for e in range(4):
                        last = mm(bank(3 + 2 * c, 4, P)[:, e, :], gtri[:, c, e, :], tri_gt[:, :], start=True, stop=True)
                    last.then_inc(S["decay_ps"], 1)
                mm(bank(6, 4, P), ones[:, :], gtri[:, 1], start=True, stop=True).then_inc(S["decay_ps"], 1)
                for c in range(2):
                    for i in range(2):
                        last = transpose(bank(7, 2, 2, P)[:, c, i, :], kqf[:, i, c * P:(c + 1) * P])
                last.then_inc(S["ktok_ps"], 1)
                pe.wait_ge(S["vf_sb"], j + 1)
                for c in range(2):
                    pe.wait_ge(S["decay_sb"], j * 5 + (2 * c + 1))
                    for e in range(4):
                        last = transpose(bank(2 + 2 * c, 4, P)[:, e, :], vf[:, e, c * P:(c + 1) * P])
                    last.then_inc(S["vtok_ps"], 1)

                def a_turned(c):
                    pe.wait_ge(S["a_sb"], j * 2 + (c + 1))
                    pe.wait_ge(S["qk_raw"], j * 2 + (c + 1))
                    for e in range(4):
                        last = transpose(bank(c, 4, P)[:, e, :], dA[:, c, e, :])
                    last.then_inc(S["at_ps"], 1)

                def y_products(v, c):
                    if v == 1:
                        pe.wait_ge(S["at_sb"], j * 2 + (c + 1))
                        pe.wait_ge(S["decay_sb"], j * 5 + (2 * c + 2))
                    else:
                        pe.wait_ge(S["t_upd"], j * 12 + (2 * (v - 2) + c + 1))
                    for e in range(4):
                        last = mm(bank(3 + 2 * c, 4, P)[:, e, :], ATr[:, c, e, :], Tr[:, c, e, :], start=True, stop=True)
                    last.then_inc(S["y_ps"], 1)

                def z_products(v, c):
                    pe.wait_ge(S["y_sb"], j * 12 + (2 * (v - 1) + c + 1))
                    pe.wait_ge(S["tt_sb"], j * 12 + (2 * (v - 1) + c + 1))
                    for e in range(4):
                        if v < LV - 1:
                            l_, r_ = TTr[:, c, e, :], yb[:, c, e, :]
                        else:
                            l_, r_ = yb[:, c, e, :], TTr[:, c, e, :]
                        last = mm(bank(6 + c, 4, P)[:, e, :], l_, r_, start=True, stop=True)
                    last.then_inc(S["z_ps"], 1)

                def x_turned(v, c):
                    if v == 0:
                        pe.wait_ge(S["t0init"] if c == 0 else S["tinit"], j * 2 + 2)
                        if c == 0:
                            pe.wait_ge(S["decay_sb"], j * 5 + 5)
                        else:
                            pe.wait_ge(S["ktok_sb"], j + 1)
                    else:
                        pe.wait_ge(S["t_upd"], j * 12 + (2 * (v - 1) + c + 1))
                    for e in range(4):
                        last = transpose(bank(c if v else 6 + c, 4, P)[:, e, :], Tr[:, c, e, :])
                    last.then_inc(S["x_ps"], 1)

                def z_tile(q, tile):
                    if tile == 0:
                        pe.wait_ge(S["lo_done"], j * 2 + (U0["z"] + q + 1))
                    o = bank(6 + q, 2, T)[:, tile, :]
                    for k in range(KD):
                        col = k * UW + tile * P
                        mm(o, whi[:, q, col:col + P], xhi[:, k, :], start=k == 0, stop=False)
                        mm(o, whi[:, q, col:col + P], xlo[:, k, :], start=False, stop=False)
                        last = mm(o, wlo[:, q, col:col + P], xhi[:, k, :], start=False, stop=k == KD - 1)
                    if tile == 1:
                        last.then_inc(S["unit_done"], 1)

                a_turned(0)
                x_turned(0, 0)
                a_turned(1)
                y_products(1, 0)
                x_turned(0, 1)
                z_products(1, 0)
                y_products(1, 1)
                for v in range(2, LV):
                    y_products(v, 0)
                    x_turned(v - 1, 0)
                    z_products(v - 1, 1)
                    z_products(v, 0)
                    y_products(v, 1)
                    x_turned(v - 1, 1)
                z_products(LV - 1, 1)
                pe.wait_ge(S["t_upd"], j * 12 + 11)
                pe.wait_ge(S["bv_sb"], j * 2 + 1)
                pe.wait_ge(S["qk_raw"], j * 2 + 1)
                for e in range(4):
                    last = mm(bank(0, 4, P)[:, e, :], TTr[:, 0, e, :], bv[:, 0, e, :], start=True, stop=True)
                last.then_inc(S["u_ps"], 1)
                z_tile(0, 0)
                pe.wait_ge(S["fv_sb"], j + 1)
                pe.wait_ge(S["ktok_sb"], j + 1)
                for e in range(4):
                    last = mm(bank(2, 4, P)[:, e, :], ktok[:, 0, e // 2, :], bv[:, 0, e, :], start=True, stop=True)
                last.then_inc(S["s_ps"], 1)
                pe.wait_ge(S["vn_sb"], j * 2 + 1)
                pe.wait_ge(S["qk_sb"], j * 2 + 1)
                for e in range(4):
                    last = mm(bank(3, 4, P)[:, e, :], vn[:, 0, e, :], dQ[:, 0, e, :], start=True, stop=True)
                last.then_inc(S["o_ps"], 1)
                pe.wait_ge(S["s_sb"], j + 1)
                pe.wait_ge(S["bv_sb"], j * 2 + 2)
                for e in range(4):
                    last = mm(bank(4, 4, P)[:, e, :], kqf[:, e // 2, P:T], Ss[:, e, :], start=True, stop=True)
                last.then_inc(S["ks_ps"], 1)
                z_tile(0, 1)
                pe.wait_ge(S["r1_sb"], j + 1)
                pe.wait_ge(S["t_upd"], j * 12 + 12)
                for e in range(4):
                    last = mm(bank(1, 4, P)[:, e, :], TTr[:, 1, e, :], bv[:, 1, e, :], start=True, stop=True)
                last.then_inc(S["u_ps"], 1)
                z_tile(1, 0)
                pe.wait_ge(S["vn_sb"], j * 2 + 2)
                pe.wait_ge(S["qk_sb"], j * 2 + 2)
                pe.wait_ge(S["qdec_sb"], j + 1)
                for e in range(4):
                    mm(bank(5, 4, P)[:, e, :], Ss[:, e, :], eq[:, e, :], start=True, stop=False)
                    last = mm(bank(5, 4, P)[:, e, :], vn[:, 1, e, :], dQ[:, 1, e, :], start=False, stop=True)
                last.then_inc(S["o_ps"], 1)
                z_tile(1, 1)
            pe.wait_ge(S["oT_sb"], 9)
            head_sums(osq, S["on_sq"], S["on_ps"])
            pe.wait_ge(S["bank_free"], B0["gout"])
            pe.wait_ge(S["hrec"], 2)
            head_rows(range(8), S["hrec"], S["on_done"], S["on_rows"])
            accumulating("gout", (8, 8), lambda k: pe.wait_ge(S["olo_done"], k // 2 + 1) if k % 2 == 0 else None, 1)
            stats_part(1, 3)

            def ffn_and_ple(layer):
                n = 2 + 4 * layer
                fin_, fout_, pin_, gate_ = (f"{v}{layer}" for v in ("fin", "fout", "pin", "gate"))
                stage_unit(fin_, 0, x_hi, x_lo, 0, operand=lambda k: pe.wait_ge(S["xlo_done"], 8 * (1 + 4 * layer) + k + 1))
                stats(n)
                stage_unit(fin_, 1, x_hi, x_lo, 0)
                with pe.Fori(1, PAIRS[fin_]) as i:
                    stage_pair(fin_, x_hi, x_lo, i)
                for k in range(2):
                    for a in range(TT):
                        last = transpose(bank(3, 2, T)[:, k, a * P:(a + 1) * P], ptok[:, layer, a, k * P:(k + 1) * P])
                last.then_inc(S["pt_ps"], 1)
                accumulating(fout_, FOUT_K, lambda k: pe.wait_ge(S["flo_done"], 11 * layer + k // 2 + 1)
                             if k % 2 == 0 else None, n + 1)

                def embeddings(q, groups):
                    for g in groups:
                        for tile in range(2):
                            o, col = bank(4 + g, 2, T)[:, tile, :], g * UW + tile * P
                            f = q == 0 and tile == 0
                            mm(o, whi[:, q, col:col + P], phl[:, q, :], start=f, stop=False, skip_group_check=True)
                            mm(o, whi[:, q, col:col + P], phl[:, 2 + q, :], start=False, stop=False, skip_group_check=True)
                            last = mm(o, wlo[:, q, col:col + P], phl[:, q, :], start=False, stop=q == 1,
                                      skip_group_check=True)
                    return last
                pe.wait_ge(S["plo_done"], layer + 1)
                pe.wait_ge(S["lo_done"], U0[pin_] + 1)
                embeddings(0, (0, 1))
                stats_part(n + 1, 3)
                embeddings(0, (2, 3)).then_inc(S["unit_done"], 1)
                pe.wait_ge(S["lo_done"], U0[pin_] + 2)
                embeddings(1, range(4)).then_inc(S["unit_done"], 1)
                stage_unit(gate_, 0, x_hi, x_lo, 0, operand=lambda k: pe.wait_ge(S["xlo_done"], 8 * (2 + 4 * layer) + k + 1))
                stage_unit(gate_, 1, x_hi, x_lo, 0)
                stage_pair(gate_, x_hi, x_lo, 1)

            ffn_and_ple(0)

            stage_unit("kv", 0, bighi, biglo8, 0, operand=lambda k: pe.wait_ge(S["xlo_done"], 8 * 3 + k + 1))
            stats(4, cols=True)
            stage_unit("kv", 1, bighi, biglo8, 0)
            for i in (1, 2):
                keys_unit("kv", i)
                values_unit("kv", i)
            pe.wait_ge(S["w1_in"], 32)
            pe.wait_ge(S["ablk_act"], 9)
            pe.wait_ge(S["ablk_dve"], 9)
            for v in range(2):
                for e in range(2):
                    for c in range(16):
                        last = mm(bank(4 + v, 2, 61)[:, e, :], pw1[:, v, c, e * P:(e + 1) * P], ablk[:, v, c, :],
                                  start=c == 0, stop=c == 15)
            last.then_inc(S["hid_ps"], 1)
            pe.wait_ge(S["xlo_done"], 8 * 5)
            logit_rows(2 * HV, 3 * NH, 7, x_hi, x_lo)
            stage_pair("q", x_hi, x_lo, 0)
            logit_cols(3 * NH, 7, 2, S["gt_ps"])
            stage_unit("q", 0, x_hi, x_lo, 1)
            pe.wait_ge(S["hid_sb"], 4)
            for e in range(2):
                last = mm(bank(6, 60), w2k[:, e].rearrange("p d n -> p (d n)"), hid[:, 0, e, :], start=e == 0, stop=e == 1)
            last.then_inc(S["kc_ps"], 1)
            pe.wait_ge(S["gt_dve"], 2)
            for gr in range(NG):
                for e in range(2):
                    last = mm(ps[0:60, 7, gr * ND:(gr + 1) * ND],
                              hrep[:, gr, e, :], w2v[:, e, :], start=e == 0, stop=e == 1)
            last.then_inc(S["kc_ps"], 1)
            stage_unit("q", 1, x_hi, x_lo, 1)
            pe.wait_ge(S["kc_sb"], 2)
            pe.wait_ge(S["bank_free"], B0["wo"])
            def scores(gi, r, skip):
                half = slice(64 * (r % 2), 64 * (r % 2) + 64)
                if r == 0:
                    pe.wait_ge(S["fx_act"], gi * 2 + 2)
                if not skip:
                    pe.wait_ge(S["p_act"], gi * 8 + (2 * r - 2))
                s1, s0 = bank(2 + 2 * (r % 2), 2, T), bank(3 + 2 * (r % 2), 2, P)
                for b in range(2):
                    mm(s0[:, b, :], qf[half, r // 2, 0:P], kf[half, b, 0:P], start=b == 0, stop=False,
                       skip_group_check=True)
                mm(s0, identb[:, :], over(causb[:, :], 1, 2), start=False, stop=True, skip_group_check=True)
                for b in range(2):
                    mm(s1[:, b, :], qf[half, r // 2, P:T], kf[half, b, :], start=b == 0, stop=False,
                       skip_group_check=True)
                mm(s1[:, :, P:T], identb[:, :], over(causb[:, :], 1, 2), start=False, stop=True,
                   skip_group_check=True).then_inc(S["sc_ps"], 1)

            for a in range(TT):
                for m in range(NH // 2):
                    last = mm(bank(2, TT, NH // 2, 2 * NC)[:, a, m, :], qT[:, m, a * P:(a + 1) * P],
                              kcz[:, m // 2].rearrange("p e n -> p (e n)"), start=True, stop=True)
            last.then_inc(S["cs_ps"], 1)
            pe.wait_ge(S["cs_dve"], 1)
            scores(0, 0, True)
            pe.wait_ge(S["cs_dve"], 9)
            for gr in range(NG):
                for a in range(TT):
                    last = transpose(bank(6 + gr // 2, 2, T)[0:60, gr % 2, a * P:(a + 1) * P],
                                     cs[:, a, NR * gr:NR * gr + NR, :].rearrange("p h n -> p (h n)"))
            last.then_inc(S["pct_ps"], 1)
            pe.wait_ge(S["pct_sb"], 2)
            def turned(gi, r, skip):
                for b in range(2):
                    pe.wait_ge(S["pw_dve"], gi * 8 + (2 * r + b + 1))
                    if not skip:
                        pe.wait_ge(S["pts_act"], gi * 8 + (2 * r + b - 1))
                    transpose(bank(6 + b, 3, P)[:, 0, :], pr0[:, r % 2, b, :])
                    for s in range(2):
                        last = transpose(bank(6 + b, 3, P)[:, 1 + s, :], pr1[:, r % 2, b, s * P:(s + 1) * P])
                    last.then_inc(S["ptr_ps"], 1)

            def output(gi, r, first):
                pe.wait_ge(S["pts_act"], gi * 8 + (2 * r + 2))
                if r == 0:
                    pe.wait_ge(S["fx_dve"], gi * 3 + 3)
                if r % 2 == 0 and not first:
                    pe.wait_ge(S["alo"], gi * 2 + (r // 2 - 1))
                o = ps[64 * (r % 2):64 * (r % 2) + 64, r // 2, 0:T]
                for b in range(2):
                    mm(o, vff[:, b, 0, :], pts[:, r % 2, b, 0:2, :].rearrange("p s q -> p (s q)"), start=b == 0,
                       stop=False, skip_group_check=True)
                    mm(o[:, P:T], vff[:, b, 1, :], pts[:, r % 2, b, 2, :], start=False, stop=False,
                       skip_group_check=True)
                last = mm(o, vz[0:60, r, :], pcf[0:60, :], start=False, stop=True, skip_group_check=True)
                last.then_inc(S["av_ps"], 1)

            def group(gi, first, last):
                scores(gi, 1, first)
                turned(gi, 0, first)
                if not first:
                    output(gi - 1, 3, False)
                for r in (2, 3):
                    scores(gi, r, False)
                    turned(gi, r - 1, False)
                    output(gi, r - 2, first)
                if not last:
                    scores(gi + 1, 0, False)
                turned(gi, 3, False)
                output(gi, 2, first)
            group(0, True, False)
            with pe.Fori(1, NG - 1) as gi:
                group(gi, False, False)
            group(NG - 1, False, True)
            output(NG - 1, 3, False)
            pe.wait_ge(S["alo"], 8)
            for i in range(2):
                for q in range(2):
                    stage_unit("wo", q, bighi, biglo8, i)
                    if i or q:
                        stats_part(5, 2 * i + q - 1)
            stats_part(5, 3)
            ffn_and_ple(1)
            pe.wait_ge(S["h_ready"], 28)
            for a in range(TT):
                for e in range(2):
                    for k in range(4):
                        last = transpose(bank(2 + 2 * a + e, 4, P)[:, k, :], h[:, 4 * e + k, a * P:(a + 1) * P])
                    last.then_inc(S["out_ps"], 1)

        @block.scalar
        def _(act):
            A = nc.scalar.activation

            n_tbl = [0]

            def table(func):
                A(tcol[:, n_tbl[0]:n_tbl[0] + 1], epsc[:, 0:1], func)
                n_tbl[0] += 1

            def split(stage, q, i=0):
                u = i * 2 + (U0[stage] + q)
                n = unit_k(stage, q) * UW
                act.wait_ge(landed[q % 2], i * 16 + (8 * U0[stage] + 16 * (q // 2 + 1)))
                if not isinstance(u, int) or u >= 2:
                    act.wait_ge(S["unit_done"], u - 1)
                A(whi[:, q % 2, 0:n], raw[:, q % 2, 0:n], ACT.Copy).then_inc(S["hi_done"], 1)

            act.wait_ge(S["cst_dve"], 1)
            act.dma_start(rows[0:16, :], mix_pre_norm.rearrange("a (k p) -> (a k) p", p=P)).then_inc(S["vec_in"], 16)
            act.dma_start(rows[16:32, :], mix_post_norm.rearrange("a (k p) -> (a k) p", p=P)).then_inc(S["vec_in"], 16)
            act.dma_start(rows[32:48, :], ffn_pre_norm.rearrange("a (k p) -> (a k) p", p=P)).then_inc(S["vec_in"], 16)
            act.dma_start(rows[48:64, :], ffn_post_norm.rearrange("a (k p) -> (a k) p", p=P)).then_inc(S["vec_in"], 16)
            act.dma_start(rows[64:72, :], kv_norm.rearrange("(k p) -> k p", p=P)).then_inc(S["vec_in"], 16)
            act.dma_start(rows[72:73, :], gdn_o_norm).then_inc(S["vec_in"], 16)
            act.dma_start(rows[96:128, :], cmp_pos.rearrange("v (c e) d -> (v c) (e d)", e=2)).then_inc(S["vec_in"], 16)
            act.dma_start(crows[:, :], gdn_conv_w[0].rearrange("j (t p) -> (j t) p", p=P)).then_inc(S["vec_in"], 16)

            def root(n, cols=False):
                r = rpost if n % 2 else rpre
                act.wait_ge(S["stat_ps"], n + 1)
                A(r[:, :], bank(2, T), ACT.Sqrt, bias=epsc[:, 0:1], scale=1.0 / DM).then_inc(S["root_done"], 1)
                if cols:
                    act.wait_ge(S["rc_ps"], n // 4 + 1)
                    A(rcol[:, :], bank(3, TT), ACT.Sqrt, bias=epsc[:, 0:1], scale=1.0 / DM).then_inc(S["rc_root"], 1)

            def squares_of_h(n, m, e):
                act.wait_ge(S["h_ready"], 4 * m + e + 1)
                A(sq[:, 2 * e:2 * e + 2, :], h[:, 2 * e:2 * e + 2, :], ACT.Square).then_inc(S["sq_ready"], 1)

            def xsplit(dst, cols, e):
                for k in (2 * e, 2 * e + 1):
                    A(dst(k), h[:, k, :], ACT.Copy, scale=gain(cols, k)).then_inc(S["xhi_done"], 1)

            def xh(k):
                return xhi[:, k, :]

            def bh(k):
                return big[:, k, :]

            def squares_of_y(units, e):
                act.wait_ge(S["unit_done"], units)
                A(sq[:, 2 * e:2 * e + 2, :], bank(e % 2, 2, T), ACT.Square).then_inc(S["sq_ready"], 1)

            split("qkv", 0)
            act.wait_ge(S["cst_dve"], N_DCST)
            for e in range(4):
                squares_of_h(0, 0, e)
            act.wait_ge(S["vec_sb"], 2)
            for e in range(4):
                xsplit(xh, MIXPRE[0], e)
            split("qkv", 1)
            root(0, cols=True)
            def silu_qkv(i, q, square=False):
                act.wait_ge(S["conv_done"], i * 2 + (q + 1))
                tiles = bass.ds(i * 4 + 2 * q, 2)
                A(qkvT[:, tiles, :], acc[:, q], ACT.Silu).then_inc(S["silu_done"], 1)
                if square:
                    act.wait_ge(S["silu_done"], i * 2 + (q + 1))
                    A(scr[:, tiles, :], qkvT[:, tiles, :], ACT.Square).then_inc(S["l2_sq"], 1)

            def qkv_pair(i, square0, square1):
                split("qkv", 0, i + 1)
                silu_qkv(i - 1, 1, square1)
                split("qkv", 1, i + 1)
                silu_qkv(i, 0, square0)
            act.wait_ge(S["small_in"], 16 * 9)
            A(wtok[:, 0, :, 0:2 * HV], wba[:, :, :], ACT.Copy).then_inc(S["wt_act"], 1)
            A(wtok[:, 0, :, 2 * HV:], wgt[:, :, :], ACT.Copy).then_inc(S["wt_act"], 1)
            split("qkv", 0, 1)
            split("qkv", 1, 1)
            act.wait_ge(S["rc_ps"], 1)
            silu_qkv(0, 0, True)
            qkv_pair(1, True, True)
            act.wait_ge(S["ba_dve"], 2)
            A(beta, balog[:, :, 0:HV], ACT.Sigmoid).then_inc(S["ba_act"], 1)
            act.wait_ge(S["ba_dve"], 5)
            A(sm[2], sm[2], ACT.Exp, scale=-1.0).then_inc(S["ba_act"], 1)
            A(alog[:, :], alog[:, :], ACT.Exp).then_inc(S["ba_act"], 1)

            table(ACT.Silu)
            with act.Fori(2, 4) as i:
                qkv_pair(i, True, True)
            qkv_pair(4, False, True)
            qkv_pair(5, False, False)
            act.wait_ge(S["l2_ps"], 1)
            l2 = bank(2, TT, 16)
            A(hcol[:, :, 0:8], l2[:, :, 0:8], ACT.Sqrt, bias=epsc[:, 1:2], scale=float(HD)).then_inc(S["l2_root"], 1)
            A(hcol[:, :, 8:16], l2[:, :, 8:16], ACT.Sqrt, bias=epsc[:, 0:1]).then_inc(S["l2_root"], 1)
            split("qkv", 0, 7)
            silu_qkv(5, 1)
            split("qkv", 1, 7)
            for i in (6, 7):
                for q in range(2):
                    silu_qkv(i, q)

            act.wait_ge(S["cum_ps"], 1)
            A(einc, bank(7, 2, TT, HV)[:, 0], ACT.Exp).then_inc(S["cum_act"], 1)
            A(faft, bank(7, 2, TT, HV)[:, 1], ACT.Exp).then_inc(S["cum_act"], 1)
            A(epsc[:, 3:4], epsc[:, 0:1], ACT.Copy).then_inc(S["oT_sb"], 1)
            act.wait_ge(S["cum_act"], 2)
            act.wait_ge(S["silu_done"], 16)
            with act.Fori(0, 4) as j:
                act.wait_ge(S["l2_done"], j * 2 + 2)
                act.wait_ge(S["oT_sb"], j * 2 + 1)
                A(kqf[:, 0:2, :], qkvT[:, bass.ds(j * 2 + HK, 2), :], ACT.Copy).then_inc(S["kqf_sb"], 1)
                A(kqf[:, 2:4, :], qkvT[:, bass.ds(j * 2, 2), :], ACT.Copy).then_inc(S["kqf_sb"], 1)
                for c in range(2):
                    for part, dst in ((0, dQ), (1, dA)):
                        act.wait_ge(S["decay_ps"], j * 5 + (2 * c + part + 1))
                        A(dst[:, c], bank(2 + 2 * c + part, 4, P), ACT.Exp).then_inc(S["decay_sb"], 1)
                act.wait_ge(S["decay_ps"], j * 5 + 5)
                A(eq, bank(6, 4, P), ACT.Exp).then_inc(S["decay_sb"], 1)
                A(vf, qkvT[:, bass.ds(j * 4 + 2 * HK, 4), :], ACT.Copy).then_inc(S["vf_sb"], 1)
                act.wait_ge(S["ktok_ps"], j + 2)
                A(ktok, bank(7, 2, 2, P), ACT.Copy).then_inc(S["ktok_sb"], 1)
                for c in range(2):
                    act.wait_ge(S["at_ps"], j * 2 + (c + 1))
                    A(ATr[:, c], bank(c, 4, P), ACT.Copy).then_inc(S["at_sb"], 1)
                    act.wait_ge(S["x_ps"], j * 12 + (c + 1))
                    A(TTr[:, c], bank(6 + c, 4, P), ACT.Copy).then_inc(S["tt_sb"], 1)
                for c in range(2):
                    act.wait_ge(S["vtok_ps"], j * 2 + (c + 1))
                    for e in range(4):
                        last = A(bv[:, c, e, :], bank(2 + 2 * c, 4, P)[:, e, :], ACT.Copy,
                                 scale=beta[:, c, bass.ds(j * 4 + e, 1)])
                    last.then_inc(S["bv_sb"], 1)
                for v in range(1, LV - 1):
                    for c in range(2):
                        act.wait_ge(S["x_ps"], j * 12 + (2 * v + c + 1))
                        A(TTr[:, c], bank(c, 4, P), ACT.Copy).then_inc(S["tt_sb"], 1)
                        q, part = divmod(2 * (v - 1) + c, 2)
                        if q < 2:
                            if part == 0:
                                act.wait_ge(landed[q], j * 16 + (8 * U0["z"] + 16))
                                act.wait_ge(S["unit_done"], j * 2 + (U0["z"] + q - 1))
                            c2 = slice(1024 * part, 1024 * part + 1024)
                            last = A(whi[:, q, c2], raw[:, q, c2], ACT.Copy)
                            if part == 1:
                                last.then_inc(S["hi_done"], 1)
                act.wait_ge(S["vn_sb"], j * 2 + 1)
                for e in range(4):
                    last = A(bv[:, 0, e, :], vn[:, 0, e, :], ACT.Copy, scale=faft[:, 0, bass.ds(j * 4 + e, 1)])
                last.then_inc(S["fv_sb"], 1)
                act.wait_ge(S["s_ps"], j + 1)
                A(Ss, bank(2, 4, P), ACT.Copy).then_inc(S["s_sb"], 1)
                for c in range(2):
                    act.wait_ge(S["o_ps"], j * 2 + (c + 1))
                    A(oT[:, bass.ds(j * 4, 4), c * P:(c + 1) * P], bank(3 + 2 * c, 4, P), ACT.Copy).then_inc(S["oT_sb"], 1)
            act.wait_ge(S["oT_sb"], 9)
            for s in range(8):
                A(osq[:, 2 * s:2 * s + 2, :], oT[:, 2 * s:2 * s + 2, :], ACT.Square).then_inc(S["on_sq"], 1)
            act.wait_ge(S["on_ps"], 1)
            A(hcol[:, :, :], bank(2, TT, 16), ACT.Sqrt, bias=epsc[:, 0:1], scale=1.0 / HD).then_inc(S["on_root"], 1)
            act.wait_ge(S["bank_free"], B0["gout"])
            for s in range(8):
                A(zT[:, 2 * s:2 * s + 2, :], zT[:, 2 * s:2 * s + 2, :], ACT.Silu).then_inc(S["sz_done"], 1)
            split("gout", 0)
            for s in range(8):
                if s == 4:
                    split("gout", 1)
                act.wait_ge(S["oz_done"], s + 1)
                A(big[:, 2 * s:2 * s + 2, :], oT[:, 2 * s:2 * s + 2, :], ACT.Copy).then_inc(S["ohi_done"], 1)

            def post_then_pre(n, m, cols, stage):
                root(n)
                split(stage, 1)
                for e in range(4):
                    act.wait_ge(S["h_ready"], 4 * m + e + 1)
                    xsplit(xh, cols, e)
                    squares_of_h(n + 1, m, e)
                root(n + 1)

            for gr in range(4):
                for q in range(2 if gr < 3 else 1):
                    split(*(("gout", q, gr + 1) if gr < 3 else ("fin0", q)))
                if gr == 3:
                    table(ACT.Sqrt)
                squares_of_y(U0["gout"] + 2 * (gr + 1), gr)
            post_then_pre(1, 1, FFNPRE[0], "fin0")

            def ffn_and_ple(layer, after):
                fin_, fout_, pin_, gate_ = (f"{v}{layer}" for v in ("fin", "fout", "pin", "gate"))

                def hidden(i):
                    act.wait_ge(S["bank_free"], i * 2 + (B0[fin_] + 1))
                    A(t1[:, 0], t0[:, 0], ACT.Silu).then_inc(S["sg_done"], 1)
                    act.wait_ge(S["hid_done"], i + (11 * layer + 1))
                    A(big[:, bass.ds(i * 2, 2), :], t2[:, 1], ACT.Copy).then_inc(S["fhi_done"], 1)
                table(ACT.Silu)
                with act.Fori(0, PAIRS[fin_] - 1) as i:
                    split(fin_, 0, i + 1)
                    split(fin_, 1, i + 1)
                    hidden(i)
                split(fout_, 0)
                split(fout_, 1)
                hidden(PAIRS[fin_] - 1)
                act.wait_ge(S["pt_ps"], layer + 1)
                A(phl[:, 0:2, :], bank(3, 2, T), ACT.Copy).then_inc(S["phi_done"], 1)
                split(fout_, 2)
                split(fout_, 3)
                for gr in range(4):
                    for q in range(2):
                        if gr < 3:
                            split(fout_, q, 2 * gr + 2)
                        elif q == 0:
                            split(pin_, 0)
                    if gr == 3:
                        table(ACT.Sqrt)
                    squares_of_y(U0[fout_] + 4 * (gr + 1), gr)
                    if gr == 3:
                        split(pin_, 1)
                    if gr < 3:
                        for q in (2, 3):
                            split(fout_, q, 2 * gr + 2)
                root(3 + 4 * layer)
                split(gate_, 0)
                for e in range(4):
                    act.wait_ge(S["h_ready"], 4 * (2 + 3 * layer) + e + 1)
                    A(xhi[:, 2 * e:2 * e + 2, :], h[:, 2 * e:2 * e + 2, :], ACT.Copy).then_inc(S["xhi_done"], 2)
                table(ACT.Sigmoid)
                split(gate_, 1)

                def next_hi(e):
                    act.wait_ge(S["h_ready"], 4 * (3 + 3 * layer) + e + 1)
                    xsplit(bh, KVN, e)
                    squares_of_h(4, 3, e)
                for g in range(4):
                    act.wait_ge(S["unit_done"], U0[gate_] + g + 1)
                    if g >= 2:
                        act.wait_ge(S["bank_free"], B0[gate_] + g - 1)
                    A(t1[:, g % 2], bank(g % 2, 2, T), ACT.Sigmoid).then_inc(S["sgm_done"], 1)
                    if g < 2:
                        split(gate_, g, 1)
                    elif after:
                        split(after, g - 2)
                    if after and g:
                        next_hi(g - 1)
                if after:
                    next_hi(3)
            ffn_and_ple(0, "kv")

            root(4, cols=True)
            act.wait_ge(S["unit_done"], U0["kv"])
            for e in range(4):
                xsplit(xh, MIXPRE[1], e)
            split("kv", 0, 1)
            split("kv", 1, 1)
            act.wait_ge(S["vec_sb"], 2)
            act.wait_ge(S["bank_free"], B0["kv"] + 1)
            block_copies(A, 0, S["ablk_act"])
            split("kv", 0, 2)
            split("kv", 1, 2)
            split("q", 0)
            split("q", 1)
            act.wait_ge(S["hb_sb"], 2)
            for v in range(2):
                for e in range(2):
                    A(hid[:, v, e, :], bank(4 + v, 2, 61)[:, e, 0:60], ACT.Silu, bias=cb[:, v, e:e + 1]).then_inc(S["hid_sb"], 1)
            split("q", 0, 1)
            split("q", 1, 1)
            split("wo", 0)
            split("wo", 1)
            act.wait_ge(S["gt_dve"], 2)
            A(gates[:, :, :], gates[:, :, :], ACT.Sigmoid).then_inc(S["gt_done"], 1)
            table(ACT.Exp)

            def operands(gi):
                A(qf, qT[:, bass.ds(gi * 2, 2), :], ACT.Copy).then_inc(S["fx_act"], 1)
                A(kf, kdup[:, :, bass.ds(gi, 1), :].rearrange("p b g s -> p (b g) s"), ACT.Copy).then_inc(S["fx_act"], 1)
            act.wait_ge(S["bank_free"], B0["wo"])
            operands(0)
            act.wait_ge(S["cs_dve"], 4)
            A(cs, cs, ACT.Exp, scale=ND ** -0.5).then_inc(S["cs_act"], 1)
            act.wait_ge(S["pct_ps"], 1)
            for e in range(2):
                A(pct[0:60, 2 * e:2 * e + 2, :], ps[0:60, 6 + e, 0:512].rearrange("p (a b) -> p a b", a=2), ACT.Copy).then_inc(S["pct_sb"], 1)
            def exps(gi, r, skip):
                act.wait_ge(S["mx_dve"], gi * 12 + (3 * r + 3))
                s1, s0 = bank(2 + 2 * (r % 2), 2, T), bank(3 + 2 * (r % 2), 2, P)
                if not skip:
                    act.wait_ge(S["ptr_ps"], gi * 8 + (2 * r - 2))
                for b in range(2):
                    A(pr0[:, r % 2, b, :], s0[:, b, :], ACT.Exp, scale=ND ** -0.5, bias=hst[:, r % 2, 1, b:b + 1],
                      accum_out=hst[:, r % 2, 2, b:b + 1])
                    A(pr1[:, r % 2, b, :], s1[:, b, :], ACT.Exp, scale=ND ** -0.5, bias=hst[:, r % 2, 1, 2 + b:3 + b],
                      accum_out=hst[:, r % 2, 2, 2 + b:3 + b]).then_inc(S["p_act"], 1)

            def turned(gi, r, skip):
                if not skip:
                    act.wait_ge(S["av_ps"], gi * 4 + (r - 1))
                for b in range(2):
                    act.wait_ge(S["ptr_ps"], gi * 8 + (2 * r + b + 1))
                    A(pts[:, r % 2, b], bank(6 + b, 3, P), ACT.Copy).then_inc(S["pts_act"], 1)

            def out_hi(gi, c):
                act.wait_ge(S["av_ps"], gi * 4 + (2 * c + 2))
                A(big[:, bass.ds(gi * 2 + c, 1), :], bank(c, 1, T), ACT.Copy).then_inc(S["ahi"], 1)

            def group(gi, first, last):
                exps(gi, 1, first)
                turned(gi, 0, first)
                if not first:
                    out_hi(gi - 1, 1)
                exps(gi, 2, False)
                turned(gi, 1, first)
                if not last:
                    act.wait_ge(S["sc_ps"], gi * 4 + 4)
                    operands(gi + 1)
                exps(gi, 3, False)
                turned(gi, 2, False)
                out_hi(gi, 0)
                if not last:
                    exps(gi + 1, 0, False)
                turned(gi, 3, False)
            exps(0, 0, True)
            group(0, True, False)
            with act.Fori(1, NG - 1) as gi:
                group(gi, False, False)
            group(NG - 1, False, True)
            out_hi(NG - 1, 1)
            for i in range(2):
                for q in range(2):
                    if i == 0:
                        split("wo", q, 1)
                    elif q == 0:
                        split("fin1", q)
                    else:
                        table(ACT.Sqrt)
                    squares_of_y(U0["wo"] + 2 * i + q + 1, 2 * i + q)
            post_then_pre(5, 4, FFNPRE[1], "fin1")
            ffn_and_ple(1, None)
            for a in range(TT):
                act.wait_ge(S["out_ps"], 2 * a + 2)
                A(otok[:, a, 512:DM], bank(3 + 2 * a, 512), ACT.Copy).then_inc(S["out_act"], 1)

        @block.vector
        def _(dve):
            V = nc.vector
            stt = V.scalar_tensor_tensor

            def split(stage, q, i=0):
                u = i * 2 + (U0[stage] + q)
                n = unit_k(stage, q) * UW
                if stage == "qkv" and not (isinstance(i, int) and i == 0):
                    n = n // 2
                dve.wait_ge(S["hi_done"], u + 1)
                V.tensor_tensor(wlo[:, q % 2, 0:n], raw[:, q % 2, 0:n], whi[:, q % 2, 0:n],
                                ALU.subtract).then_inc(S["lo_done"], 1)

            for t, v in ((rows, 0.0), (ident, 0.0), (ones, 1.0), (causb, 0.0), (cmask, 0.0), (m1t, 1.0), (kcz, 0.0),
                         (rmask, 1.0)):
                V.memset(t[tuple([slice(None)] * len(t.shape))], v).then_inc(S["cst_dve"], 1)
            for v in range(LV):
                m = masks[:, v, :].rearrange("p (m e b) -> p m e b", e=2, b=1 << v)
                for e in range(2):
                    V.memset(m[:, :, e, :], float(1 - e)).then_inc(S["cst_dve"], 1)
            V.memset(epsc[:, 0:1], EPS).then_inc(S["cst_dve"], 1)
            V.memset(epsc[:, 1:2], EPS * HD).then_inc(S["cst_dve"], 1)

            def rstd(n, cols=False):
                r = rpost if n % 2 else rpre
                dve.wait_ge(S["root_done"], n + 1)
                V.reciprocal(r[:, :], r[:, :]).then_inc(S["rstd_done"], 1)
                if cols:
                    dve.wait_ge(S["rc_root"], n // 4 + 1)
                    V.reciprocal(rcol[:, :], rcol[:, :]).then_inc(S["rcol_done"], 1)

            XN = [0]

            def xlo_part(hi, lo, cols, e):
                for k in (2 * e, 2 * e + 1):
                    dve.wait_ge(S["xhi_done"], XN[0] + k + 1)
                    if cols is None:
                        V.tensor_tensor(lo(k), h[:, k, :], hi(k), ALU.subtract).then_inc(S["xlo_done"], 1)
                    else:
                        stt(out=lo(k), in0=h[:, k, :], scalar=gain(cols, k), in1=hi(k), op0=ALU.mult,
                            op1=ALU.subtract).then_inc(S["xlo_done"], 1)
                if e == 3:
                    XN[0] += KD

            def xsplit(hi, lo, cols):
                for e in range(4):
                    xlo_part(hi, lo, cols, e)

            def xh(k):
                return xhi[:, k, :]

            def xl(k):
                return xlo[:, k, :]

            def times_rstd(dst, q, done_at):
                dve.wait_ge(S["unit_done"], done_at)
                return V.tensor_tensor(dst, bank(q, 2, T), over(rpre[:, :], 1, 2), ALU.mult).then_inc(S["bank_free"], 1)

            for e in range(4):
                dve.wait_ge(S["xt_ps"], e + 1)
                V.tensor_copy(h[:, 2 * e:2 * e + 2, :], bank(4 + e, 2, T)).then_inc(S["h_ready"], 1)
            dve.wait_ge(S["vec_ps"], 1)
            V.tensor_copy(vecs[:, :], bank(3, 4, P)[:, 0, :]).then_inc(S["vec_sb"], 1)
            V.tensor_copy(cw[:, :, :], bank(3, 4, P)[:, 1, :].rearrange("p (j t) -> p j t", j=4)).then_inc(S["vec_sb"], 1)
            dve.wait_ge(S["vec_sb"], 2)
            dve.wait_ge(S["h_ready"], 4)
            split("qkv", 0)
            xsplit(xh, xl, MIXPRE[0])
            split("qkv", 1)
            V.memset(pre[:, :, :, 0:3], 0.0).then_inc(S["conv_dve"], 1)
            rstd(0, cols=True)
            dve.wait_ge(S["rstd_done"], 1)

            def conv_in(i, q):
                dve.wait_ge(S["unit_done"], i * 2 + (q + 1))
                V.tensor_tensor(pre[:, q, :, 3:T + 3], bank(q, 2, T), over(rpre[:, :], 1, 2),
                                ALU.mult).then_inc(S["bank_free"], 1)

            def conv(i, q, n0):
                dve.wait_ge(S["bank_free"], i * 2 + (q + 1))
                if not (isinstance(i, int) and i == 0):
                    dve.wait_ge(S["silu_done"], i * 2 + (q - 1))
                for j in range(4):
                    for e in range(2):
                        if j:
                            dve.wait_ge(S["conv_dve"], n0 + 2 * (j - 1) + e + 1)
                        w = cw[:, j, bass.ds(i * 4 + 2 * q + e, 1)]
                        src = pre[:, q, e, j:j + T]
                        if j == 0:
                            ins = V.tensor_scalar(acc[:, q, e, :], src, w, None, ALU.mult)
                        else:
                            ins = stt(out=acc[:, q, e, :], in0=src, scalar=w, in1=acc[:, q, e, :], op0=ALU.mult, op1=ALU.add)
                        ins.then_inc(S["conv_done"] if (j, e) == (3, 1) else S["conv_dve"], 1)

            def logit_copy(n, b, count):
                dve.wait_ge(S["tk_ps"], count)
                V.tensor_copy(tkr[0:n, :], ps[0:n, b, 0:T]).then_inc(S["tk_sb"], 1)

            def conv_pair(i, splits):
                for q in range(2):
                    splits(q)
                    conv_in(i, q)
                    conv(i, q, i * 14 + (7 * q + 1))
            for n, (cols, w) in enumerate(((slice(0, 2 * HV), wba), (slice(2 * HV, 80), wgt))):
                dve.wait_ge(S["wt_act"], n + 1)
                V.tensor_tensor(wtok[:, 1, :, cols], w[:, :, :], wtok[:, 0, :, cols], ALU.subtract).then_inc(S["wt_dve"], 1)
            conv_pair(0, lambda q: split("qkv", q, 1))
            logit_copy(2 * HV, 4, 1)
            conv_pair(1, lambda q: split("qkv", q, 2))
            n_ba = [0]

            def ba(ins):
                ins.then_inc(S["ba_dve"], 1)
                n_ba[0] += 1
                dve.wait_ge(S["ba_dve"], n_ba[0])
            dve.wait_ge(S["rcol_done"], 1)
            dve.wait_ge(S["ba_ps"], 1)
            for a in range(TT):
                ba(V.tensor_scalar(balog[:, a, :], bank(4, TT, 2 * HV)[:, a, :], rcol[:, a:a + 1], None, ALU.mult))
            ba(V.tensor_tensor(sm[0], balog[:, :, HV:2 * HV], over(dtb[:, :], 1, TT), ALU.add))
            ba(V.tensor_scalar(sm[1], sm[0], 0.0, None, ALU.max))
            ba(stt(out=sm[2], in0=sm[0], scalar=-1.0, in1=sm[0], op0=ALU.mult, op1=ALU.max))
            dve.wait_ge(S["ba_act"], 3)
            ba(V.tensor_scalar(sm[3], sm[2], 2.0, None, ALU.add))
            ba(V.reciprocal(sm[3], sm[3]))
            ba(V.tensor_tensor(sm[3], sm[2], sm[3], ALU.mult))
            ba(V.tensor_tensor(sm[4], sm[3], sm[3], ALU.mult))
            ba(V.tensor_scalar(sm[5], sm[4], 1.0 / 13, None, ALU.mult))
            for c in (11, 9, 7, 5, 3):
                ba(stt(out=sm[5], in0=sm[5], scalar=1.0 / c, in1=sm[4], op0=ALU.add, op1=ALU.mult))
            ba(stt(out=sm[5], in0=sm[5], scalar=1.0, in1=sm[3], op0=ALU.add, op1=ALU.mult))
            ba(stt(out=sm[1], in0=sm[5], scalar=2.0, in1=sm[1], op0=ALU.mult, op1=ALU.add))
            ba(stt(out=gdec, in0=sm[1], scalar=-1.0, in1=over(alog[:, :], 1, TT), op0=ALU.mult, op1=ALU.mult))
            assert n_ba[0] == N_BA
            with dve.Fori(2, PAIRS["qkv"] - 1) as i:
                conv_pair(i, lambda q: split("qkv", q, i + 1))
            dve.wait_ge(S["l2_root"], 2)
            V.reciprocal(hcol[:, :, :], hcol[:, :, :]).then_inc(S["hrec"], 1)
            conv_pair(PAIRS["qkv"] - 1, lambda q: None)

            for n, s in enumerate(QK_ORDER):
                dve.wait_ge(S["l2_rows"], n + 1)
                V.tensor_tensor(qkvT[:, 2 * s:2 * s + 2, :], qkvT[:, 2 * s:2 * s + 2, :], bank((3, 4, 5, 6)[n % 4], 2, T),
                                ALU.mult).then_inc(S["l2_done"], 1)
            dve.wait_ge(S["cum_act"], 2)
            stt(out=nbe, in0=beta, scalar=-1.0, in1=einc, op0=ALU.mult, op1=ALU.mult).then_inc(S["cum_dve"], 1)
            dve.wait_ge(S["cum_dve"], 1)
            dve.wait_ge(S["cst_pool"], N_CST)

            def odd(ap, b):
                return ap.rearrange("p h (m e b) -> p h m e b", e=2, b=b)[:, :, :, 1, :]

            def even(ap, b):
                return ap.rearrange("p h (m e b) -> p h m e b", e=2, b=b)[:, :, :, 0, :]

            with dve.Fori(0, 4) as j:
                dve.wait_ge(S["oT_sb"], j * 2 + 1)
                for c in range(2):
                    dve.wait_ge(S["kq_ps"], j * 2 + (c + 1))
                    dve.wait_ge(S["decay_sb"], j * 5 + (2 * c + 2))
                    for e in range(4):
                        last = stt(out=dA[:, c, e, :], in0=bank(c, 4, P)[:, e // 2, :],
                                   scalar=beta[:, c, bass.ds(j * 4 + e, 1)], in1=dA[:, c, e, :], op0=ALU.mult, op1=ALU.mult)
                    last.then_inc(S["a_sb"], 1)
                    d = dQ[:, c].rearrange("p (k r) s -> p k r s", r=2)
                    V.tensor_tensor(d, over(bank(c, 4, P)[:, 2:4, :], 2, 2), d, ALU.mult).then_inc(S["qk_raw"], 1)
                    if c == 0:
                        dve.wait_ge(S["a_sb"], j * 2 + 1)
                        V.tensor_tensor(Tr[:, 0], dA[:, 0], over(m1t[:, :], 1, 4), ALU.mult).then_inc(S["t0init"], 1)
                        dve.wait_ge(S["t0init"], j * 2 + 1)
                        V.tensor_tensor(Tr[:, 0], over(ident[:, :], 1, 4), Tr[:, 0], ALU.subtract).then_inc(S["t0init"], 1)
                dve.wait_ge(S["decay_sb"], j * 5 + 5)
                e4 = eq.rearrange("p (k r) s -> p k r s", r=2)
                V.tensor_tensor(e4, over(kqf[:, 2:4, P:T], 2, 2), e4, ALU.mult).then_inc(S["qdec_sb"], 1)

                def y_out(v, c):
                    dve.wait_ge(S["y_ps"], j * 12 + (2 * (v - 1) + c + 1))
                    V.tensor_tensor(yb[:, c], bank(3 + 2 * c, 4, P), over(masks[:, v, :], 1, 4),
                                    ALU.mult).then_inc(S["y_sb"], 1)

                def z_split(q, part):
                    if part == 0:
                        dve.wait_ge(S["hi_done"], j * 2 + (U0["z"] + q + 1))
                    c4 = slice(512 * part, 512 * part + 512)
                    last = V.tensor_tensor(wlo[:, q, c4], raw[:, q, c4], whi[:, q, c4], ALU.subtract)
                    if part == 3:
                        last.then_inc(S["lo_done"], 1)

                def z_out(q):
                    dve.wait_ge(S["unit_done"], j * 2 + (U0["z"] + q + 1))
                    V.tensor_tensor(zT[:, bass.ds(j * 4 + 2 * q, 2), :], bank(6 + q, 2, T), over(rpre[:, :], 1, 2),
                                    ALU.mult).then_inc(S["bank_free"], 1)

                def update(v, c):
                    b = 1 << v
                    dve.wait_ge(S["z_ps"], j * 12 + (2 * (v - 1) + c + 1))
                    half, t = (even, Tr) if v < LV - 1 else (odd, TTr)
                    V.tensor_tensor(half(t[:, c], b), half(t[:, c], b), half(bank(6 + c, 4, P), b),
                                    ALU.subtract).then_inc(S["t_upd"], 1)

                y_out(1, 0)
                update(1, 0)
                y_out(1, 1)
                for v in range(2, LV):
                    y_out(v, 0)
                    if v > 2:
                        z_split((v - 3) // 2, 2 * ((v - 3) % 2))
                    update(v - 1, 1)
                    update(v, 0)
                    y_out(v, 1)
                    if v > 2:
                        z_split((v - 3) // 2, 2 * ((v - 3) % 2) + 1)
                update(LV - 1, 1)
                dve.wait_ge(S["u_ps"], j * 2 + 1)
                V.tensor_copy(vn[:, 0], bank(0, 4, P)).then_inc(S["vn_sb"], 1)
                dve.wait_ge(S["ks_ps"], j + 1)
                dve.wait_ge(S["bv_sb"], j * 2 + 2)
                for e in range(4):
                    last = stt(out=bv[:, 1, e, :], in0=bank(4, 4, P)[:, e, :], scalar=nbe[:, 1, bass.ds(j * 4 + e, 1)],
                               in1=bv[:, 1, e, :], op0=ALU.mult, op1=ALU.add)
                last.then_inc(S["r1_sb"], 1)
                z_out(0)
                dve.wait_ge(S["u_ps"], j * 2 + 2)
                V.tensor_copy(vn[:, 1], bank(1, 4, P)).then_inc(S["vn_sb"], 1)
                z_out(1)
            dve.wait_ge(S["on_root"], 1)
            V.reciprocal(hcol[:, :, :], hcol[:, :, :]).then_inc(S["hrec"], 1)
            dve.wait_ge(S["oT_sb"], 9)
            for s in range(8):
                o = oT[:, 2 * s:2 * s + 2, :]
                dve.wait_ge(S["on_rows"], s + 1)
                stt(out=o, in0=o, scalar=vecs[:, ONORM:ONORM + 1], in1=bank((3, 4, 5, 6)[s % 4], 2, T), op0=ALU.mult,
                    op1=ALU.mult).then_inc(S["on_done"], 1)
                dve.wait_ge(S["on_done"], s + 1)
                dve.wait_ge(S["sz_done"], s + 1)
                V.tensor_tensor(o, o, zT[:, 2 * s:2 * s + 2, :], ALU.mult).then_inc(S["oz_done"], 1)
                if s in (3, 5):
                    split("gout", s // 2 - 1)

            def y_out_group(n, gr):
                dve.wait_ge(S["sq_ready"], 4 * n + gr + 1)
                V.tensor_copy(y[:, 2 * gr:2 * gr + 2, :], bank(gr % 2, 2, T)).then_inc(S["bank_free"], 1)

            YN = [0]

            def post_norm(n, cols, end, lo_part, between=None):
                rstd(n)
                dve.wait_ge(S["rstd_done"], n + 1)
                dve.wait_ge(S["bank_free"], end)
                y0 = YN[0]

                def added(e):
                    if e == 0:
                        dve.wait_ge(S["yn_done"], y0 + 1)
                    else:
                        dve.wait_ge(S["yn_pool"], 3 * y0 + e)
                    for k in (2 * e, 2 * e + 1):
                        last = stt(out=h[:, k, :], in0=y[:, k, :], scalar=gain(cols, k), in1=h[:, k, :], op0=ALU.mult,
                                   op1=ALU.add)
                    last.then_inc(S["h_ready"], 1)
                V.tensor_tensor(y[:, 0:2, :], y[:, 0:2, :], over(rpost[:, :], 1, 2), ALU.mult).then_inc(S["yn_done"], 1)
                added(0)
                added(1)
                if between:
                    between()
                lo_part(0)
                added(2)
                lo_part(1)
                added(3)
                lo_part(2)
                lo_part(3)
                YN[0] += 1

            for gr in range(4):
                for q in range(2 if gr < 3 else 1):
                    split(*(("gout", q, gr + 1) if gr < 3 else ("fin0", q)))
                y_out_group(1, gr)
            post_norm(1, MIXPOST[0], B0["fin0"], lambda e: xlo_part(xh, xl, FFNPRE[0], e))
            split("fin0", 1)
            rstd(2)

            def ffn_and_ple(layer, after):
                fin_, fout_, pin_, gate_ = (f"{v}{layer}" for v in ("fin", "fout", "pin", "gate"))
                dve.wait_ge(S["rstd_done"], 3 + 4 * layer)

                def hidden(i, splits):
                    splits(0)
                    times_rstd(t0[:, 0], 0, i * 2 + (U0[fin_] + 1))
                    splits(1)
                    times_rstd(t2[:, 0], 1, i * 2 + (U0[fin_] + 2))
                    dve.wait_ge(S["sg_done"], i + (11 * layer + 1))
                    dve.wait_ge(S["bank_free"], i * 2 + (B0[fin_] + 2))
                    V.tensor_tensor(t2[:, 1], t1[:, 0], t2[:, 0], ALU.mult).then_inc(S["hid_done"], 1)
                    dve.wait_ge(S["fhi_done"], i + (11 * layer + 1))
                    V.tensor_tensor(big[:, bass.ds(i * 2 + KF, 2), :], t2[:, 1], big[:, bass.ds(i * 2, 2), :],
                                    ALU.subtract).then_inc(S["flo_done"], 1)
                with dve.Fori(0, PAIRS[fin_] - 1) as i:
                    hidden(i, lambda q: split(fin_, q, i + 1))
                hidden(PAIRS[fin_] - 1, lambda q: split(fout_, q))
                dve.wait_ge(S["phi_done"], layer + 1)
                V.tensor_tensor(phl[:, 2:4, :], bank(3, 2, T), phl[:, 0:2, :], ALU.subtract).then_inc(S["plo_done"], 1)
                split(fout_, 2)
                split(fout_, 3)
                for gr in range(4):
                    for q in range(2):
                        if gr < 3:
                            split(fout_, q, 2 * gr + 2)
                        elif q == 0:
                            split(pin_, 0)
                    y_out_group(3 + 4 * layer, gr)
                    if gr == 3:
                        split(pin_, 1)
                    if gr < 3:
                        for q in (2, 3):
                            split(fout_, q, 2 * gr + 2)
                post_norm(3 + 4 * layer, FFNPOST[layer], B0[gate_], lambda e: xlo_part(xh, xl, None, e),
                          lambda: split(gate_, 0))
                split(gate_, 1)

                def next_lo(e):
                    xlo_part(lambda k: big[:, k, :], lambda k: big[:, KD + k, :], KVN, e)
                for g in range(4):
                    if g < 2:
                        split(gate_, g, 1)
                    elif after:
                        split(after, g - 2)
                    dve.wait_ge(S["sgm_done"], g + (4 * layer + 1))
                    if g >= 2:
                        dve.wait_ge(S["h_ready"], 4 * (3 + 3 * layer) + g - 1)
                    V.tensor_tensor(t0[:, g % 2], bank(4 + g, 2, T), t1[:, g % 2], ALU.mult).then_inc(S["bank_free"], 1)
                    dve.wait_ge(S["bank_free"], B0[gate_] + g + 1)
                    hh = h[:, 2 * g:2 * g + 2, :]
                    V.tensor_tensor(hh, hh, t0[:, g % 2], ALU.add).then_inc(S["h_ready"], 1)
                    if after and g:
                        next_lo(g - 1)
                if after:
                    next_lo(3)
            ffn_and_ple(0, "kv")

            rstd(4, cols=True)
            xsplit(xh, xl, MIXPRE[1])
            dve.wait_ge(S["rstd_done"], 5)
            dve.wait_ge(S["rcol_done"], 2)
            for q in range(2):
                split("kv", q, 1)
                times_rstd(ckv[:, q], q, U0["kv"] + q + 1)
            dve.wait_ge(S["bank_free"], B0["kv"] + 2)
            block_copies(V.tensor_copy, 1, S["ablk_dve"])
            for b in range(2):
                split(*(("kv", 0, 2) if b == 0 else ("q", 0)))
                dve.wait_ge(S["unit_done"], U0["kv"] + 2 * b + 3)
                for e in range(2):
                    src = slice(64 * e, 64 * e + 64)
                    for d in range(2):
                        dst = kdup[64 * d:64 * d + 64, b].rearrange("p (t h) s -> p t h s", h=2)[:, :, e, :]
                        last = V.tensor_tensor(dst, bank(0, 2, T)[src], over(rpre[src, :], 1, 2), ALU.mult)
                last.then_inc(S["bank_free"], 1)
                split(*(("kv", 1, 2) if b == 0 else ("q", 1)))
                dve.wait_ge(S["unit_done"], U0["kv"] + 2 * b + 4)
                for a in range(TT):
                    last = V.tensor_scalar(vtk[:, b, a, :], bank(1, TT, T)[:, a, :], rcol[:, a:a + 1], None, ALU.mult)
                last.then_inc(S["bank_free"], 1)
            dve.wait_ge(S["hid_ps"], 1)
            for v in range(2):
                V.tensor_copy(cb[:, v], bank(4 + v, 2, 61)[:, :, 60]).then_inc(S["hb_sb"], 1)
            logit_copy(3 * NH, 7, 2)
            dve.wait_ge(S["hid_sb"], 4)
            for e in range(2):
                V.tensor_copy(hrep[:, :, e, :].rearrange("p g (r n) -> p g r n", r=NR),
                              over(hid[:, 1, e, :].rearrange("p (g n) -> p g n", g=NG), 2, NR))
            for i in range(2):
                for q in range(2):
                    if i and q:
                        dve.wait_ge(S["kc_ps"], 2)
                        for e in range(2):
                            half = slice(64 * e, 64 * e + 64)
                            V.tensor_copy(kcz[half, :, e, :], ps[half, 6, 0:60].rearrange("p (g n) -> p g n", g=NG)
                                          ).then_inc(S["kc_sb"], 1)
                        V.tensor_copy(vrep[0:60], ps[0:60, 7, 0:256].rearrange("p (g d) -> p g d", g=NG)).then_inc(S["kc_sb"], 1)
                    if (i, q) != (1, 1):
                        split(*(("q", q, 1) if i == 0 else ("wo", q)))
                    times_rstd(qT[:, 4 * i + 2 * q:4 * i + 2 * q + 2, :], q, U0["q"] + 2 * i + q + 1)
                    if (i, q) == (1, 1):
                        split("wo", 1)
                if i == 0:
                    dve.wait_ge(S["gt_ps"], 1)
                    for a in range(TT):
                        V.tensor_scalar(gates[:, a, :], bank(7, TT, 3 * NH)[:, a, :], rcol[:, a:a + 1], None,
                                        ALU.mult).then_inc(S["gt_dve"], 1)
            def maxima(gi, r):
                dve.wait_ge(S["sc_ps"], gi * 4 + (r + 1))
                s1, s0 = bank(2 + 2 * (r % 2), 2, T), bank(3 + 2 * (r % 2), 2, P)
                V.tensor_reduce(out=hst[:, r % 2, 0, 0:2], in_=s0, axis=AX, op=ALU.max).then_inc(S["mx_dve"], 1)
                V.tensor_reduce(out=hst[:, r % 2, 0, 2:4], in_=s1, axis=AX, op=ALU.max).then_inc(S["mx_dve"], 1)
                dve.wait_ge(S["mx_dve"], gi * 12 + (3 * r + 2))
                V.tensor_scalar(hst[:, r % 2, 1, :], hst[:, r % 2, 0, :], -(ND ** -0.5), None, ALU.mult).then_inc(S["mx_dve"], 1)

            n_cs = [0]

            def csw(ins):
                ins.then_inc(S["cs_dve"], 1)
                n_cs[0] += 1
                dve.wait_ge(S["cs_dve"], n_cs[0])
            dve.wait_ge(S["cs_ps"], 1)
            csw(V.tensor_tensor(cs, bank(2, TT, NH, NC), over(cmask[:, :, :], 2, NH), ALU.add))
            csf = cs.rearrange("p a h n -> p (a h) n")
            csw(V.tensor_reduce(out=cst[:, 0, :], in_=csf, axis=AX, op=ALU.max))
            csw(V.tensor_scalar(cst[:, 0, :], cst[:, 0, :], -1e25, None, ALU.max))
            csw(V.tensor_tensor(csf, csf, over(cst[:, 0, :], 2, NC), ALU.subtract))
            maxima(0, 0)
            dve.wait_ge(S["cs_act"], 1)
            csw(V.tensor_reduce(out=cst[:, 1, :], in_=csf, axis=AX, op=ALU.add))
            csw(V.tensor_scalar(cst[:, 1, :], cst[:, 1, :], 1e-30, None, ALU.max))
            csw(V.reciprocal(cst[:, 1, :], cst[:, 1, :]))
            dve.wait_ge(S["gt_done"], 1)
            g4 = gates[:, :, :].rearrange("p a (h b) -> p a h b", b=3)
            csw(V.tensor_tensor(cst[:, 2, :].rearrange("p (a h) -> p a h", a=TT),
                                cst[:, 1, :].rearrange("p (a h) -> p a h", a=TT), g4[:, :, :, 0], ALU.mult))
            csw(V.tensor_tensor(csf, csf, over(cst[:, 2, :], 2, NC), ALU.mult))
            dve.wait_ge(S["pct_sb"], 2)
            dve.wait_ge(S["kc_sb"], 3)
            def values(gi, first):
                if not first:
                    dve.wait_ge(S["av_ps"], gi * 4)
                V.tensor_copy(vff.rearrange("p b a d -> p (b a) d"),
                              vtk.rearrange("p b a (g d) -> p (b a) g d", g=NG)[:, :, bass.ds(gi, 1), :]
                              .rearrange("p b g d -> p b (g d)")).then_inc(S["fx_dve"], 1)
                V.tensor_copy(pcf[0:60, :], pct[0:60, bass.ds(gi, 1), :].rearrange("p g q -> p (g q)")).then_inc(S["fx_dve"], 1)
                V.tensor_tensor(vz[0:60], over(vrep[0:60, bass.ds(gi, 1), :].rearrange("p g d -> p (g d)"), 1, NR),
                                over(rmask[0:60, :], 2, ND), ALU.mult).then_inc(S["fx_dve"], 1)

            def weights(gi, r):
                for b in range(2):
                    dve.wait_ge(S["p_act"], gi * 8 + (2 * r + b + 1))
                    l = hst[:, r % 2, 2, :].rearrange("p (a b) -> p a b", a=TT)[:, :, b:b + 1]
                    V.reciprocal(l, l).then_inc(S["rl_dve"], 1)
                    dve.wait_ge(S["rl_dve"], gi * 16 + (4 * r + 2 * b + 1))
                    stt(out=l, in0=l, scalar=1e30, in1=gates[:, :, bass.ds(gi * 12 + (3 * r + 1 + b), 1)], op0=ALU.min,
                        op1=ALU.mult).then_inc(S["rl_dve"], 1)
                    dve.wait_ge(S["rl_dve"], gi * 16 + (4 * r + 2 * b + 2))
                    V.tensor_scalar(pr0[:, r % 2, b, :], pr0[:, r % 2, b, :], l[:, 0, :], None, ALU.mult)
                    V.tensor_scalar(pr1[:, r % 2, b, :], pr1[:, r % 2, b, :], l[:, 1, :], None,
                                    ALU.mult).then_inc(S["pw_dve"], 1)

            def out_lo(gi, c):
                dve.wait_ge(S["ahi"], gi * 2 + (c + 1))
                V.tensor_tensor(big[:, bass.ds(gi * 2 + (KD + c), 1), :], bank(c, 1, T),
                                big[:, bass.ds(gi * 2 + c, 1), :], ALU.subtract).then_inc(S["alo"], 1)

            def group(gi, first, last):
                weights(gi, 0)
                maxima(gi, 1)
                weights(gi, 1)
                values(gi, first)
                maxima(gi, 2)
                if not first:
                    out_lo(gi - 1, 1)
                weights(gi, 2)
                maxima(gi, 3)
                weights(gi, 3)
                out_lo(gi, 0)
                if not last:
                    maxima(gi + 1, 0)
            group(0, True, False)
            with dve.Fori(1, NG - 1) as gi:
                group(gi, False, False)
            group(NG - 1, False, True)
            out_lo(NG - 1, 1)
            for i in range(2):
                for q in range(2):
                    if i == 0 or q == 0:
                        split(*(("wo", q, 1) if i == 0 else ("fin1", q)))
                    y_out_group(5, 2 * i + q)
            post_norm(5, MIXPOST[1], B0["fin1"], lambda e: xlo_part(xh, xl, FFNPRE[1], e))
            split("fin1", 1)
            rstd(6)
            ffn_and_ple(1, None)
            for a in range(TT):
                dve.wait_ge(S["out_ps"], 2 * a + 1)
                V.tensor_copy(otok[:, a, 0:512], bank(2 + 2 * a, 512)).then_inc(S["out_sb"], 1)
    return nc


_INS = ["x", "p", "mix_pre_norm", "mix_post_norm", "ffn_pre_norm", "ffn_post_norm", "gdn_w_in", "gdn_conv_w",
        "gdn_a_log", "gdn_dt_bias", "gdn_o_norm", "gdn_w_out", "kv_norm", "kv_w", "cmp_pos", "cmp_w1", "cmp_w2",
        "nsa_w_qg", "nsa_w_o", "ffn_w_in", "ffn_w_out", "ple_w_in", "ple_w_gate"]


def kernel(**inputs):
    import numpy as np
    import concourse.bacc as bacc
    from concourse.bass_utils import run_bass_kernel_spmd

    nc = bacc.Bacc("TRN2", target_bir_lowering=False, num_devices=1)
    arrays, args = {}, []
    for name in _INS:
        a = np.ascontiguousarray(inputs[name])
        arrays[f"in_{name}"] = a
        args.append(nc.dram_tensor(f"in_{name}", a.shape, mybir.dt.from_np(a.dtype), kind="ExternalInput").ap())
    out = nc.dram_tensor("out_h", inputs["x"].shape, F32, kind="ExternalOutput").ap()
    build(nc, *args, out)
    r = run_bass_kernel_spmd(nc, [arrays], core_ids=[0])
    return r.results[0]["out_h"]
```
